# Optimizing a Trainium2 kernel written in Bass

```python
import math
import jax, jax.numpy as jnp
from jax import lax
import numpy as np

D_MODEL = 1024
BATCH = 1
SEQ = 512
DEPTH = 1

CHUNK = 64
Q_BLOCK = 128
MEM_LEN = 256
SB_HEADS = 8
SB_HEAD_DIM = 64
SB_W = SB_HEADS * SB_HEAD_DIM
RET_HEADS = 8
RET_QK_DIM = 64
RET_V_DIM = 128
RET_QK_W = RET_HEADS * RET_QK_DIM
RET_V_W = RET_HEADS * RET_V_DIM
ROPE_BASE = 10000.0
IN_SPLITS = (SB_W, SB_W, SB_W, RET_QK_W, RET_QK_W, RET_V_W, RET_V_W, D_MODEL, D_MODEL)
IN_W = sum(IN_SPLITS)
X_HEADS = 4
X_HEAD_DIM = D_MODEL // X_HEADS
N_EXPERTS = 32
TOP_K = 4
D_FF = D_MODEL
SWIGLU_LIMIT = 7.0
SWIGLU_ALPHA = 1.702
EXPERT_BLOCK = 128
NORM_EPS = 1e-5

kernel_name = "hybrid_stickbreak_retention_xattn_moe"

def rmsnorm(x, g):
    xf = x.astype(jnp.float32)
    y = xf * lax.rsqrt(jnp.mean(xf * xf, axis=-1, keepdims=True) + NORM_EPS)
    return (y * g.astype(jnp.float32)).astype(x.dtype)

def rotary(x):
    S, d = x.shape[1], x.shape[3]
    inv = ROPE_BASE ** (-jnp.arange(0, d, 2, dtype=jnp.float32) / d)
    ang = jnp.arange(S, dtype=jnp.float32)[:, None] * inv[None, :]
    cos = jnp.cos(ang)[None, :, None, :]
    sin = jnp.sin(ang)[None, :, None, :]
    xf = x.astype(jnp.float32)
    x1, x2 = xf[..., : d // 2], xf[..., d // 2 :]
    return jnp.concatenate([x1 * cos - x2 * sin, x1 * sin + x2 * cos], axis=-1).astype(x.dtype)

def stick_breaking_attention(q, k, v):
    S, d = q.shape[1], q.shape[3]
    scale = d ** -0.5
    outs = []
    for i in range(S // Q_BLOCK):
        start, end = i * Q_BLOCK, (i + 1) * Q_BLOCK
        z = jnp.einsum('bqhd,bkhd->bhqk', q[:, start:end], k[:, :end]).astype(jnp.float32) * scale
        t_pos = jnp.arange(start, end)[:, None]
        s_pos = jnp.arange(end)[None, :]
        mask = s_pos < t_pos
        log_1m = jnp.where(mask, jax.nn.log_sigmoid(-z), 0.0)
        between = lax.cumsum(log_1m, axis=3, reverse=True) - log_1m
        w = jnp.where(mask, jnp.exp(jax.nn.log_sigmoid(z) + between), 0.0)
        outs.append(jnp.einsum('bhqk,bkhd->bqhd', w.astype(v.dtype), v[:, :end]))
    return jnp.concatenate(outs, axis=1)

def retention(q, k, v):
    B, S, H, dk = q.shape
    dv = v.shape[3]
    N = S // CHUNK
    log_g = jnp.log1p(-jnp.exp2(-5.0 - jnp.arange(H, dtype=jnp.float32)))
    qf = q.astype(jnp.float32).reshape(B, N, CHUNK, H, dk)
    kf = (k.astype(jnp.float32) * dk ** -0.5).reshape(B, N, CHUNK, H, dk)
    vf = v.astype(jnp.float32).reshape(B, N, CHUNK, H, dv)
    pos = jnp.arange(CHUNK, dtype=jnp.float32)
    diff = pos[:, None] - pos[None, :]
    decay = jnp.where(diff >= 0, jnp.exp(log_g[:, None, None] * jnp.maximum(diff, 0.0)), 0.0)
    scores = jnp.einsum('bnchd,bnshd->bnhcs', qf, kf) * decay
    o_intra = jnp.einsum('bnhcs,bnshe->bnche', scores, vf)
    k_dec = jnp.exp(log_g[:, None] * (CHUNK - 1 - pos)[None, :])
    kv = jnp.einsum('bnshd,hs,bnshe->nbhde', kf, k_dec, vf)
    chunk_dec = jnp.exp(log_g * CHUNK)[None, :, None, None]

    def step(state, kv_n):
        return state * chunk_dec + kv_n, state

    _, s_prev = lax.scan(step, jnp.zeros((B, H, dk, dv), jnp.float32), kv)
    q_dec = jnp.exp(log_g[:, None] * (pos + 1.0)[None, :])
    o_cross = jnp.einsum('bnchd,hc,nbhde->bnche', qf, q_dec, s_prev)
    return (o_intra + o_cross).reshape(B, S, H, dv)

def head_groupnorm(y):
    mu = jnp.mean(y, axis=-1, keepdims=True)
    var = jnp.mean(jnp.square(y - mu), axis=-1, keepdims=True)
    return (y - mu) * lax.rsqrt(var + NORM_EPS)

def token_mixer(h, w_in, w_sb_o, w_ret_o, w_mix_out):
    B, S, _ = h.shape
    proj = h @ w_in
    idx = list(np.cumsum(IN_SPLITS)[:-1])
    sb_q, sb_k, sb_v, r_q, r_k, r_v, r_g, g_sb, g_ret = jnp.split(proj, idx, axis=-1)
    y_sb = stick_breaking_attention(sb_q.reshape(B, S, SB_HEADS, SB_HEAD_DIM),
                                    sb_k.reshape(B, S, SB_HEADS, SB_HEAD_DIM),
                                    sb_v.reshape(B, S, SB_HEADS, SB_HEAD_DIM)).reshape(B, S, SB_W)
    y_sb = y_sb @ w_sb_o
    rq = rotary(r_q.reshape(B, S, RET_HEADS, RET_QK_DIM))
    rk = rotary(r_k.reshape(B, S, RET_HEADS, RET_QK_DIM))
    y_ret = head_groupnorm(retention(rq, rk, r_v.reshape(B, S, RET_HEADS, RET_V_DIM))).reshape(B, S, RET_V_W)
    y_ret = (jax.nn.silu(r_g.astype(jnp.float32)) * y_ret).astype(h.dtype) @ w_ret_o
    merged = jax.nn.sigmoid(g_sb) * y_sb + jax.nn.sigmoid(g_ret) * y_ret
    return merged @ w_mix_out

def memory_cross_attention(h, m, w_cq, w_ckv, w_co):
    B, S, D = h.shape
    q = (h @ w_cq).reshape(B, S, X_HEADS, X_HEAD_DIM)
    kv = m @ w_ckv
    k = kv[..., :D].reshape(B, -1, X_HEADS, X_HEAD_DIM)
    v = kv[..., D:].reshape(B, -1, X_HEADS, X_HEAD_DIM)
    s = jnp.einsum('bqhd,bmhd->bhqm', q, k).astype(jnp.float32) * X_HEAD_DIM ** -0.5
    p = jax.nn.softmax(s, axis=-1).astype(v.dtype)
    o = jnp.einsum('bhqm,bmhd->bqhd', p, v).reshape(B, S, D)
    return o @ w_co

def moe_ffn(h, w_router, b_router, w1, b1, w2, b2):
    B, S, D = h.shape
    T = B * S
    A = T * TOP_K
    ht = h.reshape(T, D)
    logits = ht.astype(jnp.float32) @ w_router.astype(jnp.float32) + b_router.astype(jnp.float32)
    top_val, top_idx = lax.top_k(logits, TOP_K)
    gate = jax.nn.softmax(top_val, axis=-1)
    flat_e = top_idx.reshape(A)
    flat_tok = jnp.arange(A, dtype=jnp.int32) // TOP_K
    order = jnp.argsort(flat_e)
    sorted_e = flat_e[order]
    sorted_tok = flat_tok[order]
    sorted_gate = gate.reshape(A)[order]
    counts = jnp.bincount(flat_e, length=N_EXPERTS)
    padded = ((counts + EXPERT_BLOCK - 1) // EXPERT_BLOCK) * EXPERT_BLOCK
    pad_end = jnp.cumsum(padded)
    pad_start = pad_end - padded
    cnt_start = jnp.cumsum(counts) - counts
    row = pad_start[sorted_e] + (jnp.arange(A) - cnt_start[sorted_e])
    n_blocks = (A + N_EXPERTS * (EXPERT_BLOCK - 1) + EXPERT_BLOCK - 1) // EXPERT_BLOCK
    P = n_blocks * EXPERT_BLOCK
    row_tok = jnp.zeros((P,), jnp.int32).at[row].set(sorted_tok)
    block_e = jnp.minimum(jnp.searchsorted(pad_end, jnp.arange(n_blocks) * EXPERT_BLOCK, side='right'),
                          N_EXPERTS - 1)
    xin = ht[row_tok].reshape(n_blocks, EXPERT_BLOCK, D)

    def expert_block(args):
        xb, e = args
        hc = xb @ w1[e] + b1[e]
        glu = jnp.minimum(hc[..., :D_FF], SWIGLU_LIMIT)
        lin = jnp.clip(hc[..., D_FF:], -SWIGLU_LIMIT, SWIGLU_LIMIT)
        act = glu * jax.nn.sigmoid(SWIGLU_ALPHA * glu) * (lin + 1.0)
        return act @ w2[e] + b2[e]

    yrows = lax.map(expert_block, (xin, block_e)).reshape(P, D)
    y_assign = yrows[row] * sorted_gate[:, None].astype(yrows.dtype)
    out = jax.ops.segment_sum(y_assign, sorted_tok, num_segments=T)
    return out.reshape(B, S, D)

def setup_inputs(seed: int = 0) -> dict:
    key = jax.random.key(seed)
    ks = jax.random.split(key, 20)
    f32 = jnp.float32

    def w(k, shape, fan_in):
        return jax.random.normal(k, shape, f32) * fan_in ** -0.5

    def gain(k, shape):
        return 1.0 + 0.02 * jax.random.normal(k, shape, f32)

    L = DEPTH
    return {
        "x": jax.random.normal(ks[0], (BATCH, SEQ, D_MODEL), f32),
        "mem": jax.random.normal(ks[1], (BATCH, MEM_LEN, D_MODEL), f32),
        "g_mix": gain(ks[2], (L, D_MODEL)),
        "w_in": w(ks[3], (L, D_MODEL, IN_W), D_MODEL),
        "w_sb_o": w(ks[4], (L, SB_W, D_MODEL), SB_W),
        "w_ret_o": w(ks[5], (L, RET_V_W, D_MODEL), RET_V_W),
        "w_mix_out": w(ks[6], (L, D_MODEL, D_MODEL), D_MODEL),
        "g_xattn": gain(ks[7], (L, D_MODEL)),
        "g_mem": gain(ks[8], (L, D_MODEL)),
        "w_cq": w(ks[9], (L, D_MODEL, D_MODEL), D_MODEL),
        "w_ckv": w(ks[10], (L, D_MODEL, 2 * D_MODEL), D_MODEL),
        "w_co": w(ks[11], (L, D_MODEL, D_MODEL), D_MODEL),
        "g_moe": gain(ks[12], (L, D_MODEL)),
        "w_router": w(ks[13], (L, D_MODEL, N_EXPERTS), D_MODEL),
        "b_router": 0.01 * jax.random.normal(ks[14], (L, N_EXPERTS), f32),
        "w_exp_in": w(ks[15], (L, N_EXPERTS, D_MODEL, 2 * D_FF), D_MODEL),
        "b_exp_in": 0.01 * jax.random.normal(ks[16], (L, N_EXPERTS, 2 * D_FF), f32),
        "w_exp_out": w(ks[17], (L, N_EXPERTS, D_FF, D_MODEL), D_FF),
        "b_exp_out": 0.01 * jax.random.normal(ks[18], (L, N_EXPERTS, D_MODEL), f32),
        "g_final": gain(ks[19], (D_MODEL,)),
    }

def reference(x, mem, g_mix, w_in, w_sb_o, w_ret_o, w_mix_out, g_xattn, g_mem, w_cq, w_ckv, w_co,
              g_moe, w_router, b_router, w_exp_in, b_exp_in, w_exp_out, b_exp_out, g_final):
    for l in range(DEPTH):
        x = x + token_mixer(rmsnorm(x, g_mix[l]), w_in[l], w_sb_o[l], w_ret_o[l], w_mix_out[l])
        x = x + memory_cross_attention(rmsnorm(x, g_xattn[l]), rmsnorm(mem, g_mem[l]),
                                       w_cq[l], w_ckv[l], w_co[l])
        x = x + moe_ffn(rmsnorm(x, g_moe[l]), w_router[l], b_router[l],
                        w_exp_in[l], b_exp_in[l], w_exp_out[l], b_exp_out[l])
    return rmsnorm(x, g_final)


_drawn_inputs = setup_inputs


def setup_inputs(seed=0):
    import zlib

    import numpy as np

    out = dict(_drawn_inputs(seed))
    spreads = {}
    factors = {'g_xattn': 3.022,
     'g_mem': 4.384,
     'b_exp_in': 37.054,
     'b_exp_out': 42.805,
     'g_final': 8.027,
     'g_moe': 5.034,
     'b_router': 7.202}
    for name, (base, spread) in spreads.items():
        noise = np.random.default_rng([zlib.crc32(name.encode()), seed]).standard_normal(out[name].shape)
        drawn = base * np.exp(spread * noise) if base else spread * noise
        out[name] = __import__('jax').numpy.asarray(drawn.astype(out[name].dtype))
    for name, factor in factors.items():
        out[name] = (out[name] * factor).astype(out[name].dtype)
    return out
```

```python
from contextlib import ExitStack

import numpy as np

import concourse.bass as bass
from concourse import mybir

ALU = mybir.AluOpType
ACT = mybir.ActivationFunctionType
F32 = mybir.dt.float32
F32R = mybir.dt.float32r
U32 = mybir.dt.uint32
AX = mybir.AxisListType

P = 128
T = 512
TT = T // P
D = 1024
KT = D // P
M = 256
MT = M // P
HEADS = 8
XH = 4
XD = D // XH
NE = 32
TOPK = 4
DFF = 1024
EPS = 1e-5
LIMIT = 7.0
ALPHA = 1.702
NC = 4 * NE
OVER = T * TOPK // P - 1
RAW = 4
SPL = 3
CH = 2048
AHEAD = 2
EC = 12

SLABS = [("sbq", "T", 2, 4, T, "act"), ("sbk", "T", 2, 4, T, "act"), ("sbv", "N", 2, 4, 512, "act"),
         ("rq", "T", 2, 4, T, "act"), ("rk", "T", 2, 4, T, "act"),
         ("rv0", "N", 2, 4, 512, "act"), ("rv1", "N", 2, 4, 512, "act"),
         ("rg0", "N", 2, 4, 512, "act"), ("rg1", "N", 2, 4, 512, "act"),
         ("gs0", "T", 2, 4, T, "act"), ("gs1", "T", 2, 4, T, "act"),
         ("gr0", "T", 2, 4, T, "act"), ("gr1", "T", 2, 4, T, "act"),
         ("so0", "T", 1, 4, T, "dve"), ("ro0", "T", 2, 4, T, "dve"),
         ("so1", "T", 1, 4, T, "dve"), ("ro1", "T", 2, 4, T, "dve"),
         ("mo0", "N", 2, 4, 512, "dve"), ("mo1", "N", 2, 4, 512, "dve"),
         ("mk0", "T", 2, 4, M, "act"), ("mk1", "T", 2, 4, M, "act"),
         ("mv0", "N", 2, 2, 512, "act"), ("mv1", "N", 2, 2, 512, "act"),
         ("cq0", "T", 2, 4, T, "act"), ("cq1", "T", 2, 4, T, "act"),
         ("co0", "N", 2, 4, 512, "dve"), ("co1", "N", 2, 4, 512, "dve")]


class Slab:

    def __init__(self, spec, chunk0, tile0, prev):
        self.name, self.kind, self.chunks, self.tiles, self.cols, self.owner = spec
        self.chunk0 = chunk0
        self.tile0 = tile0
        self.out0 = prev.get(self.owner, 0)


def lay_slabs():
    slabs, chunk, tile, outs = {}, 0, 0, {"act": 0, "dve": 0}
    last_user = [None] * 4
    for spec in SLABS:
        s = Slab(spec, chunk, tile, outs)
        s.bank_free = [last_user[t] for t in range(s.tiles)]
        for t in range(s.tiles):
            last_user[t] = (s.owner, outs[s.owner] + t + 1)
        chunk += s.chunks
        tile += s.tiles - 1
        outs[s.owner] += s.tiles
        slabs[s.name] = s
    return slabs, chunk, outs


def constant_tables():
    i = np.arange(P)
    mats = np.zeros((8, P, P), np.float32)
    mats[0] = np.eye(P)
    mats[1] = -1.0 * (i[:, None] >= i[None, :])
    mats[2] = -1.0
    for m in range(P):
        d = m % 64
        mats[3, m + 32 if d < 32 else m - 32, m] = -1.0 if d < 32 else 1.0
    mats[4] = i[:, None] < i[None, :]
    mats[5] = 1.0
    mats[6] = i[None, :]
    mats[7, :64] = (i[:64, None] % NE) == (i[None, :] % NE)
    inv = np.float32(10000.0) ** (-np.arange(0, 64, 2, dtype=np.float32) / np.float32(64))
    ang = (np.arange(T, dtype=np.float32)[None, :] * inv[:, None]).astype(np.float32)
    rot = np.stack([np.tile(np.cos(ang), (4, 1)), np.tile(np.sin(ang), (4, 1))]).astype(np.float32)
    lg = np.log1p(-np.exp2(-5.0 - np.arange(HEADS)))
    u = np.arange(T)[None, :] - i[:, None]
    dec = np.where(u >= 0, np.exp(lg[:, None, None] * np.maximum(u, 0)), 0.0) / 8.0
    return {"c_mats": mats, "c_rot": rot, "c_dec": dec.astype(np.float32)}


def layer_kernel(nc, x, mem, g_mix, w_in, w_sb_o, w_ret_o, w_mix_out, g_xattn, g_mem, w_cq, w_ckv, w_co,
                 g_moe, w_router, b_router, w_exp_in, b_exp_in, w_exp_out, b_exp_out, g_final,
                 c_mats, c_rot, c_dec, out):
    slabs, DENSE, outs_total = lay_slabs()
    assert DENSE % RAW == 0 and EC % RAW == 0 and EC % SPL == 0
    y_main = nc.dram_tensor("y_main", [NE * P, D], F32, kind="Internal").ap()
    y_over = nc.dram_tensor("y_over", [(NC - NE) * P, D], F32, kind="Internal").ap()

    with ExitStack() as ctx:
        def sb(name, shape, dt=F32):
            return ctx.enter_context(nc.sbuf_tensor(name, shape, dt))

        def sem(name):
            return ctx.enter_context(nc.semaphore(name))

        raw = sb("raw", [P, RAW, CH])
        wh = sb("wh", [P, SPL, CH], F32R)
        wl = sb("wl", [P, SPL, CH], F32R)
        oph = sb("oph", [P, KT * T], F32R)
        opl = sb("opl", [P, KT * T], F32R)
        op2 = sb("op2", [P, 4096], F32R)
        pick = sb("pick", [P, TT, P], F32R)
        bsel = sb("bsel", [64, P], F32R)
        bias = sb("bias", [64, 3 * D], F32R)
        mats = sb("mats", [P, 4, P])
        small = sb("small", [P, 88])
        work = sb("work", [P, 15872])
        ps = ctx.enter_context(nc.psum_tensor("ps", [P, 8, 512], F32))

        ident, neg_from, neg_ones, rot_swap = (mats[:, n, :] for n in range(4))
        gmix_c, gxat_c, gmem_c = (small[:, 8 * n:8 * n + 8] for n in range(3))
        ss, rstd = small[:, 24:28], small[:, 28:32]
        msum, mrstd = small[:, 32:34], small[:, 34:36]
        retstat = small[:, 36:60]
        retmv = small[:, 60:68]
        retrs = small[:, 68:72]
        xmax = small[:, 72:76]
        xsum = small[:, 76:80]
        xrec = small[:, 80:84]
        cur = small[:, 84:88].rearrange("p (t o) -> p t o", t=TT)

        def w_(a, n):
            return work[:, a:a + n]

        def view(a, tiles, n):
            return w_(a, tiles * n).rearrange("p (t n) -> p t n", t=tiles)

        x_nat = view(0, TT, D)
        q_sb, k_sb, v_sb = view(0, 4, T), view(2048, 4, T), view(4096, TT, 512)
        abs_z = view(6144, 3, 512)
        soft = view(7680, 2, 1280)
        wts = view(10240, 2, 1280)
        q_r, k_r, v_r = view(0, 4, T), view(2048, 4, T), view(4096, TT, D)
        y_r = view(8192, TT, D)
        cosine, sine = w_(12288, T), w_(12800, T)
        rot_tmp = view(13312, 2, T)
        decay = view(12288, 2, T)
        scores = view(13312, 2, 1280)
        m_sb, m_ret = view(0, KT, T), view(4096, KT, T)
        res = view(8192, TT, D)
        xs2 = view(0, TT, D)
        q_x, k_x, v_x = view(0, KT, T), view(4096, KT, M), view(6144, MT, D)
        mem_nat = view(12288, MT, D)
        prob = view(12288, 4, M)
        prob_t = view(13312, 2, MT * T)
        h_nat = view(0, TT, D)
        bias_f = work[0:64, 4096:7168]
        h_t = view(4096, 2, D)
        g_moe_b = w_(7168, D)
        mats2 = view(12288, 4, P)
        before, ones, iota, exp_rows = (mats2[:, n, :] for n in range(4))
        logit = view(12800, TT, NE)
        at = 12928
        names = {}
        for name, n in (("top", 32), ("topi", 32), ("idxf", 16), ("gate", 16), ("gsum", 4), ("grec", 4), ("nmax", 4),
                        ("rk", 16), ("jj", 16), ("jm", 16), ("rowf", 16), ("rowi", 16), ("rowj", 16), ("gate2", 16), ("oh", 512), ("oh2", 512), ("sel", 128),
                        ("rank", 128), ("slot", 128), ("cnt", 32), ("slots", 512), ("brt", 32), ("tabi", 16), ("nov", 1)):
            names[name] = w_(at, n)
            at += n
        assert at <= 15616
        w_rt = view(15616, KT, NE)
        top = names["top"].rearrange("p (t n) -> p t n", t=TT)
        topi = names["topi"].bitcast(U32).rearrange("p (t n) -> p t n", t=TT)
        idxf = names["idxf"].rearrange("p (t n) -> p t n", t=TT)
        gate = names["gate"].rearrange("p (t n) -> p t n", t=TT)
        rowi, rowj = names["rowi"].bitcast(U32), names["rowj"].bitcast(U32)
        oh = names["oh"].rearrange("p (t k e) -> p t k e", t=TT, k=TOPK)
        oh2 = names["oh2"].rearrange("p (t k e) -> p t k e", t=TT, k=TOPK)
        sel = names["sel"].rearrange("p (t e) -> p t e", t=TT)
        rank = names["rank"].rearrange("p (t e) -> p t e", t=TT)
        slot = names["slot"].rearrange("p (t e) -> p t e", t=TT)
        slots = names["slots"].rearrange("p (t c) -> p t c", t=TT)
        table = names["tabi"][0:1, :].bitcast(U32)
        n_over = names["nov"][0:1, :].bitcast(U32)
        ov_ex, ov_pos, ov_c = (work[0:1, 4096 + 96 * n:4096 + 96 * n + 96] for n in range(3))
        ov_eq = work[0:1, 4608:4608 + 16 * 96].rearrange("p (i c) -> p i c", i=16)
        ov_tab = work[0:1, 6400:6416]
        x_h = op2[:, 0:1024].rearrange("p (t n) -> p t n", t=KT)
        x_l = op2[:, 1024:2048].rearrange("p (t n) -> p t n", t=KT)
        a_h = op2[:, 2048:3072].rearrange("p (t n) -> p t n", t=KT)
        a_l = op2[:, 3072:4096].rearrange("p (t n) -> p t n", t=KT)
        glu, sig, lin, act_o = (view(1024 * n, 2, 512) for n in range(4))
        y_sb = w_(4096, D)
        y_rows = view(0, 4, D)
        g_fin_b = w_(5120, D)
        o_sb = view(6144, 2, D)

        op_h = oph[:, :].rearrange("p (t n) -> p t n", t=KT)
        op_l = opl[:, :].rearrange("p (t n) -> p t n", t=KT)
        op2_h = op2[:, 0:2048].rearrange("p (t n) -> p t n", t=4)
        op2_l = op2[:, 2048:4096].rearrange("p (t n) -> p t n", t=4)
        opm_h = op2[:, 0:2048].rearrange("p (t n) -> p t n", t=KT)
        opm_l = op2[:, 2048:4096].rearrange("p (t n) -> p t n", t=KT)
        hn_h = oph[:, :].rearrange("p (t n) -> p t n", t=TT)
        hn_l = opl[:, :].rearrange("p (t n) -> p t n", t=TT)

        w_landed = [sem(f"w_landed{n}") for n in range(RAW)]
        w_hi, w_lo, w_used = sem("w_hi"), sem("w_lo"), sem("w_used")
        in_x, in_mats, in_cols, in_rot, in_mem, in_res = (
            sem(n) for n in ("in_x", "in_mats", "in_cols", "in_rot", "in_mem", "in_res"))
        in_dec = [sem("in_dec0"), sem("in_dec1")]
        in_moe, in_bias, in_gfin = sem("in_moe"), sem("in_bias"), sem("in_gfin")
        act_chain, dve_chain = sem("act_chain"), sem("dve_chain")
        tile_done = sem("tile_done")
        tile_out = {"act": sem("tile_out_act"), "dve": sem("tile_out_dve")}
        tr_done, op_hi, op_lo = sem("tr_done"), sem("op_hi"), sem("op_lo")
        z_done, soft_raw, soft_done, zc_done, wexp_done, wts_done, o_done, o_hi, o_lo = (
            sem(n) for n in ("z_done", "soft_raw", "soft_done", "zc_done", "wexp_done", "wts_done", "o_done", "o_hi", "o_lo"))
        ln_done = sem("ln_done")
        rot_done, rot_out = sem("rot_done"), sem("rot_out")
        sc_done, sc_out, ro_done, ro_out = (sem(n) for n in ("sc_done", "sc_out", "ro_done", "ro_out"))
        rs_var, rs_sqrt = sem("rs_var"), sem("rs_sqrt")
        n_sq, n_inv, n_sqrt, n_xs = (sem(n) for n in ("n_sq", "n_inv", "n_sqrt", "n_xs"))
        xs_done, xs_max, xs_exp, xs_prob, xt_done, xt_out, xo_done = (
            sem(n) for n in ("xs_done", "xs_max", "xs_exp", "xs_prob", "xt_done", "xt_out", "xo_done"))
        ht_done, ht_out, lg_done, gate_exp, rank_in, rank_done, route_done = (
            sem(n) for n in ("ht_done", "ht_out", "lg_done", "gate_exp", "rank_in", "rank_done", "route_done"))
        nat_ready, nat_hi, nat_lo, b_hi, b_lo = (sem(n) for n in ("nat_ready", "nat_hi", "nat_lo", "b_hi", "b_lo"))
        cur_ready, pick_ready, bsel_ready, bsel_used = (sem(n) for n in ("cur_ready", "pick_ready", "bsel_ready", "bsel_used"))
        gath, x_out, glu_step, sig_done, at_done, a_hi, a_lo = (
            sem(n) for n in ("gath", "x_out", "glu_step", "sig_done", "at_done", "a_hi", "a_lo"))
        y_evac, y_stored = sem("y_evac"), sem("y_stored")
        pool_turn = sem("pool_turn")
        zero_ready, over_stored, over_used = (sem(n) for n in ("zero_ready", "over_stored", "over_used"))
        row_in = [sem(f"row_in{n}") for n in range(4)]
        over_in = [sem(f"over_in{n}") for n in range(4)]
        row_used, f_out = sem("row_used"), sem("f_out")
        stored = [sem("stored0"), sem("stored1")]

        def dense_source(g):
            for s in slabs.values():
                if s.chunk0 <= g < s.chunk0 + s.chunks:
                    break
            half, name = g - s.chunk0, s.name
            order = list(slabs)
            if order.index(name) < 13:
                src, col = w_in[0], order.index(name)
            else:
                src = {"so": w_sb_o, "ro": w_ret_o, "mo": w_mix_out, "mk": w_ckv, "mv": w_ckv,
                       "cq": w_cq, "co": w_co}[name[:2]][0]
                col = int(name[2]) + (2 if name[:2] == "mv" else 0)
            return src[half * 512:(half + 1) * 512, col * 512:(col + 1) * 512].rearrange("(a p) n -> p a n", p=P)

        def expert_sources(e):
            w1 = w_exp_in[0, bass.ds(e, 1), :, :].rearrange("o (a p) n -> p (o a) n", p=P)
            w2 = w_exp_out[0, bass.ds(e, 1), :, :].rearrange("o (a p) n -> p (o a) n", p=P)
            for half in range(2):
                for gl in range(2):
                    col = gl * DFF + half * 512
                    for a in (0, 4):
                        yield w1[:, a:a + 4, col:col + 512], "p (a n) -> p a n", 4
            for q in range(4):
                yield w2[:, 2 * q:2 * q + 2, :], "p (a n) -> p a n", 2

        class Chain:

            def __init__(self, eng, s):
                self.eng, self.s, self.n = eng, s, 0

            def __call__(self, ins):
                ins.then_inc(self.s, 1)
                self.n += 1

            def wait(self):
                self.eng.wait_ge(self.s, self.n)

        def head_out_act(act, h):
            act.wait_ge(o_done, h + 1)
            r = 64 * (h % 2)
            nc.scalar.activation(op2_h[r:r + 64, h // 2, :], ps[r:r + 64, 6 + h % 2, :], ACT.Copy).then_inc(o_hi, 1)

        def cross_hi(act, hd):
            for dt in range(2):
                act.wait_ge(xo_done, 2 * hd + dt + 1)
                nc.scalar.activation(op_h[:, 2 * hd + dt, :], ps[:, 6 + dt, :], ACT.Copy).then_inc(op_hi, 1)

        def head_out_dve(dve, h):
            dve.wait_ge(o_hi, h + 1)
            r = 64 * (h % 2)
            nc.vector.tensor_tensor(op2_l[r:r + 64, h // 2, :], ps[r:r + 64, 6 + h % 2, :], op2_h[r:r + 64, h // 2, :],
                                    ALU.subtract).then_inc(o_lo, 1)

        def cross_lo(dve, hd):
            for dt in range(2):
                k = 2 * hd + dt
                dve.wait_ge(op_hi, 5 * KT + k + 1)
                nc.vector.tensor_tensor(op_l[:, k, :], ps[:, 6 + dt, :], op_h[:, k, :], ALU.subtract).then_inc(op_lo, 1)

        def head_out(pe, h):
            pe.wait_ge(wts_done, 4 * h + 4)
            if h >= 2:
                pe.wait_ge(o_lo, h - 1)
            for kb in range(4):
                n = T - P * kb
                ins = nc.tensor.matmul(ps[:, 6 + h % 2, kb * P:T], v_sb[:, kb, (h // 2) * P:(h // 2 + 1) * P],
                                       wts[:, h % 2, OFF[kb]:OFF[kb] + n], start=(kb == 0), stop=(kb == 3),
                                       skip_group_check=True)
            ins.then_inc(o_done, 1)

        def cross_out(pe, hd):
            pe.wait_ge(xt_out, TT * (hd + 1))
            for dt in range(2):
                if hd >= 1:
                    pe.wait_ge(op_lo, 5 * KT + 2 * (hd - 1) + dt + 1)
                for m in range(MT):
                    a = hd * XD + dt * P
                    ins = nc.tensor.matmul(ps[:, 6 + dt, :], v_x[:, m, a:a + P],
                                           prob_t[:, hd % 2, m * T:(m + 1) * T], start=(m == 0), stop=(m == MT - 1))
                ins.then_inc(xo_done, 1)

        block = ctx.enter_context(nc.Block())

        @block.sync
        def _(sp):
            sp.dma_start(x_nat, x[0].rearrange("(t p) d -> p t d", p=P)).then_inc(in_x, 16)
            for g in range(DENSE):
                if g >= RAW:
                    sp.wait_ge(w_lo, g - RAW + 1)
                sp.dma_start(raw[:, g % RAW, :].rearrange("p (a n) -> p a n", a=4),
                             dense_source(g)).then_inc(w_landed[g % RAW], 16)

            def load_expert(i, e):
                for c, (src, pat, a) in enumerate(expert_sources(e)):
                    sp.wait_ge(w_lo, i * EC + (DENSE + c - RAW + 1))
                    sp.dma_start(raw[:, c % RAW, :].rearrange(pat, a=a), src).then_inc(w_landed[c % RAW], 16)

            with sp.Fori(0, NE) as i:
                load_expert(i, i)
            sp.wait_ge(route_done, 3)
            n = sp.value_load(n_over, min_val=0, max_val=OVER)
            with sp.If(n > 0):
                with sp.Fori(0, OVER) as j:
                    with sp.If(j < n):
                        c = sp.value_load(table[0:1, bass.ds(j, 1)], min_val=0, max_val=NC - NE - 1)
                        load_expert(j + NE, c % NE)
            for tt in range(TT):
                sp.wait_ge(f_out, tt + 1)
                sp.dma_start(out[0, tt * P:(tt + 1) * P, :], o_sb[:, tt % 2, :]).then_inc(stored[tt % 2], 16)
            sp.wait_ge(stored[0], 32)
            sp.wait_ge(stored[1], 32)

        @block.gpsimd
        def _(pool):
            pool.dma_start(mats[:, :, :], c_mats[0:4].rearrange("c p n -> p c n")).then_inc(in_mats, 16)
            for dst, src in ((gmix_c, g_mix), (gxat_c, g_xattn), (gmem_c, g_mem)):
                with nc.allow_non_contiguous_dma(reason="a gain for each channel"):
                    pool.dma_start(dst, src[0].rearrange("(k p) -> p k", p=P)).then_inc(in_cols, 16)

            def keep_before(view_):
                return nc.gpsimd.affine_select(out=view_, in_=view_, pattern=[[1, P]], compare_op=ALU.is_gt, fill=0.0,
                                               base=0, channel_multiplier=-1)

            units = [(h, kb) for h in range(HEADS) for kb in (3, 2, 1, 0)]
            for step in range(len(units) + 3):
                if step < len(units):
                    h, kb = units[step]
                    pool.wait_ge(soft_raw, step + 1)
                    keep_before(soft[:, h % 2, OFF[kb]:OFF[kb] + P]).then_inc(soft_done, 1)
                if step >= 3:
                    h, kb = units[step - 3]
                    pool.wait_ge(wexp_done, step - 3 + 1)
                    keep_before(wts[:, h % 2, OFF[kb]:OFF[kb] + P]).then_inc(wts_done, 1)
            pool.wait_ge(o_done, HEADS)
            pool.dma_start(w_(12288, 2 * T).rearrange("p (c n) -> p c n", c=2),
                           c_rot.rearrange("c p n -> p c n")).then_inc(in_rot, 16)
            for h in range(HEADS):
                if h == 0:
                    pool.wait_ge(rot_out, 8)
                if h >= 2:
                    pool.wait_ge(sc_out, 4 * (h - 1))
                pool.dma_start(decay[:, h % 2, :], c_dec[h]).then_inc(in_dec[h % 2], 16)
            pool.wait_ge(tr_done, TR_RET)
            pool.dma_start(res, x[0].rearrange("(t p) d -> p t d", p=P)).then_inc(in_res, 16)
            pool.dma_start(mem_nat, mem[0].rearrange("(t p) d -> p t d", p=P)).then_inc(in_mem, 16)
            pool.wait_ge(xo_done, 2 * XH)
            pool.dma_start(mats2, c_mats[4:8].rearrange("c p n -> p c n")).then_inc(in_moe, 16)
            pool.dma_start(names["brt"], b_router[0].partition_broadcast(P)).then_inc(in_moe, 16)
            pool.dma_start(w_rt, w_router[0].rearrange("(k p) e -> p k e", p=P)).then_inc(in_moe, 16)
            pool.dma_start(g_moe_b, g_moe[0].partition_broadcast(P)).then_inc(in_moe, 16)
            for r in range(2):
                pool.dma_start(bias_f[32 * r:32 * r + 32, 0:2 * D], b_exp_in[0]).then_inc(in_bias, 16)
                pool.dma_start(bias_f[32 * r:32 * r + 32, 2 * D:3 * D], b_exp_out[0]).then_inc(in_bias, 16)

            def choose(i, c, first=False):
                if not first:
                    pool.wait_ge(gath, 4 * i)
                nc.gpsimd.tensor_copy(cur, slots[:, :, bass.ds(c, 1)]).then_inc(cur_ready, 1)
                pool.wait_ge(cur_ready, i + 1)
                pool.sem_inc(pool_turn, 1)
                for t in range(TT):
                    nc.gpsimd.tensor_scalar(pick[:, t, :], iota, cur[:, t, :], None, ALU.is_equal).then_inc(pick_ready, 1)
                if not first:
                    pool.wait_ge(bsel_used, i)
                nc.gpsimd.tensor_copy(bsel[:, :], exp_rows[0:64, bass.ds(c, 1)].to_broadcast([64, P])).then_inc(bsel_ready, 1)

            pool.wait_ge(in_moe, 64)
            pool.wait_ge(route_done, 3)
            choose(0, 0, first=True)
            with pool.Fori(1, NE) as i:
                choose(i, i)
            n = pool.value_load(n_over, min_val=0, max_val=OVER)
            with pool.If(n > 0):
                pool.wait_ge(y_stored, NE * 16)
                nc.gpsimd.memset(y_sb, 0.0).then_inc(zero_ready, 1)
                pool.wait_ge(zero_ready, 1)
                pool.dma_start(y_over.rearrange("(c p) d -> p c d", p=P),
                               y_sb.unsqueeze(1).to_broadcast([P, NC - NE, D])).then_inc(over_stored, 16)
                with pool.Fori(0, OVER) as j:
                    with pool.If(j < n):
                        c = pool.value_load(table[0:1, bass.ds(j, 1)], min_val=0, max_val=NC - NE - 1)
                        choose(j + NE, c + NE)
                pool.wait_ge(over_stored, n * 16 + 16)
                pool.sem_inc(pool_turn, 1)
                for u in range(TT * TOPK):
                    if u >= 4:
                        pool.wait_ge(over_used, u - 3)
                    pool.indirect_dma_start(out=y_rows[:, u % 4, :], out_offset=None, in_=y_over,
                                            in_offset=bass.IndirectOffsetOnAxis(ap=rowj[:, u:u + 1], axis=0)
                                            ).then_inc(over_in[u % 4], 16)
                pool.wait_ge(over_used, TT * TOPK)
            pool.wait_ge(y_stored, NE * 16)
            pool.dma_start(g_fin_b, g_final.partition_broadcast(P)).then_inc(in_gfin, 16)
            for u in range(TT * TOPK):
                if u >= 4:
                    pool.wait_ge(row_used, u - 3)
                pool.indirect_dma_start(out=y_rows[:, u % 4, :], out_offset=None, in_=y_main,
                                        in_offset=bass.IndirectOffsetOnAxis(ap=rowi[:, u:u + 1], axis=0)
                                        ).then_inc(row_in[u % 4], 16)

        @block.scalar
        def _(act):
            chain = Chain(act, act_chain)

            def split(g):
                slot = g % SPL
                act.wait_ge(w_landed[g % RAW], 16 * (g // RAW + 1))
                if g >= SPL:
                    act.wait_ge(w_used, g - SPL + 1)
                nc.scalar.activation(wh[:, slot, :], raw[:, g % RAW, :], ACT.Copy).then_inc(w_hi, 1)

            def take(name, f):
                s = slabs[name]
                for c in range(s.chunks):
                    split(s.chunk0 + c + AHEAD)
                if s.owner != "act":
                    return
                for t in range(s.tiles):
                    if t < s.tiles - 1:
                        act.wait_ge(tile_done, s.tile0 + t + 1)
                    else:
                        act.wait_ge(w_used, s.chunk0 + s.chunks)
                    f(t).then_inc(tile_out["act"], 1)

            def norm_stats(xv, tiles, acc, rs, sq0, inv_n):
                for t in range(tiles):
                    if t:
                        act.wait_ge(n_sq, sq0 + t)
                    nc.scalar.activation(ps[:, 6:8, :].rearrange("p a n -> p (a n)"), xv[:, t, :], ACT.Square,
                                         accum_out=acc[:, t:t + 1]).then_inc(n_sq, 1)
                act.wait_ge(n_inv, inv_n)
                nc.scalar.activation(rs, rs, ACT.Sqrt).then_inc(n_sqrt, 1)

            def operand_hi(dst, n0, tiles, cols, gain=None, first_tr=0):
                for k in range(tiles):
                    act.wait_ge(tr_done, first_tr + k + 1)
                    src = ps[:, 4 + k % 4, 0:cols]
                    nc.scalar.activation(dst[:, k, :], src, ACT.Copy,
                                         scale=1.0 if gain is None else gain[:, k:k + 1]).then_inc(op_hi, 1)

            act.wait_ge(in_x, 16)
            norm_stats(x_nat, TT, ss, rstd, 0, 1)
            split(0)
            split(1)
            act.wait_ge(in_cols, 48)
            operand_hi(op_h, 0, KT, T, gmix_c, 0)

            def copy(dst, scale=1.0):
                def f(t):
                    return nc.scalar.activation(dst[:, t, :], ps[:, t, 0:dst.shape[2]], ACT.Copy, scale=scale)
                return f

            take("sbq", copy(q_sb, 64 ** -0.5))
            take("sbk", copy(k_sb))
            take("sbv", copy(v_sb))
            act.preload_act_table_set("natural_log_exp_and_others")
            units = [(h, kb) for h in range(HEADS) for kb in (3, 2, 1, 0)]
            for step in range(len(units) + 3):
                if step < len(units):
                    h, kb = units[step]
                    n = T - P * kb
                    z = abs_z[:, step % 3, 0:n]
                    act.wait_ge(z_done, step + 1)
                    if step >= 3:
                        act.wait_ge(soft_raw, step - 2)
                    chain(nc.scalar.activation(z, ps[:, step % 6, 0:n], ACT.Abs))
                    chain.wait()
                    chain(nc.scalar.activation(z, z, ACT.Exp, scale=-1.0))
                    chain.wait()
                    nc.scalar.activation(z, z, ACT.Ln, bias=1.0).then_inc(ln_done, 1)
                if step >= 3:
                    u = step - 3
                    h, kb = units[u]
                    n = T - P * kb
                    act.wait_ge(zc_done, u + 1)
                    if h >= 2 and kb == 3:
                        act.wait_ge(o_done, h - 1)
                    nc.scalar.activation(wts[:, h % 2, OFF[kb]:OFF[kb] + n], ps[:, u % 6, 0:n],
                                         ACT.Exp).then_inc(wexp_done, 1)
                if step >= 7 and (step - 7) % 4 == 0:
                    head_out_act(act, (step - 7) // 4)
            head_out_act(act, HEADS - 1)
            take("rq", copy(q_r))
            take("rk", copy(k_r))
            for n in range(2):
                def into(t, n=n):
                    return nc.scalar.activation(v_r[:, t, n * 512:(n + 1) * 512], ps[:, t, :], ACT.Copy)
                take(f"rv{n}", into)
            for n in range(2):
                def into(t, n=n):
                    return nc.scalar.activation(y_r[:, t, n * 512:(n + 1) * 512], ps[:, t, :], ACT.Silu)
                take(f"rg{n}", into)
            for h in range(HEADS):
                act.wait_ge(rs_var, h + 1)
                nc.scalar.activation(retrs, retrs, ACT.Sqrt).then_inc(rs_sqrt, 1)
            for n in range(2):
                def into(t, n=n):
                    return nc.scalar.activation(m_sb[:, 4 * n + t, :], ps[:, t, :], ACT.Sigmoid)
                take(f"gs{n}", into)
            for n in range(2):
                def into(t, n=n):
                    return nc.scalar.activation(m_ret[:, 4 * n + t, :], ps[:, t, :], ACT.Sigmoid)
                take(f"gr{n}", into)
            operand_hi(op_h, 8, KT, T, None, KT)
            for name in ("so0", "ro0", "so1", "ro1"):
                take(name, None)
            act.wait_ge(tile_out["dve"], MERGED)
            act.wait_ge(w_used, slabs["ro1"].chunk0 + 2)
            for k in range(KT):
                nc.scalar.activation(op_h[:, k, :], m_sb[:, k, :], ACT.Copy).then_inc(op_hi, 1)
            act.wait_ge(in_mem, 16)
            norm_stats(mem_nat, MT, msum, mrstd, 4, 2)
            operand_hi(opm_h, 24, KT, M, gmem_c, 2 * KT)
            take("mo0", None)
            take("mo1", None)
            act.wait_ge(tile_out["dve"], MIXED)
            norm_stats(res, TT, ss, rstd, 6, 3)
            for n in range(2):
                def into(t, n=n):
                    return nc.scalar.activation(k_x[:, 4 * n + t, :], ps[:, t, 0:M], ACT.Copy)
                take(f"mk{n}", into)
            for n in range(2):
                def into(t, n=n):
                    return nc.scalar.activation(v_x[:, t, n * 512:(n + 1) * 512], ps[:, t, :], ACT.Copy)
                take(f"mv{n}", into)
            operand_hi(op_h, 32, KT, T, gxat_c, 3 * KT)
            for n in range(2):
                def into(t, n=n):
                    return nc.scalar.activation(q_x[:, 4 * n + t, :], ps[:, t, :], ACT.Copy, scale=XD ** -0.5)
                take(f"cq{n}", into)
            for u in range(XH * TT):
                act.wait_ge(xs_max, u + 1)
                nc.scalar.activation(prob[:, u % 4, :], ps[:, u % 4, 0:M], ACT.Exp, bias=xmax[:, u % 4:u % 4 + 1],
                                     accum_out=xsum[:, u % 4:u % 4 + 1]).then_inc(xs_exp, 1)
                if u % TT == 3 and u > TT:
                    cross_hi(act, u // TT - 1)
            cross_hi(act, XH - 1)
            take("co0", None)
            take("co1", None)
            act.wait_ge(tile_out["dve"], outs_total["dve"])
            norm_stats(res, TT, ss, rstd, 10, 4)
            act.wait_ge(in_bias, 64)
            nc.scalar.activation(bias[:, :], bias_f, ACT.Copy).then_inc(b_hi, 1)
            for t in range(TT):
                act.wait_ge(nat_ready, t + 1)
                nc.scalar.activation(hn_h[:, t, :], h_nat[:, t, :], ACT.Copy).then_inc(nat_hi, 1)
            for t in range(TT):
                act.wait_ge(ht_done, t + 1)
                if t == 0:
                    act.wait_ge(b_lo, 1)
                if t >= 2:
                    act.wait_ge(lg_done, t - 1)
                nc.scalar.activation(h_t[:, t % 2, :], ps[:, 4 + 2 * (t % 2):6 + 2 * (t % 2), :].rearrange("p a n -> p (a n)"),
                                     ACT.Copy).then_inc(ht_out, 1)
            act.wait_ge(route_done, 1)
            for t in range(TT):
                ins = nc.scalar.activation(gate[:, t, :], top[:, t, 0:TOPK], ACT.Exp, bias=names["nmax"][:, t:t + 1],
                                           accum_out=names["gsum"][:, t:t + 1])
                ins.then_inc(gate_exp, 1)

            act.preload_act_table_set("sigmoid_and_others")

            def esplit(i, c):
                cc = c % EC
                act.wait_ge(w_landed[cc % RAW], (i * (EC // RAW) + (DENSE + c) // RAW + 1) * 16)
                act.wait_ge(w_used, i * EC + (DENSE + c - SPL + 1))
                nc.scalar.activation(wh[:, (DENSE + c) % SPL, :], raw[:, cc % RAW, :], ACT.Copy).then_inc(w_hi, 1)

            def x_evac(i, u):
                act.wait_ge(gath, i * 4 + (u + 1))
                dst = (x_h, x_l)[u // 2][:, 4 * (u % 2):4 * (u % 2) + 4, :]
                nc.scalar.activation(dst, ps[:, 6 + u % 2, :].rearrange("p (a n) -> p a n", a=4), ACT.Copy).then_inc(x_out, 1)

            def y_take(i):
                for n in range(2):
                    nc.scalar.activation(y_sb[:, n * 512:(n + 1) * 512], ps[:, 4 + n, :], ACT.Copy).then_inc(y_evac, 1)

            def y_store(i, c, dram, done):
                act.wait_ge(y_evac, i * 2 + 2)
                act.dma_start(dram.rearrange("(c p) d -> c p d", p=P)[bass.ds(c, 1), :, :].rearrange("o p d -> p (o d)"),
                              y_sb[:, :]).then_inc(done, 16)

            def expert(i, later=False, first=False, last=False, alone=False):
                if not alone and not first:
                    esplit(i, 2)
                    x_evac(i, 3)
                    act.wait_ge(w_used, i * EC + DENSE)
                    if later:
                        act.wait_ge(y_stored, i * 16 - 16)
                    y_take(i - 1)
                    y_store(i - 1, i - 1, y_main, y_stored)
                else:
                    if alone:
                        esplit(i, 0)
                        esplit(i, 1)
                        for u in range(4):
                            x_evac(i, u)
                    esplit(i, 2)
                for step in range(1, EC):
                    if step == 10:
                        act_hi(i, 1)
                        if not (last or alone):
                            x_evac(i + 1, 0)
                    if step == 11 and not (last or alone):
                        x_evac(i + 1, 1)
                        x_evac(i + 1, 2)
                    if step + AHEAD < EC or not (last or alone):
                        esplit(i, step + AHEAD)
                    if step == 2 or step == 6:
                        half = step // 4
                        act.wait_ge(glu_step, i * 8 + (4 * half + 1))
                        nc.scalar.activation(sig[:, half, :], glu[:, half, :], ACT.Sigmoid, scale=ALPHA).then_inc(sig_done, 1)
                    if step == 6:
                        act_hi(i, 0)

            def act_hi(i, half):
                act.wait_ge(at_done, i * 2 + (half + 1))
                nc.scalar.activation(a_h[:, 4 * half:4 * half + 4, :], ps[:, 6 + half, :].rearrange("p (a n) -> p a n", a=4),
                                     ACT.Copy).then_inc(a_hi, 1)

            for u in range(4):
                x_evac(0, u)
            expert(0, first=True)
            expert(1)
            with act.Fori(2, NE - 1) as i:
                expert(i, later=True)
            expert(NE - 1, later=True, last=True)
            act.wait_ge(w_used, NE * EC + DENSE)
            act.wait_ge(y_stored, NE * 16 - 16)
            y_take(NE - 1)
            y_store(NE - 1, NE - 1, y_main, y_stored)
            n = act.value_load(n_over, min_val=0, max_val=OVER)
            with act.If(n > 0):
                with act.Fori(0, OVER) as j:
                    with act.If(j < n):
                        c = act.value_load(table[0:1, bass.ds(j, 1)], min_val=0, max_val=NC - NE - 1)
                        expert(j + NE, alone=True)
                        act.wait_ge(w_used, j * EC + ((NE + 1) * EC + DENSE))
                        act.wait_ge(over_stored, j * 16 + 16)
                        y_take(j + NE)
                        y_store(j + NE, c, y_over, over_stored)
            act.preload_act_table_set("sqrt_and_others")
            for t in range(TT):
                act.wait_ge(row_used, 4 * t + 4)
                nc.scalar.activation(ps[:, 6:8, :].rearrange("p a n -> p (a n)"), res[:, t, :], ACT.Square,
                                     accum_out=ss[:, t:t + 1]).then_inc(n_sq, 1)
                act.wait_ge(n_inv, 5 + t)
                nc.scalar.activation(rstd[:, t:t + 1], rstd[:, t:t + 1], ACT.Sqrt).then_inc(n_sqrt, 1)

        @block.vector
        def _(dve):
            chain = Chain(dve, dve_chain)

            def split(g):
                dve.wait_ge(w_hi, g + 1)
                slot = g % SPL
                nc.vector.tensor_tensor(wl[:, slot, :], raw[:, g % RAW, :], wh[:, slot, :], ALU.subtract).then_inc(w_lo, 1)

            def take(name, f):
                s = slabs[name]
                for c in range(s.chunks):
                    split(s.chunk0 + c + AHEAD)
                if s.owner != "dve":
                    return
                for t in range(s.tiles):
                    if t < s.tiles - 1:
                        dve.wait_ge(tile_done, s.tile0 + t + 1)
                    else:
                        dve.wait_ge(w_used, s.chunk0 + s.chunks)
                    f(t).then_inc(tile_out["dve"], 1)

            def norm_scale(xv, dst, tiles, acc, rs, sq_n, inv_n):
                dve.wait_ge(n_sq, sq_n)
                chain(nc.vector.tensor_scalar(rs, acc, 1.0 / D, EPS, ALU.mult, ALU.add))
                chain.wait()
                nc.vector.reciprocal(rs, rs).then_inc(n_inv, 1)
                dve.wait_ge(n_sqrt, inv_n)
                for t in range(tiles):
                    nc.vector.tensor_scalar(dst[:, t, :], xv[:, t, :], rs[:, t:t + 1], None, ALU.mult).then_inc(n_xs, 1)

            def operand_lo(dst, hi, n0, tiles, cols, gain=None):
                for k in range(tiles):
                    dve.wait_ge(op_hi, n0 + k + 1)
                    src = ps[:, 4 + k % 4, 0:cols]
                    if gain is None:
                        ins = nc.vector.tensor_tensor(dst[:, k, :], src, hi[:, k, :], ALU.subtract)
                    else:
                        ins = nc.vector.scalar_tensor_tensor(dst[:, k, :], src, gain[:, k:k + 1], hi[:, k, :],
                                                             ALU.mult, ALU.subtract)
                    ins.then_inc(op_lo, 1)

            norm_scale(x_nat, x_nat, TT, ss, rstd, 4, 1)
            split(0)
            split(1)
            operand_lo(op_l, op_h, 0, KT, T, gmix_c)
            for name in ("sbq", "sbk", "sbv"):
                take(name, None)
            units = [(h, kb) for h in range(HEADS) for kb in (3, 2, 1, 0)]
            for step in range(len(units) + 1):
                if step >= 1:
                    u = step - 1
                    h, kb = units[u]
                    n = T - P * kb
                    dve.wait_ge(ln_done, u + 1)
                    if h >= 2 and kb == 3:
                        dve.wait_ge(zc_done, 4 * (h - 1))
                    nc.vector.scalar_tensor_tensor(soft[:, h % 2, OFF[kb]:OFF[kb] + n], ps[:, u % 6, 0:n], 0.0,
                                                   abs_z[:, u % 3, 0:n], ALU.max, ALU.add).then_inc(soft_raw, 1)
                if step >= 8 and step % 4 == 0:
                    head_out_dve(dve, step // 4 - 2)
            head_out_dve(dve, HEADS - 1)
            take("rq", None)
            take("rk", None)
            dve.wait_ge(in_rot, 16)
            for u in range(8):
                v = (q_r, k_r)[u // 4][:, u % 4, :]
                dve.wait_ge(rot_done, u + 1)
                if u >= 2:
                    dve.wait_ge(rot_out, u - 1)
                chain(nc.vector.tensor_tensor(rot_tmp[:, u % 2, :], ps[:, 4 + u % 4, :], sine, ALU.mult))
                chain(nc.vector.tensor_tensor(v, v, cosine, ALU.mult))
                chain.wait()
                nc.vector.tensor_tensor(v, v, rot_tmp[:, u % 2, :], ALU.add).then_inc(rot_out, 1)
            for name in ("rv0", "rv1", "rg0", "rg1"):
                take(name, None)
            for h in range(HEADS + 1):
                if h < HEADS:
                    dve.wait_ge(in_dec[h % 2], 16 * (h // 2 + 1))
                    if h >= 2:
                        dve.wait_ge(ro_done, h - 1)
                    for kb in range(4):
                        n = T - P * kb
                        dve.wait_ge(sc_done, 4 * h + kb + 1)
                        nc.vector.tensor_tensor(scores[:, h % 2, OFFA[kb]:OFFA[kb] + n], ps[:, 4 + kb, 0:n],
                                                decay[:, h % 2, 0:n], ALU.mult).then_inc(sc_out, 1)
                if h >= 1:
                    g = h - 1
                    bank = ps[:, g % 2, :].rearrange("p (t n) -> p t n", t=TT)
                    dve.wait_ge(ro_done, g + 1)
                    for t in range(TT):
                        chain(nc.vector.bn_stats(retstat[:, 6 * t:6 * t + 6], bank[:, t, :]))
                    chain.wait()
                    for t in range(TT):
                        chain(nc.vector.bn_aggr(retmv[:, 2 * t:2 * t + 2], retstat[:, 6 * t:6 * t + 6]))
                    chain.wait()
                    mv = retmv.rearrange("p (t c) -> p c t", t=TT)
                    chain(nc.vector.tensor_scalar(retrs, mv[:, 1, :], EPS, None, ALU.add))
                    chain.wait()
                    nc.vector.reciprocal(retrs, retrs).then_inc(rs_var, 1)
                    dve.wait_ge(rs_sqrt, g + 1)
                    for t in range(TT):
                        yv = y_r[:, t, g * P:(g + 1) * P]
                        chain(nc.vector.scalar_tensor_tensor(yv, bank[:, t, :], mv[:, 0, t:t + 1], yv,
                                                             ALU.subtract, ALU.mult))
                    chain.wait()
                    for t in range(TT):
                        yv = y_r[:, t, g * P:(g + 1) * P]
                        nc.vector.tensor_scalar(yv, yv, retrs[:, t:t + 1], None, ALU.mult).then_inc(ro_out, 1)
                    dve.wait_ge(ro_out, 4 * (g + 1))
            for name in ("gs0", "gs1", "gr0", "gr1"):
                take(name, None)
            operand_lo(op_l, op_h, KT, KT, T)
            dve.wait_ge(tile_out["act"], GATED)
            for n in range(2):
                def gate_sb(t, n=n):
                    v = m_sb[:, 4 * n + t, :]
                    return nc.vector.tensor_tensor(v, ps[:, t, :], v, ALU.mult)
                take(f"so{n}", gate_sb)

                def gate_ret(t, n=n):
                    v = m_ret[:, 4 * n + t, :]
                    chain(nc.vector.tensor_tensor(v, ps[:, t, :], v, ALU.mult))
                    chain.wait()
                    return nc.vector.tensor_tensor(m_sb[:, 4 * n + t, :], m_sb[:, 4 * n + t, :], v, ALU.add)
                take(f"ro{n}", gate_ret)
            for k in range(KT):
                dve.wait_ge(op_hi, 2 * KT + k + 1)
                nc.vector.tensor_tensor(op_l[:, k, :], m_sb[:, k, :], op_h[:, k, :], ALU.subtract).then_inc(op_lo, 1)
            norm_scale(mem_nat, mem_nat, MT, msum, mrstd, 6, 2)
            operand_lo(opm_l, opm_h, 3 * KT, KT, M, gmem_c)
            dve.wait_ge(in_res, 16)
            for n in range(2):
                def add_res(t, n=n):
                    v = res[:, t, n * 512:(n + 1) * 512]
                    return nc.vector.tensor_tensor(v, ps[:, t, :], v, ALU.add)
                take(f"mo{n}", add_res)
            norm_scale(res, xs2, TT, ss, rstd, 10, 3)
            for name in ("mk0", "mk1", "mv0", "mv1"):
                take(name, None)
            operand_lo(op_l, op_h, 4 * KT, KT, T, gxat_c)
            take("cq0", None)
            take("cq1", None)
            for u in range(XH * TT + 2):
                if u < XH * TT:
                    dve.wait_ge(xs_done, u + 1)
                    if u >= 4:
                        dve.wait_ge(xs_exp, u - 3)
                    nc.vector.tensor_reduce(xmax[:, u % 4:u % 4 + 1], ps[:, u % 4, 0:M], AX.X, ALU.max,
                                            negate=True).then_inc(xs_max, 1)
                if 1 <= u <= XH * TT:
                    v = u - 1
                    dve.wait_ge(xs_exp, v + 1)
                    chain(nc.vector.reciprocal(xrec[:, v % 4:v % 4 + 1], xsum[:, v % 4:v % 4 + 1]))
                    chain.wait()
                    nc.vector.tensor_scalar(prob[:, v % 4, :], prob[:, v % 4, :], xrec[:, v % 4:v % 4 + 1], None,
                                            ALU.mult).then_inc(xs_prob, 1)
                if u >= 2:
                    v = u - 2
                    hd, t = v // TT, v % TT
                    dve.wait_ge(xt_done, v + 1)
                    if hd >= 2 and t == 0:
                        dve.wait_ge(xo_done, 2 * (hd - 1))
                    dst = prob_t[:, hd % 2, :].rearrange("p (m n) -> p m n", m=MT)[:, :, t * P:(t + 1) * P]
                    nc.vector.tensor_copy(dst, ps[:, 4 + v % 2, 0:M].rearrange("p (m n) -> p m n", m=MT)).then_inc(xt_out, 1)
                    if t == 2 and hd >= 1:
                        cross_lo(dve, hd - 1)
            cross_lo(dve, XH - 1)
            for n in range(2):
                def add_res(t, n=n):
                    v = res[:, t, n * 512:(n + 1) * 512]
                    return nc.vector.tensor_tensor(v, ps[:, t, :], v, ALU.add)
                take(f"co{n}", add_res)
            dve.wait_ge(n_sq, 14)
            chain(nc.vector.tensor_scalar(rstd, ss, 1.0 / D, EPS, ALU.mult, ALU.add))
            chain.wait()
            nc.vector.reciprocal(rstd, rstd).then_inc(n_inv, 1)
            dve.wait_ge(n_sqrt, 4)
            dve.wait_ge(in_moe, 64)
            for t in range(TT):
                nc.vector.scalar_tensor_tensor(h_nat[:, t, :], res[:, t, :], rstd[:, t:t + 1], g_moe_b,
                                               ALU.mult, ALU.mult).then_inc(nat_ready, 1)
            dve.wait_ge(b_hi, 1)
            nc.vector.tensor_tensor(bias[32:64, :], bias_f[32:64, :], bias[32:64, :].bitcast(F32), ALU.subtract).then_inc(b_lo, 1)
            for t in range(TT):
                dve.wait_ge(nat_hi, t + 1)
                nc.vector.tensor_tensor(hn_l[:, t, :], h_nat[:, t, :], hn_h[:, t, :], ALU.subtract).then_inc(nat_lo, 1)
            for t in range(TT):
                dve.wait_ge(lg_done, t + 1)
                chain(nc.vector.tensor_tensor(logit[:, t, :], ps[:, t, 0:NE], names["brt"], ALU.add))
            chain.wait()
            for t in range(TT):
                chain(nc.vector.max(top[:, t, :], logit[:, t, :]))
            chain.wait()
            nc.vector.tensor_scalar(names["nmax"].rearrange("p (t o) -> p t o", o=1), top[:, :, 0:1], -1.0, None,
                                    ALU.mult).then_inc(route_done, 1)
            for t in range(TT):
                chain(nc.vector.max_index(topi[:, t, :], top[:, t, :], logit[:, t, :]))
            chain.wait()
            chain(nc.vector.tensor_copy(idxf, topi[:, :, 0:TOPK]))
            chain.wait()
            iota_b = iota[:, 0:NE].unsqueeze(1).unsqueeze(1).to_broadcast([P, TT, TOPK, NE])
            chain(nc.vector.tensor_tensor(oh, iota_b, idxf.unsqueeze(3).to_broadcast([P, TT, TOPK, NE]), ALU.is_equal))
            chain.wait()
            nc.vector.tensor_reduce(sel, oh.rearrange("p t k e -> p t e k"), AX.X, ALU.add).then_inc(rank_in, 1)
            dve.wait_ge(gate_exp, 4)
            chain(nc.vector.reciprocal(names["grec"], names["gsum"]))
            chain.wait()
            chain(nc.vector.tensor_tensor(gate, gate, names["grec"].unsqueeze(2).to_broadcast([P, TT, TOPK]), ALU.mult))
            dve.wait_ge(rank_done, 1)
            chain(nc.vector.tensor_copy(rank, ps[:, 2, 0:TT * NE].rearrange("p (t e) -> p t e", t=TT)))
            chain(nc.vector.tensor_copy(names["cnt"], ps[:, 3, 0:NE]))
            chain.wait()
            chain(nc.vector.tensor_tensor(oh2, oh, rank.unsqueeze(2).to_broadcast([P, TT, TOPK, NE]), ALU.mult))
            chain(nc.vector.scalar_tensor_tensor(slot, rank, 1.0, sel, ALU.add, ALU.mult))
            chain.wait()
            rk = names["rk"]
            chain(nc.vector.tensor_reduce(rk.rearrange("p (t k) -> p t k", t=TT), oh2, AX.X, ALU.add))
            for j in range(4):
                chain(nc.vector.tensor_scalar(slots[:, :, j * NE:(j + 1) * NE], slot, -1.0 - P * j, None, ALU.add))
            chain.wait()
            jj, jm, rowf, g16, g2 = names["jj"], names["jm"], names["rowf"], names["gate"], names["gate2"]
            chain(nc.vector.tensor_scalar(jj, rk, float(P), None, ALU.is_ge))
            chain(nc.vector.tensor_scalar(jm, rk, float(P), None, ALU.is_lt))
            chain(nc.vector.tensor_scalar(rowf, rk, float(P - 1), None, ALU.min))
            chain.wait()
            chain(nc.vector.tensor_tensor(g2, g16, jj, ALU.mult))
            chain(nc.vector.scalar_tensor_tensor(rowf, names["idxf"], float(P), rowf, ALU.mult, ALU.add))
            chain.wait()
            chain(nc.vector.tensor_copy(rowi, rowf))
            chain(nc.vector.tensor_tensor(g16, g16, jm, ALU.mult))
            chain.wait()
            chain(nc.vector.scalar_tensor_tensor(rowf, names["idxf"], float(P), rk, ALU.mult, ALU.add))
            for j in (2, 3):
                chain(nc.vector.scalar_tensor_tensor(jj, rk, float(P * j), jj, ALU.is_ge, ALU.add))
                chain.wait()
            chain(nc.vector.scalar_tensor_tensor(rowf, jj, float(NE * P - P), rowf, ALU.mult, ALU.add))
            chain.wait()
            chain(nc.vector.tensor_scalar(rowf, rowf, float(-NE * P), 0.0, ALU.add, ALU.max))
            chain.wait()
            nc.vector.tensor_copy(rowj, rowf).then_inc(route_done, 1)
            cnt = names["cnt"]
            for j in range(3):
                chain(nc.vector.tensor_scalar(ov_ex[:, j * NE:(j + 1) * NE], cnt[0:1, :], float(P * (j + 1)), None, ALU.is_gt))
            chain.wait()
            chain(nc.vector.tensor_tensor_scan(ov_pos, ov_ex, ov_ex, 0.0, ALU.add, ALU.bypass))
            chain(nc.vector.tensor_tensor(ov_c, iota[0:1, 0:96], ov_ex, ALU.mult))
            chain.wait()
            chain(nc.vector.tensor_scalar(ov_tab, iota[0:1, 0:16], 1.0, None, ALU.add))
            chain.wait()
            chain(nc.vector.tensor_tensor(ov_eq, ov_pos.unsqueeze(1).to_broadcast([1, 16, 96]),
                                          ov_tab.unsqueeze(2).to_broadcast([1, 16, 96]), ALU.is_equal))
            chain.wait()
            chain(nc.vector.tensor_tensor(ov_eq, ov_eq, ov_c.unsqueeze(1).to_broadcast([1, 16, 96]), ALU.mult))
            chain.wait()
            chain(nc.vector.tensor_reduce(ov_tab, ov_eq, AX.X, ALU.add))
            chain.wait()
            chain(nc.vector.tensor_copy(table, ov_tab))
            chain.wait()
            nc.vector.tensor_copy(n_over, ov_pos[:, 95:96]).then_inc(route_done, 1)

            def esplit(i, c):
                cc = c % EC
                dve.wait_ge(w_hi, i * EC + (DENSE + c + 1))
                s = (DENSE + c) % SPL
                nc.vector.tensor_tensor(wl[:, s, :], raw[:, cc % RAW, :], wh[:, s, :], ALU.subtract).then_inc(w_lo, 1)

            def expert(i, last=False, alone=False):
                if alone:
                    esplit(i, 0)
                    esplit(i, 1)
                for step in range(EC):
                    if step == 10:
                        act_lo(i, 1)
                    if step + AHEAD < EC or not (last or alone):
                        esplit(i, step + AHEAD)
                    half = step // 4 % 2
                    if step in (2, 6):
                        dve.wait_ge(w_used, i * EC + (DENSE + step))
                        nc.vector.tensor_scalar(glu[:, half, :], ps[:, 2 * half, :], LIMIT, None,
                                                ALU.min).then_inc(glu_step, 1)
                    if step in (4, 8):
                        half = step // 4 - 1
                        k = i * 8 + 4 * half
                        dve.wait_ge(w_used, i * EC + (DENSE + step))
                        nc.vector.tensor_scalar(lin[:, half, :], ps[:, 2 * half + 1, :], -LIMIT, LIMIT,
                                                ALU.max, ALU.min).then_inc(glu_step, 1)
                        dve.wait_ge(glu_step, k + 2)
                        nc.vector.scalar_tensor_tensor(act_o[:, half, :], lin[:, half, :], 1.0, glu[:, half, :],
                                                       ALU.add, ALU.mult).then_inc(glu_step, 1)
                        dve.wait_ge(glu_step, k + 3)
                        dve.wait_ge(sig_done, i * 2 + (half + 1))
                        nc.vector.tensor_tensor(act_o[:, half, :], act_o[:, half, :], sig[:, half, :],
                                                ALU.mult).then_inc(glu_step, 1)
                    if step == 6:
                        act_lo(i, 0)

            def act_lo(i, half):
                dve.wait_ge(a_hi, i * 2 + (half + 1))
                nc.vector.tensor_tensor(a_l[:, 4 * half:4 * half + 4, :], ps[:, 6 + half, :].rearrange("p (a n) -> p a n", a=4),
                                        a_h[:, 4 * half:4 * half + 4, :], ALU.subtract).then_inc(a_lo, 1)

            with dve.Fori(0, NE - 1) as i:
                expert(i)
            expert(NE - 1, last=True)
            n = dve.value_load(n_over, min_val=0, max_val=OVER)
            with dve.If(n > 0):
                with dve.Fori(0, OVER) as j:
                    with dve.If(j < n):
                        expert(j + NE, alone=True)
                for u in range(TT * TOPK):
                    dve.wait_ge(over_in[u % 4], 16 * (u // 4 + 1))
                    if u:
                        dve.wait_ge(over_used, u)
                    nc.vector.scalar_tensor_tensor(res[:, u // TOPK, :], y_rows[:, u % 4, :], g2[:, u:u + 1],
                                                   res[:, u // TOPK, :], ALU.mult, ALU.add).then_inc(over_used, 1)
                dve.wait_ge(over_used, TT * TOPK)
            for t in range(TT):
                for k in range(TOPK):
                    u = TOPK * t + k
                    dve.wait_ge(row_in[u % 4], 16 * (u // 4 + 1))
                    if k:
                        dve.wait_ge(row_used, u)
                    nc.vector.scalar_tensor_tensor(res[:, t, :], y_rows[:, u % 4, :], gate[:, t, k:k + 1], res[:, t, :],
                                                   ALU.mult, ALU.add).then_inc(row_used, 1)
                dve.wait_ge(n_sq, 15 + t)
                chain(nc.vector.tensor_scalar(rstd[:, t:t + 1], ss[:, t:t + 1], 1.0 / D, EPS, ALU.mult, ALU.add))
                chain.wait()
                nc.vector.reciprocal(rstd[:, t:t + 1], rstd[:, t:t + 1]).then_inc(n_inv, 1)
                dve.wait_ge(n_sqrt, 5 + t)
                dve.wait_ge(in_gfin, 16)
                if t >= 2:
                    dve.wait_ge(stored[t % 2], 16 * (t // 2))
                nc.vector.scalar_tensor_tensor(o_sb[:, t % 2, :], res[:, t, :], rstd[:, t:t + 1], g_fin_b,
                                               ALU.mult, ALU.mult).then_inc(f_out, 1)

        @block.tensor
        def _(pe):
            def three(o, a_hi_, a_lo_, b_hi_, b_lo_, start, stop):
                nc.tensor.matmul(o, a_hi_, b_hi_, start=start, stop=False)
                nc.tensor.matmul(o, a_hi_, b_lo_, start=False, stop=False)
                return nc.tensor.matmul(o, a_lo_, b_hi_, start=False, stop=stop)

            def project(name, oh_, ol_, ready=None):
                s = slabs[name]
                for c in range(s.chunks):
                    g = s.chunk0 + c
                    pe.wait_ge(w_lo, g + 1)
                    w_h, w_l = (v[:, g % SPL, :].rearrange("p (a n) -> p a n", a=4) for v in (wh, wl))
                    for t in range(s.tiles):
                        if c == 0 and s.bank_free[t]:
                            owner, count = s.bank_free[t]
                            pe.wait_ge(tile_out[owner], count)
                        for a in range(4):
                            k = 4 * c + a
                            if ready and t == 0:
                                pe.wait_ge(ready[0], ready[1] + k + 1)
                            first, last = k == 0, k == 4 * s.chunks - 1
                            o = ps[:, t, 0:s.cols]
                            cut = slice(t * P, (t + 1) * P)
                            if s.kind == "T":
                                ins = three(o, w_h[:, a, cut], w_l[:, a, cut], oh_[:, k, :], ol_[:, k, :], first, last)
                            else:
                                ins = three(o, oh_[:, k, cut], ol_[:, k, cut], w_h[:, a, :], w_l[:, a, :], first, last)
                        if t == s.tiles - 1:
                            ins.then_inc(w_used, 1)
                        elif c == s.chunks - 1:
                            ins.then_inc(tile_done, 1)

            def transposes(src, tiles, n0):
                for k in range(KT):
                    if n0 + k >= 4:
                        pe.wait_ge(op_lo, n0 + k - 3)
                    for t in range(tiles):
                        ins = nc.tensor.transpose(ps[:, 4 + k % 4, t * P:(t + 1) * P], src[:, t, k * P:(k + 1) * P], ident)
                    ins.then_inc(tr_done, 1)

            pe.wait_ge(in_mats, 16)
            pe.wait_ge(n_xs, TT)
            transposes(x_nat, TT, 0)
            project("sbq", op_h, op_l, (op_lo, 0))
            project("sbk", op_h, op_l)
            project("sbv", op_h, op_l)
            units = [(h, kb) for h in range(HEADS) for kb in (3, 2, 1, 0)]
            pe.wait_ge(tile_out["act"], 12)
            for step in range(len(units) + 5):
                if step < len(units):
                    h, kb = units[step]
                    n = T - P * kb
                    r = 64 * (h % 2)
                    if step >= 6:
                        pe.wait_ge(wexp_done, step - 5)
                    nc.tensor.matmul(ps[:, step % 6, 0:n], k_sb[r:r + 64, h // 2, kb * P:(kb + 1) * P],
                                     q_sb[r:r + 64, h // 2, kb * P:T], start=True, stop=True).then_inc(z_done, 1)
                if 3 <= step < len(units) + 3:
                    u = step - 3
                    h, kb = units[u]
                    pe.wait_ge(soft_done, u + 1)
                    for b in range(3, kb - 1, -1):
                        n = T - P * b
                        ins = nc.tensor.matmul(ps[:, u % 6, P * (b - kb):P * (b - kb) + n], neg_from if b == kb else neg_ones,
                                               soft[:, h % 2, OFF[b]:OFF[b] + n], start=False, stop=True,
                                               skip_group_check=True)
                    ins.then_inc(zc_done, 1)
                if step >= 8 and step % 4 == 0:
                    head_out(pe, step // 4 - 2)
            pe.wait_ge(wexp_done, len(units))
            project("rq", op_h, op_l)
            project("rk", op_h, op_l)
            pe.wait_ge(tile_out["act"], 20)
            for u in range(8):
                if u >= 4:
                    pe.wait_ge(rot_out, u - 3)
                elif u == 0:
                    pe.wait_ge(o_lo, HEADS)
                nc.tensor.matmul(ps[:, 4 + u % 4, :], rot_swap, (q_r, k_r)[u // 4][:, u % 4, :], start=True,
                                 stop=True).then_inc(rot_done, 1)
            for name in ("rv0", "rv1", "rg0", "rg1"):
                project(name, op_h, op_l)
            pe.wait_ge(tile_out["act"], 36)
            pe.wait_ge(rot_out, 8)
            for h in range(HEADS + 1):
                if h < HEADS:
                    r = 64 * (h % 2)
                    for kb in range(4):
                        n = T - P * kb
                        if h >= 1:
                            pe.wait_ge(sc_out, 4 * (h - 1) + kb + 1)
                        nc.tensor.matmul(ps[:, 4 + kb, 0:n], k_r[r:r + 64, h // 2, kb * P:(kb + 1) * P],
                                         q_r[r:r + 64, h // 2, kb * P:T], start=True, stop=True).then_inc(sc_done, 1)
                if h >= 1:
                    g = h - 1
                    pe.wait_ge(sc_out, 4 * (g + 1))
                    if g >= 2:
                        pe.wait_ge(ro_out, 4 * (g - 1))
                    for t in range(TT):
                        for kb in range(t + 1):
                            a = OFFA[kb] + (t - kb) * P
                            ins = nc.tensor.matmul(ps[:, g % 2, t * P:(t + 1) * P], scores[:, g % 2, a:a + P],
                                                   v_r[:, kb, g * P:(g + 1) * P], start=(kb == 0), stop=(kb == t))
                    ins.then_inc(ro_done, 1)
            pe.wait_ge(ro_out, 4 * HEADS)
            for name in ("gs0", "gs1", "gr0", "gr1"):
                project(name, op_h, op_l)
            transposes(y_r, TT, KT)
            project("so0", op2_h, op2_l)
            project("ro0", op_h, op_l, (op_lo, KT))
            project("so1", op2_h, op2_l)
            project("ro1", op_h, op_l)
            pe.wait_ge(n_xs, TT + MT)
            transposes(mem_nat, MT, 3 * KT)
            project("mo0", op_h, op_l, (op_lo, 2 * KT))
            project("mo1", op_h, op_l)
            project("mk0", opm_h, opm_l, (op_lo, 3 * KT))
            for name in ("mk1", "mv0", "mv1"):
                project(name, opm_h, opm_l)
            pe.wait_ge(n_xs, 2 * TT + MT)
            transposes(xs2, TT, 4 * KT)
            project("cq0", op_h, op_l, (op_lo, 4 * KT))
            project("cq1", op_h, op_l)
            pe.wait_ge(tile_out["act"], outs_total["act"])
            for u in range(XH * TT + 5):
                if u < XH * TT:
                    hd, t = u // TT, u % TT
                    if u >= 4:
                        pe.wait_ge(xs_exp, u - 3)
                    for dt in range(2):
                        ins = nc.tensor.matmul(ps[:, u % 4, 0:M], q_x[:, 2 * hd + dt, t * P:(t + 1) * P],
                                               k_x[:, 2 * hd + dt, :], start=(dt == 0), stop=(dt == 1))
                    ins.then_inc(xs_done, 1)
                if 2 <= u < XH * TT + 2:
                    v = u - 2
                    pe.wait_ge(xs_prob, v + 1)
                    if v >= 2:
                        pe.wait_ge(xt_out, v - 1)
                    for m in range(MT):
                        ins = nc.tensor.transpose(ps[:, 4 + v % 2, m * P:(m + 1) * P], prob[:, v % 4, m * P:(m + 1) * P], ident)
                    ins.then_inc(xt_done, 1)
                if u >= 8 and u % TT == 0:
                    cross_out(pe, u // TT - 2)
            project("co0", op_h, op_l, (op_lo, 5 * KT))
            project("co1", op_h, op_l)
            pe.wait_ge(tile_out["dve"], outs_total["dve"])
            pe.wait_ge(in_moe, 64)
            pe.wait_ge(n_sqrt, 4)
            for t in range(TT + 1):
                if t < TT:
                    pe.wait_ge(nat_ready, t + 1)
                    if t >= 2:
                        pe.wait_ge(ht_out, t - 1)
                    for k in range(KT):
                        ins = nc.tensor.transpose(ps[:, 4 + 2 * (t % 2) + k // 4, (k % 4) * P:(k % 4 + 1) * P],
                                                  h_nat[:, t, k * P:(k + 1) * P], ident)
                    ins.then_inc(ht_done, 1)
                if t >= 1:
                    v = t - 1
                    pe.wait_ge(ht_out, v + 1)
                    for k in range(KT):
                        ins = nc.tensor.matmul(ps[:, v, 0:NE], h_t[:, v % 2, k * P:(k + 1) * P], w_rt[:, k, :],
                                               start=(k == 0), stop=(k == KT - 1))
                    ins.then_inc(lg_done, 1)
            pe.wait_ge(rank_in, 1)
            for t in range(TT):
                for b in range(t + 1):
                    nc.tensor.matmul(ps[:, 2, t * NE:(t + 1) * NE], before if b == t else ones, sel[:, b, :],
                                     start=(b == 0), stop=(b == t))
            for b in range(TT):
                ins = nc.tensor.matmul(ps[:, 3, 0:NE], ones, sel[:, b, :], start=(b == 0), stop=(b == TT - 1))
            ins.then_inc(rank_done, 1)

            def gather(i, u):
                src = (hn_h, hn_l)[u // 2]
                for a in range(4):
                    k = 4 * (u % 2) + a
                    for t in range(TT):
                        ins = nc.tensor.matmul(ps[:, 6 + u % 2, a * P:(a + 1) * P], src[:, t, k * P:(k + 1) * P], pick[:, t, :],
                                               start=(t == 0), stop=(t == TT - 1))
                ins.then_inc(gath, 1)

            def gather_alone(i):
                pe.wait_ge(pick_ready, i * TT + TT)
                for u in range(4):
                    if u >= 2:
                        pe.wait_ge(x_out, i * 4 + (u - 1))
                    gather(i, u)

            def expert(i, following=False, first=False):
                for q in range(4):
                    bank = ps[:, q, :]
                    col = (q % 2) * DFF + (q // 2) * 512
                    if q == 0:
                        pe.wait_ge(bsel_ready, i + 1)
                    nc.tensor.matmul(bank, bsel[:, :], bias[:, col:col + 512], start=True, stop=False)
                    for half in range(2):
                        c = 2 * q + half
                        pe.wait_ge(w_lo, i * EC + (DENSE + c + 1))
                        if q == 0:
                            pe.wait_ge(x_out, i * 4 + 3 + half)
                        s = (DENSE + c) % SPL
                        for a in range(4):
                            k = 4 * half + a
                            ins = three(bank, x_h[:, k, :], x_l[:, k, :], wh[:, s, a * 512:(a + 1) * 512],
                                        wl[:, s, a * 512:(a + 1) * 512], False, half == 1 and a == 3)
                        ins.then_inc(w_used, 1)
                    if q == 2:
                        turn(i, 0)
                for n in range(2):
                    if n == 0 and not first:
                        pe.wait_ge(y_evac, i * 2)
                    ins = nc.tensor.matmul(ps[:, 4 + n, :], bsel[:, :], bias[:, 2 * D + n * 512:2 * D + (n + 1) * 512],
                                           start=True, stop=False)
                ins.then_inc(bsel_used, 1)
                for q in range(4):
                    c = 8 + q
                    pe.wait_ge(w_lo, i * EC + (DENSE + c + 1))
                    if q % 2 == 0:
                        pe.wait_ge(a_lo, i * 2 + (q // 2 + 1))
                    s = (DENSE + c) % SPL
                    for a in range(2):
                        f = 2 * q + a
                        for n in range(2):
                            cut = slice(a * D + n * 512, a * D + (n + 1) * 512)
                            ins = three(ps[:, 4 + n, :], a_h[:, f, :], a_l[:, f, :], wh[:, s, cut], wl[:, s, cut],
                                        False, f == 7)
                    ins.then_inc(w_used, 1)
                    if q == 1:
                        turn(i, 1)
                    if following and q == 1:
                        pe.wait_ge(pick_ready, i * TT + 2 * TT)
                        gather(i + 1, 0)
                    if following and q == 2:
                        gather(i + 1, 1)
                        pe.wait_ge(x_out, i * 4 + 5)
                        gather(i + 1, 2)
                    if following and q == 3:
                        pe.wait_ge(x_out, i * 4 + 6)
                        gather(i + 1, 3)

            def turn(i, half):
                pe.wait_ge(glu_step, i * 8 + (4 * half + 4))
                for a in range(4):
                    ins = nc.tensor.transpose(ps[:, 6 + half, a * P:(a + 1) * P], act_o[:, half, a * P:(a + 1) * P], ident)
                ins.then_inc(at_done, 1)

            pe.wait_ge(nat_lo, TT)
            pe.wait_ge(b_lo, 1)
            pe.wait_ge(route_done, 3)
            gather_alone(0)
            expert(0, following=True, first=True)
            with pe.Fori(1, NE - 1) as i:
                expert(i, following=True)
            expert(NE - 1)
            n = pe.value_load(n_over, min_val=0, max_val=OVER)
            with pe.If(n > 0):
                with pe.Fori(0, OVER) as j:
                    with pe.If(j < n):
                        gather_alone(j + NE)
                        expert(j + NE)

OFF = {3: 0, 2: 128, 1: 384, 0: 768}
OFFA = {0: 0, 1: 512, 2: 896, 3: 1152}
TR_RET = 2 * KT
_S, _N, _O = lay_slabs()
MERGED = _S["ro1"].out0 + 4
MIXED = _S["mo1"].out0 + 4
GATED = _S["gr1"].out0 + 4

_INS = ["x", "mem", "g_mix", "w_in", "w_sb_o", "w_ret_o", "w_mix_out", "g_xattn", "g_mem", "w_cq", "w_ckv", "w_co",
        "g_moe", "w_router", "b_router", "w_exp_in", "b_exp_in", "w_exp_out", "b_exp_out", "g_final"]


def kernel(**inputs):
    import concourse.bacc as _bacc
    from concourse.bass_utils import run_bass_kernel_spmd as _run

    nc = _bacc.Bacc("TRN2", target_bir_lowering=False, num_devices=1)
    arrays, args = {}, []
    given = {name: np.ascontiguousarray(inputs[name]) for name in _INS}
    given.update(constant_tables())
    for name, a in given.items():
        arrays[f"in_{name}"] = a
        args.append(nc.dram_tensor(f"in_{name}", a.shape, mybir.dt.from_np(a.dtype), kind="ExternalInput").ap())
    args.append(nc.dram_tensor("out_rows", (1, T, D), F32, kind="ExternalOutput").ap())
    layer_kernel(nc, *args)
    r = _run(nc, [arrays], core_ids=[0])
    return r.results[0]["out_rows"]
```

```python
from contextlib import ExitStack

import numpy as np

import concourse.bass as bass
from concourse import mybir

ALU = mybir.AluOpType
ACT = mybir.ActivationFunctionType
F32 = mybir.dt.float32
F32R = mybir.dt.float32r
BF16 = mybir.dt.bfloat16
U32 = mybir.dt.uint32
AX = mybir.AxisListType

P = 128
T = 512
TT = T // P
D = 1024
KT = D // P
M = 256
MT = M // P
HEADS = 8
XH = 4
XD = D // XH
NE = 32
TOPK = 4
DFF = 1024
EPS = 1e-5
LIMIT = 7.0
ALPHA = 1.702
BC = 3 * D // 2
NC = 4 * NE
OVER = T * TOPK // P - 1
RAW = 4
RAWE = 6
CH = 2048
PC = CH // 2
SPL = 6
AHEAD = 5
EC = 12
EP = 2 * EC
POOL = (9, 14, 18, 20, 22)

SLABS = [("sbq", "T", 2, 4, T, "act"), ("sbk", "T", 2, 4, T, "act"), ("sbv", "N", 2, 4, 512, "act"),
         ("rq", "T", 2, 4, T, "act"), ("rk", "T", 2, 4, T, "act"),
         ("rv0", "N", 2, 4, 512, "act"), ("rv1", "N", 2, 4, 512, "act"),
         ("rg0", "N", 2, 4, 512, "act"), ("rg1", "N", 2, 4, 512, "act"),
         ("gs0", "T", 2, 4, T, "act"), ("gs1", "T", 2, 4, T, "act"),
         ("gr0", "T", 2, 4, T, "act"), ("gr1", "T", 2, 4, T, "act"),
         ("so0", "T", 1, 4, T, "dve"), ("ro0", "T", 2, 4, T, "dve"),
         ("so1", "T", 1, 4, T, "dve"), ("ro1", "T", 2, 4, T, "dve"),
         ("mo0", "N", 2, 4, 512, "dve"), ("mo1", "N", 2, 4, 512, "dve"),
         ("mk0", "T", 2, 4, M, "act"), ("mk1", "T", 2, 4, M, "act"),
         ("mv0", "N", 2, 2, 512, "act"), ("mv1", "N", 2, 2, 512, "act"),
         ("cq0", "T", 2, 4, T, "act"), ("cq1", "T", 2, 4, T, "act"),
         ("co0", "N", 2, 4, 512, "dve"), ("co1", "N", 2, 4, 512, "dve")]


class Slab:

    def __init__(self, spec, chunk0, tile0, prev):
        self.name, self.kind, self.chunks, self.tiles, self.cols, self.owner = spec
        self.chunk0 = chunk0
        self.tile0 = tile0
        self.out0 = prev.get(self.owner, 0)


def lay_slabs():
    slabs, chunk, tile, outs = {}, 0, 0, {"act": 0, "dve": 0}
    last_user = [None] * 4
    for spec in SLABS:
        s = Slab(spec, chunk, tile, outs)
        s.bank_free = [last_user[t] for t in range(s.tiles)]
        for t in range(s.tiles):
            last_user[t] = (s.owner, outs[s.owner] + t + 1)
        chunk += s.chunks
        tile += s.tiles - 1
        outs[s.owner] += s.tiles
        slabs[s.name] = s
    return slabs, chunk, outs


LOG_DECAY = np.log1p(-np.exp2(-5.0 - np.arange(HEADS)))


def constant_tables():
    i = np.arange(P)
    mats = np.zeros((8, P, P), np.float32)
    mats[0] = np.eye(P)
    mats[1] = -1.0 * (i[:, None] >= i[None, :])
    mats[2] = -1.0
    for m in range(P):
        d = m % 64
        mats[3, m + 32 if d < 32 else m - 32, m] = -1.0 if d < 32 else 1.0
    mats[4] = i[:, None] < i[None, :]
    mats[5] = 1.0
    mats[6] = i[None, :]
    mats[7] = (i[:, None] % NE) == (i[None, :] % NE)
    inv = np.float32(10000.0) ** (-np.arange(0, 64, 2, dtype=np.float32) / np.float32(64))
    ang = (np.arange(T, dtype=np.float32)[None, :] * inv[:, None]).astype(np.float32)
    rot = np.stack([np.tile(np.cos(ang), (4, 1)), np.tile(np.sin(ang), (4, 1))]).astype(np.float32)
    u = np.arange(2 * P)[None, :] - i[:, None]
    dec = np.where(u >= 0, np.exp(LOG_DECAY[:, None, None] * np.maximum(u, 0)), 0.0) / 8.0
    return {"c_mats": mats, "c_rot": rot, "c_dec": dec.astype(np.float32)}


def layer_kernel(nc, x, mem, g_mix, w_in, w_sb_o, w_ret_o, w_mix_out, g_xattn, g_mem, w_cq, w_ckv, w_co,
                 g_moe, w_router, b_router, w_exp_in, b_exp_in, w_exp_out, b_exp_out, g_final,
                 c_mats, c_rot, c_dec, out):
    slabs, DENSE, outs_total = lay_slabs()
    assert DENSE % RAW == 0 and EC % RAWE == 0 and EP % SPL == 0
    DP = 2 * DENSE
    y_main = nc.dram_tensor("y_main", [NE * P, D], F32, kind="Internal").ap()
    y_over = nc.dram_tensor("y_over", [(NC - NE) * P, D], F32, kind="Internal").ap()

    with ExitStack() as ctx:
        def sb(name, shape, dt=F32):
            return ctx.enter_context(nc.sbuf_tensor(name, shape, dt))

        def sem(name):
            return ctx.enter_context(nc.semaphore(name))

        raw = sb("raw", [P, RAW, CH])
        wh = sb("wh", [P, SPL, PC], F32R)
        wl = sb("wl", [P, SPL, PC], F32R)
        oph = sb("oph", [P, KT * T], F32R)
        opl = sb("opl", [P, KT * T], F32R)
        op2 = sb("op2", [P, 4096], F32R)
        acts = sb("acts", [P, 3072], F32R)
        bsel = sb("bsel", [P, P], F32R)
        bias = sb("bias", [P, BC], F32R)
        ident = sb("ident", [P, P])[:, :]
        small = sb("small", [P, 92])
        work = sb("work", [P, 15360])
        ps = ctx.enter_context(nc.psum_tensor("ps", [P, 8, 512], F32))

        gmix_c, gxat_c, gmem_c = (small[:, 8 * n:8 * n + 8] for n in range(3))
        ss, rstd = small[:, 24:28], small[:, 28:32]
        msum, mrstd = small[:, 32:34], small[:, 34:36]
        retstat = small[:, 36:60]
        retmv = small[:, 60:68]
        retrs = small[:, 68:72]
        xmax = small[:, 72:76]
        xsum = small[:, 76:80]
        xrec = small[:, 80:84]
        cur = small[:, 84:92].rearrange("p (t o) -> p t o", t=TT)

        def w_(a, n):
            return work[:, a:a + n]

        def view(a, tiles, n):
            return w_(a, tiles * n).rearrange("p (t n) -> p t n", t=tiles)

        neg_from, neg_ones, rot_swap = (w_(14976 + P * n, P) for n in range(3))
        x_nat = view(0, TT, D)
        q_sb, k_sb, v_sb = view(0, 4, T), view(2048, 4, T), view(4096, TT, 512)
        abs_z = view(6144, 3, 512)
        soft = view(7680, 2, 1280)
        wts = view(10240, 2, 1280)
        q_r, k_r, v_r = view(0, 4, T), view(2048, 4, T), view(4096, TT, D)
        y_r = view(8192, TT, D)
        cosine, sine = w_(12288, T), w_(12800, T)
        rot_tmp = view(13312, 2, T)
        decay = view(12288, 2, 2 * P)
        scores = view(12800, 2, 1280)
        m_sb, m_ret = view(0, KT, T), view(4096, KT, T)
        res = view(8192, TT, D)
        xs2 = view(0, TT, D)
        q_x, k_x, v_x = view(0, KT, T), view(4096, KT, M), view(6144, MT, D)
        mem_nat = view(12288, MT, D)
        prob = view(12288, 4, M)
        prob_t = view(13312, 2, MT * T)
        h_nat = view(0, TT, D)
        bias_f = w_(4096, BC)
        h_t = view(4096, 4, T)
        g_moe_b = w_(7168, D)
        mats2 = view(12288, 4, P)
        before, ones, iota, exp_rows = (mats2[:, n, :] for n in range(4))
        logit = view(12800, TT, NE)
        before_b, ones_b = (w_(15104 + 64 * n, 64).bitcast(BF16) for n in range(2))
        sel_b = w_(15232, 64).bitcast(BF16).rearrange("p (t e) -> p t e", t=TT)
        g_moe_c = small[:, 0:8]
        logit_t = work[0:NE, 6656:7168]
        square = view(0, 8, 512)
        ss_more = xmax
        at = 12928
        names = {}
        for name, n in (("top", 32), ("topi", 32), ("idxf", 16), ("gate", 16), ("gsum", 4), ("grec", 4), ("nmax", 4),
                        ("rk", 16), ("jj", 16), ("jm", 16), ("rowf", 16), ("rowi", 16), ("rowj", 16), ("gate2", 16), ("oh", 512), ("sel", 128),
                        ("rank", 128), ("slot", 128), ("cnt", 32), ("slots", 512), ("brt", 32), ("tabi", 16), ("nov", 1)):
            names[name] = w_(at, n)
            at += n
        assert at <= 15360
        w_rt = view(6144, KT, NE)
        top = names["top"].rearrange("p (t n) -> p t n", t=TT)
        topi = names["topi"].bitcast(U32).rearrange("p (t n) -> p t n", t=TT)
        idxf = names["idxf"].rearrange("p (t n) -> p t n", t=TT)
        gate = names["gate"].rearrange("p (t n) -> p t n", t=TT)
        rowi, rowj = names["rowi"].bitcast(U32), names["rowj"].bitcast(U32)
        oh = names["oh"].rearrange("p (t k e) -> p t k e", t=TT, k=TOPK)
        oh2 = w_(6656, 512).rearrange("p (t k e) -> p t k e", t=TT, k=TOPK)
        sel = names["sel"].rearrange("p (t e) -> p t e", t=TT)
        rank = names["rank"].rearrange("p (t e) -> p t e", t=TT)
        slot = names["slot"].rearrange("p (t e) -> p t e", t=TT)
        slots = names["slots"].rearrange("p (t c) -> p t c", t=TT)
        table = names["tabi"][0:1, :].bitcast(U32)
        n_over = names["nov"][0:1, :].bitcast(U32)
        ov_ex, ov_pos, ov_c = (work[0:1, 4096 + 96 * n:4096 + 96 * n + 96] for n in range(3))
        ov_eq = work[0:1, 4608:4608 + 16 * 96].rearrange("p (i c) -> p i c", i=16)
        ov_tab = work[0:1, 6400:6416]
        x_h = op2[:, 0:2048].rearrange("p (t b n) -> p t b n", t=KT, b=2)
        x_l = op2[:, 2048:4096].rearrange("p (t b n) -> p t b n", t=KT, b=2)
        glu, sig, lin = (w_(512 * n, 512) for n in range(3))
        pick = acts[:, 0:1024].rearrange("p (t b n) -> p t b n", t=TT, b=2)
        a_h, a_l = (acts[:, 1024 * n:1024 * n + 1024].rearrange("p (h t n) -> p h t n", h=2, t=4) for n in (1, 2))
        y_sb = w_(3072, D)
        raw_more = view(4096, 2, CH)

        def wait_lo(eng, i, p):
            mine = sum(q <= p % EP for q in POOL)
            b = p // EP
            if p % EP in POOL:
                eng.wait_ge(w_lo_pool, i * len(POOL) + (b * len(POOL) + mine))
            else:
                eng.wait_ge(w_lo, i * (EP - len(POOL)) + (b * (EP - len(POOL)) + DP + p % EP + 1 - mine))

        def raw_e(c):
            return raw[:, c % RAWE, :] if c % RAWE < RAW else raw_more[:, c % RAWE - RAW, :]

        y_rows = view(0, 4, D)
        g_fin_b = w_(5120, D)
        o_sb = view(6144, 2, D)

        op_h = oph[:, :].rearrange("p (t n) -> p t n", t=KT)
        op_l = opl[:, :].rearrange("p (t n) -> p t n", t=KT)
        op2_h = op2[:, 0:2048].rearrange("p (t n) -> p t n", t=4)
        op2_l = op2[:, 2048:4096].rearrange("p (t n) -> p t n", t=4)
        opm_h = op2[:, 0:2048].rearrange("p (t n) -> p t n", t=KT)
        opm_l = op2[:, 2048:4096].rearrange("p (t n) -> p t n", t=KT)
        hn_h = oph[:, :].rearrange("p (t n) -> p t n", t=TT)
        hn_l = opl[:, :].rearrange("p (t n) -> p t n", t=TT)

        w_landed = [sem(f"w_landed{n}") for n in range(RAWE)]
        w_hi, w_lo, w_lo_pool, w_used = sem("w_hi"), sem("w_lo"), sem("w_lo_pool"), sem("w_used")
        in_x, in_mats, in_cols, in_rot, in_mem, in_res = (
            sem(n) for n in ("in_x", "in_mats", "in_cols", "in_rot", "in_mem", "in_res"))
        in_dec = [sem("in_dec0"), sem("in_dec1")]
        in_moe, in_bias, in_gfin = sem("in_moe"), sem("in_bias"), sem("in_gfin")
        act_chain, dve_chain = sem("act_chain"), sem("dve_chain")
        tile_done = sem("tile_done")
        tile_out = {"act": sem("tile_out_act"), "dve": sem("tile_out_dve")}
        tr_done, op_hi, op_lo = sem("tr_done"), sem("op_hi"), sem("op_lo")
        z_done, soft_raw, soft_done, zc_done, wexp_done, wts_done, o_done, o_hi, o_lo = (
            sem(n) for n in ("z_done", "soft_raw", "soft_done", "zc_done", "wexp_done", "wts_done", "o_done", "o_hi", "o_lo"))
        ln_done = sem("ln_done")
        rot_done, rot_out = sem("rot_done"), sem("rot_out")
        sc_done, sc_out, ro_done, ro_out = (sem(n) for n in ("sc_done", "sc_out", "ro_done", "ro_out"))
        rs_var, rs_sqrt = sem("rs_var"), sem("rs_sqrt")
        n_sq, n_inv, n_sqrt, n_xs = (sem(n) for n in ("n_sq", "n_inv", "n_sqrt", "n_xs"))
        xs_done, xs_max, xs_exp, xs_prob, xt_done, xt_out, xo_done = (
            sem(n) for n in ("xs_done", "xs_max", "xs_exp", "xs_prob", "xt_done", "xt_out", "xo_done"))
        ht_done, ht_out, lg_half, lgt_done, lgt_out, lg_done, gate_exp, rank_in, rank_done, route_done = (
            sem(n) for n in ("ht_done", "ht_out", "lg_half", "lgt_done", "lgt_out", "lg_done", "gate_exp", "rank_in",
                             "rank_done", "route_done"))
        in_rt, rt_ready, pick0_ready = sem("in_rt"), sem("rt_ready"), sem("pick0_ready")
        nat_ready, nat_hi, nat_lo, b_hi, b_lo = (sem(n) for n in ("nat_ready", "nat_hi", "nat_lo", "b_hi", "b_lo"))
        cur_ready, pick_ready, bsel_ready, bsel_used = (sem(n) for n in ("cur_ready", "pick_ready", "bsel_ready", "bsel_used"))
        gath, x_out, glu_step, sig_done, gs_done, at_done, a_hi, a_lo = (
            sem(n) for n in ("gath", "x_out", "glu_step", "sig_done", "gs_done", "at_done", "a_hi", "a_lo"))
        y_evac, y_stored = sem("y_evac"), sem("y_stored")
        pool_turn, sp_turn = sem("pool_turn"), sem("sp_turn")
        zero_ready, over_stored, over_used = (sem(n) for n in ("zero_ready", "over_stored", "over_used"))
        row_in = [sem(f"row_in{n}") for n in range(4)]
        over_in = [sem(f"over_in{n}") for n in range(4)]
        row_used, f_out = sem("row_used"), sem("f_out")
        stored = [sem("stored0"), sem("stored1")]

        def dense_source(g):
            for s in slabs.values():
                if s.chunk0 <= g < s.chunk0 + s.chunks:
                    break
            half, name = g - s.chunk0, s.name
            order = list(slabs)
            if order.index(name) < 13:
                src, col = w_in[0], order.index(name)
            else:
                src = {"so": w_sb_o, "ro": w_ret_o, "mo": w_mix_out, "mk": w_ckv, "mv": w_ckv,
                       "cq": w_cq, "co": w_co}[name[:2]][0]
                col = int(name[2]) + (2 if name[:2] == "mv" else 0)
            return src[half * 512:(half + 1) * 512, col * 512:(col + 1) * 512].rearrange("(a p) n -> p a n", p=P)

        def expert_sources(e):
            w1 = w_exp_in[0, bass.ds(e, 1), :, :].rearrange("o (a p) n -> p (o a) n", p=P)
            w2 = w_exp_out[0, bass.ds(e, 1), :, :].rearrange("o (a p) n -> p (o a) n", p=P)
            for half in range(2):
                for gl in range(2):
                    col = gl * DFF + half * 512
                    for a in (0, 4):
                        yield w1[:, a:a + 4, col:col + 512], "p (a n) -> p a n", 4
            for q in range(4):
                yield w2[:, 2 * q:2 * q + 2, :], "p (a n) -> p a n", 2

        class Chain:

            def __init__(self, eng, s):
                self.eng, self.s, self.n = eng, s, 0

            def __call__(self, ins):
                ins.then_inc(self.s, 1)
                self.n += 1

            def wait(self):
                self.eng.wait_ge(self.s, self.n)

        def head_out_act(act, h):
            act.wait_ge(o_done, h + 1)
            r = 64 * (h % 2)
            nc.scalar.activation(op2_h[r:r + 64, h // 2, :], ps[r:r + 64, 6 + h % 2, :], ACT.Copy).then_inc(o_hi, 1)

        def cross_hi(act, hd):
            for dt in range(2):
                act.wait_ge(xo_done, 2 * hd + dt + 1)
                nc.scalar.activation(op_h[:, 2 * hd + dt, :], ps[:, 6 + dt, :], ACT.Copy).then_inc(op_hi, 1)

        def head_out_dve(dve, h):
            dve.wait_ge(o_hi, h + 1)
            r = 64 * (h % 2)
            nc.vector.tensor_tensor(op2_l[r:r + 64, h // 2, :], ps[r:r + 64, 6 + h % 2, :], op2_h[r:r + 64, h // 2, :],
                                    ALU.subtract).then_inc(o_lo, 1)

        def cross_lo(dve, hd):
            for dt in range(2):
                k = 2 * hd + dt
                dve.wait_ge(op_hi, 5 * KT + k + 1)
                nc.vector.tensor_tensor(op_l[:, k, :], ps[:, 6 + dt, :], op_h[:, k, :], ALU.subtract).then_inc(op_lo, 1)

        def head_out(pe, h):
            pe.wait_ge(wts_done, 4 * h + 4)
            if h >= 2:
                pe.wait_ge(o_lo, h - 1)
            for kb in range(4):
                n = T - P * kb
                ins = nc.tensor.matmul(ps[:, 6 + h % 2, kb * P:T], v_sb[:, kb, (h // 2) * P:(h // 2 + 1) * P],
                                       wts[:, h % 2, OFF[kb]:OFF[kb] + n], start=(kb == 0), stop=(kb == 3),
                                       skip_group_check=True)
            ins.then_inc(o_done, 1)

        def cross_out(pe, hd):
            pe.wait_ge(xt_out, TT * (hd + 1))
            for dt in range(2):
                if hd >= 1:
                    pe.wait_ge(op_lo, 5 * KT + 2 * (hd - 1) + dt + 1)
                for m in range(MT):
                    a = hd * XD + dt * P
                    ins = nc.tensor.matmul(ps[:, 6 + dt, :], v_x[:, m, a:a + P],
                                           prob_t[:, hd % 2, m * T:(m + 1) * T], start=(m == 0), stop=(m == MT - 1))
                ins.then_inc(xo_done, 1)

        block = ctx.enter_context(nc.Block())

        @block.sync
        def _(sp):
            sp.dma_start(x_nat, x[0].rearrange("(t p) d -> p t d", p=P)).then_inc(in_x, 16)
            for g in range(DENSE):
                if g >= RAW:
                    sp.wait_ge(w_lo, 2 * (g - RAW + 1))
                sp.dma_start(raw[:, g % RAW, :].rearrange("p (a n) -> p a n", a=4),
                             dense_source(g)).then_inc(w_landed[g % RAW], 16)

            def load_expert(i, e, first=False):
                for c, (src, pat, a) in enumerate(expert_sources(e)):
                    if not first or c >= RAWE:
                        p = 2 * (c - RAWE)
                        if p % EP in POOL or (p + 1) % EP in POOL:
                            wait_lo(sp, i, p)
                            sp.sem_inc(sp_turn, 1)
                        wait_lo(sp, i, p + 1)
                    elif c < RAW:
                        sp.wait_ge(w_lo, DP + 2 * (c - RAW + 1))
                    elif c == RAW:
                        sp.wait_ge(route_done, 3)
                    sp.dma_start(raw_e(c).rearrange(pat, a=a), src).then_inc(w_landed[c % RAWE], 16)

            load_expert(0, 0, first=True)
            with sp.Fori(1, NE) as i:
                load_expert(i, i)
            n = sp.value_load(n_over, min_val=0, max_val=OVER)
            with sp.If(n > 0):
                with sp.Fori(0, OVER) as j:
                    with sp.If(j < n):
                        c = sp.value_load(table[0:1, bass.ds(j, 1)], min_val=0, max_val=NC - NE - 1)
                        load_expert(j + NE, c % NE)
            for tt in range(TT):
                sp.wait_ge(f_out, tt + 1)
                sp.dma_start(out[0, tt * P:(tt + 1) * P, :], o_sb[:, tt % 2, :]).then_inc(stored[tt % 2], 16)
            sp.wait_ge(stored[0], 32)
            sp.wait_ge(stored[1], 32)

        @block.gpsimd
        def _(pool):
            pool.dma_start(ident, c_mats[0]).then_inc(in_mats, 16)
            pool.dma_start(w_(14976, 3 * P).rearrange("p (c n) -> p c n", c=3),
                           c_mats[1:4].rearrange("c p n -> p c n")).then_inc(in_mats, 16)
            for dst, src in ((gmix_c, g_mix), (gxat_c, g_xattn), (gmem_c, g_mem)):
                with nc.allow_non_contiguous_dma(reason="a gain for each channel"):
                    pool.dma_start(dst, src[0].rearrange("(k p) -> p k", p=P)).then_inc(in_cols, 16)

            def keep_before(view_):
                return nc.gpsimd.affine_select(out=view_, in_=view_, pattern=[[1, P]], compare_op=ALU.is_gt, fill=0.0,
                                               base=0, channel_multiplier=-1)

            units = [(h, kb) for h in range(HEADS) for kb in (3, 2, 1, 0)]
            for step in range(len(units) + 3):
                if step < len(units):
                    h, kb = units[step]
                    pool.wait_ge(soft_raw, step + 1)
                    keep_before(soft[:, h % 2, OFF[kb]:OFF[kb] + P]).then_inc(soft_done, 1)
                if step >= 3:
                    h, kb = units[step - 3]
                    pool.wait_ge(wexp_done, step - 3 + 1)
                    keep_before(wts[:, h % 2, OFF[kb]:OFF[kb] + P]).then_inc(wts_done, 1)
            pool.wait_ge(o_done, HEADS)
            pool.dma_start(w_(12288, 2 * T).rearrange("p (c n) -> p c n", c=2),
                           c_rot.rearrange("c p n -> p c n")).then_inc(in_rot, 16)
            for h in range(HEADS):
                if h == 0:
                    pool.wait_ge(rot_out, 8)
                if h >= 2:
                    pool.wait_ge(sc_out, 4 * (h - 1))
                pool.dma_start(decay[:, h % 2, :], c_dec[h]).then_inc(in_dec[h % 2], 16)
            pool.wait_ge(tr_done, TR_RET)
            pool.dma_start(res, x[0].rearrange("(t p) d -> p t d", p=P)).then_inc(in_res, 16)
            pool.dma_start(mem_nat, mem[0].rearrange("(t p) d -> p t d", p=P)).then_inc(in_mem, 16)
            pool.wait_ge(xo_done, 2 * XH)
            pool.dma_start(mats2, c_mats[4:8].rearrange("c p n -> p c n")).then_inc(in_moe, 16)
            pool.dma_start(names["brt"], b_router[0].partition_broadcast(P)).then_inc(in_moe, 16)
            pool.dma_start(w_rt, w_router[0].rearrange("(k p) e -> p k e", p=P)).then_inc(in_rt, 16)
            with nc.allow_non_contiguous_dma(reason="a gain for each channel"):
                pool.dma_start(g_moe_c, g_moe[0].rearrange("(k p) -> p k", p=P)).then_inc(in_rt, 16)
            pool.dma_start(g_moe_b, g_moe[0].partition_broadcast(P)).then_inc(in_moe, 16)
            for r in range(2):
                rows, more = slice(NE * r, NE * r + NE), slice(64 + NE * r, 64 + NE * r + NE)
                pool.dma_start(bias_f[rows, :], b_exp_in[0, :, 0:BC]).then_inc(in_bias, 16)
                pool.dma_start(bias_f[more, 0:2 * D - BC], b_exp_in[0, :, BC:2 * D]).then_inc(in_bias, 16)
                pool.dma_start(bias_f[more, 2 * D - BC:BC], b_exp_out[0]).then_inc(in_bias, 16)

            pool.wait_ge(in_rt, 32)
            nc.gpsimd.tensor_tensor(w_rt, w_rt, g_moe_c.unsqueeze(2).to_broadcast([P, KT, NE]), ALU.mult).then_inc(rt_ready, 1)
            pool.wait_ge(in_moe, 48)
            nc.gpsimd.tensor_copy(before_b, before).then_inc(rt_ready, 1)
            nc.gpsimd.tensor_copy(ones_b, ones).then_inc(rt_ready, 1)

            def choose_rows(m, c=None):
                pool.wait_ge(gath, m * 8)
                if c is None:
                    nc.gpsimd.tensor_copy(cur, slots[:, :, bass.ds(m * 2, 2)]).then_inc(cur_ready, 1)
                else:
                    nc.gpsimd.tensor_copy(cur, slots[:, :, bass.ds(c, 1)].to_broadcast([P, TT, 2])).then_inc(cur_ready, 1)
                pool.wait_ge(cur_ready, m)
                pool.sem_inc(pool_turn, 1)
                for t in range(TT):
                    for b in range(2):
                        nc.gpsimd.tensor_scalar(pick[:, t, b, :], iota, cur[:, t, b:b + 1], None,
                                                ALU.is_equal).then_inc(pick_ready, 1)

            def choose_bias(i, c, first=False):
                if not first:
                    pool.wait_ge(bsel_used, i)
                nc.gpsimd.tensor_copy(bsel[:, :], exp_rows[:, bass.ds(c, 1)].to_broadcast([P, P])).then_inc(bsel_ready, 1)

            choose_bias(0, 0, first=True)
            pool.wait_ge(route_done, 3)

            def gate_sigmoid(i, half):
                pool.wait_ge(sig_done, i * 2 + (half + 1))
                nc.gpsimd.tensor_tensor(sig, glu, sig, ALU.mult).then_inc(gs_done, 1)

            def split(i, p):
                pool.wait_ge(w_hi, i * EP + (DP + p + 1))
                s = (DP + p) % SPL
                nc.gpsimd.tensor_tensor(wl[:, s, :], raw_e(p // 2)[:, p % 2 * PC:(p % 2 + 1) * PC], wh[:, s, :],
                                        ALU.subtract).then_inc(w_lo_pool, 1)

            def block_work(i):
                split(i, POOL[0])
                gate_sigmoid(i, 0)
                split(i, POOL[1])
                gate_sigmoid(i, 1)
                for p in POOL[2:]:
                    split(i, p)

            def pair(m, last=False):
                i = m * 2
                block_work(i)
                choose_bias(i + 1, i + 1)
                if not last:
                    choose_rows(m + 1)
                block_work(i + 1)
                if not last:
                    choose_bias(i + 2, i + 2)

            pair(0)
            with pool.Fori(1, NE // 2 - 1) as m:
                pair(m)
            pair(NE // 2 - 1, last=True)
            n = pool.value_load(n_over, min_val=0, max_val=OVER)
            with pool.If(n > 0):
                pool.wait_ge(y_stored, NE * 16)
                nc.gpsimd.memset(y_sb, 0.0).then_inc(zero_ready, 1)
                with pool.Fori(0, OVER) as j:
                    with pool.If(j < n):
                        c = pool.value_load(table[0:1, bass.ds(j, 1)], min_val=0, max_val=NC - NE - 1)
                        choose_rows(j + NE // 2, c=c + NE)
                        choose_bias(j + NE, c % NE)
                        block_work(j + NE)
                pool.wait_ge(over_stored, n * 16 + 16)
                pool.sem_inc(pool_turn, 1)
                for u in range(TT * TOPK):
                    if u >= 4:
                        pool.wait_ge(over_used, u - 3)
                    pool.indirect_dma_start(out=y_rows[:, u % 4, :], out_offset=None, in_=y_over,
                                            in_offset=bass.IndirectOffsetOnAxis(ap=rowj[:, u:u + 1], axis=0)
                                            ).then_inc(over_in[u % 4], 16)
                pool.wait_ge(over_used, TT * TOPK)
            pool.wait_ge(y_stored, NE * 16)
            pool.dma_start(g_fin_b, g_final.partition_broadcast(P)).then_inc(in_gfin, 16)
            for u in range(TT * TOPK):
                if u >= 4:
                    pool.wait_ge(row_used, u - 3)
                pool.indirect_dma_start(out=y_rows[:, u % 4, :], out_offset=None, in_=y_main,
                                        in_offset=bass.IndirectOffsetOnAxis(ap=rowi[:, u:u + 1], axis=0)
                                        ).then_inc(row_in[u % 4], 16)

        @block.scalar
        def _(act):
            chain = Chain(act, act_chain)

            def split(g):
                slot = g % SPL
                c = g // 2
                if g % 2 == 0:
                    act.wait_ge(w_landed[c % RAW], 16 * (c // RAW + 1))
                if g >= SPL:
                    act.wait_ge(w_used, g - SPL + 1)
                nc.scalar.activation(wh[:, slot, :], raw[:, c % RAW, g % 2 * PC:(g % 2 + 1) * PC], ACT.Copy).then_inc(w_hi, 1)

            def take(name, f, meanwhile={}):
                s = slabs[name]
                for c in range(2 * s.chunks):
                    split(2 * s.chunk0 + c + AHEAD)
                    if c in meanwhile:
                        meanwhile[c]()
                if s.owner != "act":
                    return
                for t in range(s.tiles):
                    if t < s.tiles - 1:
                        act.wait_ge(tile_done, s.tile0 + t + 1)
                    else:
                        act.wait_ge(w_used, 2 * (s.chunk0 + s.chunks))
                    f(t).then_inc(tile_out["act"], 1)

            def norm_stats(xv, tiles, acc, rs, sq0, inv_n):
                for t in range(tiles):
                    if t:
                        act.wait_ge(n_sq, sq0 + t)
                    nc.scalar.activation(ps[:, 6:8, :].rearrange("p a n -> p (a n)"), xv[:, t, :], ACT.Square,
                                         accum_out=acc[:, t:t + 1]).then_inc(n_sq, 1)
                act.wait_ge(n_inv, inv_n)
                nc.scalar.activation(rs, rs, ACT.Sqrt).then_inc(n_sqrt, 1)

            def operand_hi(dst, n0, tiles, cols, gain=None, first_tr=0):
                for k in range(tiles):
                    act.wait_ge(tr_done, first_tr + k + 1)
                    src = ps[:, 4 + k % 4, 0:cols]
                    nc.scalar.activation(dst[:, k, :], src, ACT.Copy,
                                         scale=1.0 if gain is None else gain[:, k:k + 1]).then_inc(op_hi, 1)

            act.wait_ge(in_x, 16)
            norm_stats(x_nat, TT, ss, rstd, 0, 1)
            for g in range(AHEAD):
                split(g)
            act.wait_ge(in_cols, 48)
            operand_hi(op_h, 0, KT, T, gmix_c, 0)

            def copy(dst, scale=1.0):
                def f(t):
                    return nc.scalar.activation(dst[:, t, :], ps[:, t, 0:dst.shape[2]], ACT.Copy, scale=scale)
                return f

            take("sbq", copy(q_sb, 64 ** -0.5))
            take("sbk", copy(k_sb))
            take("sbv", copy(v_sb))
            act.preload_act_table_set("natural_log_exp_and_others")
            units = [(h, kb) for h in range(HEADS) for kb in (3, 2, 1, 0)]
            for step in range(len(units) + 3):
                if step < len(units):
                    h, kb = units[step]
                    n = T - P * kb
                    z = abs_z[:, step % 3, 0:n]
                    act.wait_ge(z_done, step + 1)
                    if step >= 3:
                        act.wait_ge(soft_raw, step - 2)
                    chain(nc.scalar.activation(z, ps[:, step % 6, 0:n], ACT.Abs))
                    chain.wait()
                    chain(nc.scalar.activation(z, z, ACT.Exp, scale=-1.0))
                    chain.wait()
                    nc.scalar.activation(z, z, ACT.Ln, bias=1.0).then_inc(ln_done, 1)
                if step >= 3:
                    u = step - 3
                    h, kb = units[u]
                    n = T - P * kb
                    act.wait_ge(zc_done, u + 1)
                    if h >= 2 and kb == 3:
                        act.wait_ge(o_done, h - 1)
                    nc.scalar.activation(wts[:, h % 2, OFF[kb]:OFF[kb] + n], ps[:, u % 6, 0:n],
                                         ACT.Exp).then_inc(wexp_done, 1)
                if step >= 7 and (step - 7) % 4 == 0:
                    head_out_act(act, (step - 7) // 4)
            head_out_act(act, HEADS - 1)
            take("rq", copy(q_r))
            take("rk", copy(k_r))
            for n in range(2):
                def into(t, n=n):
                    return nc.scalar.activation(v_r[:, t, n * 512:(n + 1) * 512], ps[:, t, :], ACT.Copy)
                take(f"rv{n}", into)
            for n in range(2):
                def into(t, n=n):
                    return nc.scalar.activation(y_r[:, t, n * 512:(n + 1) * 512], ps[:, t, :], ACT.Silu)
                take(f"rg{n}", into)
            for h in range(HEADS):
                act.wait_ge(rs_var, h + 1)
                nc.scalar.activation(retrs, retrs, ACT.Sqrt).then_inc(rs_sqrt, 1)
            for n in range(2):
                def into(t, n=n):
                    return nc.scalar.activation(m_sb[:, 4 * n + t, :], ps[:, t, :], ACT.Sigmoid)
                take(f"gs{n}", into)
            for n in range(2):
                def into(t, n=n):
                    return nc.scalar.activation(m_ret[:, 4 * n + t, :], ps[:, t, :], ACT.Sigmoid)
                take(f"gr{n}", into)
            operand_hi(op_h, 8, KT, T, None, KT)
            for name in ("so0", "ro0", "so1", "ro1"):
                take(name, None)
            act.wait_ge(tile_out["dve"], MERGED)
            act.wait_ge(w_used, 2 * slabs["ro1"].chunk0 + 4)
            for k in range(KT):
                nc.scalar.activation(op_h[:, k, :], m_sb[:, k, :], ACT.Copy).then_inc(op_hi, 1)
            act.wait_ge(in_mem, 16)
            norm_stats(mem_nat, MT, msum, mrstd, 4, 2)
            operand_hi(opm_h, 24, KT, M, gmem_c, 2 * KT)
            take("mo0", None)
            take("mo1", None)
            act.wait_ge(tile_out["dve"], MIXED)
            norm_stats(res, TT, ss, rstd, 6, 3)
            for n in range(2):
                def into(t, n=n):
                    return nc.scalar.activation(k_x[:, 4 * n + t, :], ps[:, t, 0:M], ACT.Copy)
                take(f"mk{n}", into)
            for n in range(2):
                def into(t, n=n):
                    return nc.scalar.activation(v_x[:, t, n * 512:(n + 1) * 512], ps[:, t, :], ACT.Copy)
                take(f"mv{n}", into)
            operand_hi(op_h, 32, KT, T, gxat_c, 3 * KT)
            for n in range(2):
                def into(t, n=n):
                    return nc.scalar.activation(q_x[:, 4 * n + t, :], ps[:, t, :], ACT.Copy, scale=XD ** -0.5)
                take(f"cq{n}", into)
            for u in range(XH * TT):
                act.wait_ge(xs_max, u + 1)
                nc.scalar.activation(prob[:, u % 4, :], ps[:, u % 4, 0:M], ACT.Exp, bias=xmax[:, u % 4:u % 4 + 1],
                                     accum_out=xsum[:, u % 4:u % 4 + 1]).then_inc(xs_exp, 1)
                if u % TT == 3 and u > TT:
                    cross_hi(act, u // TT - 1)
            cross_hi(act, XH - 1)
            take("co0", None)
            act.wait_ge(in_bias, 96)
            nc.scalar.activation(bias[:, :], bias_f, ACT.Copy).then_inc(b_hi, 1)
            act.preload_act_table_set("sqrt_and_others")

            def squares(half):
                acc = (ss, ss_more)[half]
                for t in range(TT):
                    act.wait_ge(tile_out["dve"], slabs[f"co{half}"].out0 + t + 1)
                    nc.scalar.activation(square[:, 4 * half + t, :], res[:, t, half * 512:(half + 1) * 512], ACT.Square,
                                         accum_out=acc[:, t:t + 1]).then_inc(n_sq, 1)

            def router_tile(k):
                act.wait_ge(ht_done, k + 1)
                if k == 4:
                    act.wait_ge(lg_half, 1)
                nc.scalar.activation(h_t[:, k % 4, :], ps[:, ROUTER_BANK[k], :], ACT.Copy).then_inc(ht_out, 1)

            def first_tiles():
                act.wait_ge(b_lo, 2)
                for k in range(4):
                    router_tile(k)

            take("co1", None, {1: lambda: squares(0), 2: first_tiles})
            squares(1)
            act.wait_ge(n_inv, 4)
            nc.scalar.activation(rstd, rstd, ACT.Sqrt).then_inc(n_sqrt, 1)
            act.preload_act_table_set("natural_log_exp_and_others")

            def row_hi(t):
                act.wait_ge(nat_ready, t + 1)
                nc.scalar.activation(hn_h[:, t, :], h_nat[:, t, :], ACT.Copy).then_inc(nat_hi, 1)

            router_tile(4)
            router_tile(5)
            row_hi(0)
            router_tile(6)
            router_tile(7)
            row_hi(1)
            act.wait_ge(lgt_done, 1)
            nc.scalar.activation(logit_t, ps[0:NE, 4, :], ACT.Copy).then_inc(lgt_out, 1)
            row_hi(2)
            row_hi(3)
            act.wait_ge(route_done, 1)
            for t in range(TT):
                ins = nc.scalar.activation(gate[:, t, :], top[:, t, 0:TOPK], ACT.Exp, bias=names["nmax"][:, t:t + 1],
                                           accum_out=names["gsum"][:, t:t + 1])
                ins.then_inc(gate_exp, 1)

            act.preload_act_table_set("sigmoid_and_others")

            def esplit(i, p):
                c = p // 2
                if p % 2 == 0:
                    landed = (EC // RAWE) * 16
                    before_ = (DENSE // RAW * 16 if c % RAWE < RAW else 0) + (c // RAWE + 1) * 16
                    act.wait_ge(w_landed[c % RAWE], i * landed + before_)
                act.wait_ge(w_used, i * EP + (DP + p - SPL + 1))
                nc.scalar.activation(wh[:, (DP + p) % SPL, :], raw_e(c)[:, p % 2 * PC:(p % 2 + 1) * PC], ACT.Copy).then_inc(w_hi, 1)

            def x_evac(m, u):
                act.wait_ge(gath, m * 8 + (u + 1))
                dst = (x_h, x_l)[u % 2][:, u - u % 2:u - u % 2 + 2, :, :].rearrange("p t b n -> p (t b n)")
                nc.scalar.activation(dst, ps[:, u % 4, :], ACT.Copy).then_inc(x_out, 1)

            def y_take(i):
                for n in range(2):
                    nc.scalar.activation(y_sb[:, n * 512:(n + 1) * 512], ps[:, 4 + n, :], ACT.Copy).then_inc(y_evac, 1)

            def y_store(i, c, dram, done):
                act.wait_ge(y_evac, i * 2 + 2)
                act.dma_start(dram.rearrange("(c p) d -> c p d", p=P)[bass.ds(c, 1), :, :].rearrange("o p d -> p (o d)"),
                              y_sb[:, :]).then_inc(done, 16)

            def expert(i, m, b=0, later=False, first=False, last=False, alone=False):
                if alone:
                    for p in range(AHEAD):
                        esplit(i, p)
                    for u in range(8):
                        x_evac(m, u)
                for p in range(EP):
                    if p + AHEAD < EP or not (last or alone):
                        esplit(i, p + AHEAD)
                    if p == 0 and not (first or alone):
                        if b == 0:
                            x_evac(m, 7)
                        act.wait_ge(w_used, i * EP + DP)
                        if later:
                            act.wait_ge(y_stored, i * 16 - 16)
                        y_take(i - 1)
                        y_store(i - 1, i - 1, y_main, y_stored)
                    if p == 5 or p == 13:
                        half = p // 8
                        act.wait_ge(glu_step, i * 6 + (3 * half + 1))
                        nc.scalar.activation(sig, glu, ACT.Sigmoid, scale=ALPHA).then_inc(sig_done, 1)
                    if p == 12:
                        act_hi(i, 0)
                    if p == 19:
                        act_hi(i, 1)
                    if p >= 17 and b == 1 and not last:
                        x_evac(m + 1, p - 17)

            def act_hi(i, half):
                act.wait_ge(at_done, i * 2 + (half + 1))
                nc.scalar.activation(a_h[:, half, :, :], ps[:, 6 + half, :].rearrange("p (a n) -> p a n", a=4),
                                     ACT.Copy).then_inc(a_hi, 1)

            for u in range(8):
                x_evac(0, u)
            expert(0, 0, first=True)
            expert(1, 0, b=1)
            with act.Fori(1, NE // 2 - 1) as m:
                expert(m * 2, m, later=True)
                expert(m * 2 + 1, m, b=1, later=True)
            expert(NE - 2, NE // 2 - 1, later=True)
            expert(NE - 1, NE // 2 - 1, b=1, later=True, last=True)
            act.wait_ge(w_used, NE * EP + DP)
            act.wait_ge(y_stored, NE * 16 - 16)
            y_take(NE - 1)
            y_store(NE - 1, NE - 1, y_main, y_stored)
            n = act.value_load(n_over, min_val=0, max_val=OVER)
            with act.If(n > 0):
                act.wait_ge(zero_ready, 1)
                act.dma_start(y_over.rearrange("(c p) d -> p c d", p=P),
                              y_sb.unsqueeze(1).to_broadcast([P, NC - NE, D])).then_inc(over_stored, 16)
                with act.Fori(0, OVER) as j:
                    with act.If(j < n):
                        c = act.value_load(table[0:1, bass.ds(j, 1)], min_val=0, max_val=NC - NE - 1)
                        expert(j + NE, j + NE // 2, alone=True)
                        act.wait_ge(w_used, j * EP + ((NE + 1) * EP + DP))
                        act.wait_ge(over_stored, j * 16 + 16)
                        y_take(j + NE)
                        y_store(j + NE, c, y_over, over_stored)
            act.preload_act_table_set("sqrt_and_others")
            for t in range(TT):
                act.wait_ge(row_used, 4 * t + 4)
                nc.scalar.activation(ps[:, 6:8, :].rearrange("p a n -> p (a n)"), res[:, t, :], ACT.Square,
                                     accum_out=ss[:, t:t + 1]).then_inc(n_sq, 1)
                act.wait_ge(n_inv, 5 + t)
                nc.scalar.activation(rstd[:, t:t + 1], rstd[:, t:t + 1], ACT.Sqrt).then_inc(n_sqrt, 1)

        @block.vector
        def _(dve):
            chain = Chain(dve, dve_chain)

            def split(g):
                dve.wait_ge(w_hi, g + 1)
                slot = g % SPL
                nc.vector.tensor_tensor(wl[:, slot, :], raw[:, g // 2 % RAW, g % 2 * PC:(g % 2 + 1) * PC], wh[:, slot, :], ALU.subtract).then_inc(w_lo, 1)

            def take(name, f):
                s = slabs[name]
                for c in range(2 * s.chunks):
                    split(2 * s.chunk0 + c + AHEAD)
                if s.owner != "dve":
                    return
                for t in range(s.tiles):
                    if t < s.tiles - 1:
                        dve.wait_ge(tile_done, s.tile0 + t + 1)
                    else:
                        dve.wait_ge(w_used, 2 * (s.chunk0 + s.chunks))
                    f(t).then_inc(tile_out["dve"], 1)

            def norm_scale(xv, dst, tiles, acc, rs, sq_n, inv_n):
                dve.wait_ge(n_sq, sq_n)
                chain(nc.vector.tensor_scalar(rs, acc, 1.0 / D, EPS, ALU.mult, ALU.add))
                chain.wait()
                nc.vector.reciprocal(rs, rs).then_inc(n_inv, 1)
                dve.wait_ge(n_sqrt, inv_n)
                for t in range(tiles):
                    nc.vector.tensor_scalar(dst[:, t, :], xv[:, t, :], rs[:, t:t + 1], None, ALU.mult).then_inc(n_xs, 1)

            def operand_lo(dst, hi, n0, tiles, cols, gain=None):
                for k in range(tiles):
                    dve.wait_ge(op_hi, n0 + k + 1)
                    src = ps[:, 4 + k % 4, 0:cols]
                    if gain is None:
                        ins = nc.vector.tensor_tensor(dst[:, k, :], src, hi[:, k, :], ALU.subtract)
                    else:
                        ins = nc.vector.scalar_tensor_tensor(dst[:, k, :], src, gain[:, k:k + 1], hi[:, k, :],
                                                             ALU.mult, ALU.subtract)
                    ins.then_inc(op_lo, 1)

            norm_scale(x_nat, x_nat, TT, ss, rstd, 4, 1)
            for g in range(AHEAD):
                split(g)
            operand_lo(op_l, op_h, 0, KT, T, gmix_c)
            for name in ("sbq", "sbk", "sbv"):
                take(name, None)
            units = [(h, kb) for h in range(HEADS) for kb in (3, 2, 1, 0)]
            for step in range(len(units) + 1):
                if step >= 1:
                    u = step - 1
                    h, kb = units[u]
                    n = T - P * kb
                    dve.wait_ge(ln_done, u + 1)
                    if h >= 2 and kb == 3:
                        dve.wait_ge(zc_done, 4 * (h - 1))
                    nc.vector.scalar_tensor_tensor(soft[:, h % 2, OFF[kb]:OFF[kb] + n], ps[:, u % 6, 0:n], 0.0,
                                                   abs_z[:, u % 3, 0:n], ALU.max, ALU.add).then_inc(soft_raw, 1)
                if step >= 8 and step % 4 == 0:
                    head_out_dve(dve, step // 4 - 2)
            head_out_dve(dve, HEADS - 1)
            take("rq", None)
            take("rk", None)
            dve.wait_ge(in_rot, 16)
            for u in range(8):
                v = (q_r, k_r)[u // 4][:, u % 4, :]
                dve.wait_ge(rot_done, u + 1)
                if u >= 2:
                    dve.wait_ge(rot_out, u - 1)
                chain(nc.vector.tensor_tensor(rot_tmp[:, u % 2, :], ps[:, 4 + u % 4, :], sine, ALU.mult))
                chain(nc.vector.tensor_tensor(v, v, cosine, ALU.mult))
                chain.wait()
                nc.vector.tensor_tensor(v, v, rot_tmp[:, u % 2, :], ALU.add).then_inc(rot_out, 1)
            for name in ("rv0", "rv1", "rg0", "rg1"):
                take(name, None)
            for h in range(HEADS + 1):
                if h < HEADS:
                    dve.wait_ge(in_dec[h % 2], 16 * (h // 2 + 1))
                    if h >= 2:
                        dve.wait_ge(ro_done, h - 1)
                    for kb in range(4):
                        n = T - P * kb
                        dve.wait_ge(sc_done, 4 * h + kb + 1)
                        near = min(n, 2 * P)
                        ins = nc.vector.tensor_tensor(scores[:, h % 2, OFFA[kb]:OFFA[kb] + near], ps[:, 4 + kb, 0:near],
                                                      decay[:, h % 2, 0:near], ALU.mult)
                        for b in range(2, n // P):
                            ins = nc.vector.scalar_tensor_tensor(
                                scores[:, h % 2, OFFA[kb] + b * P:OFFA[kb] + b * P + P], ps[:, 4 + kb, b * P:b * P + P],
                                float(np.exp(LOG_DECAY[h] * P * (b - 1))), decay[:, h % 2, P:2 * P], ALU.mult, ALU.mult)
                        ins.then_inc(sc_out, 1)
                if h >= 1:
                    g = h - 1
                    bank = ps[:, g % 2, :].rearrange("p (t n) -> p t n", t=TT)
                    dve.wait_ge(ro_done, g + 1)
                    for t in range(TT):
                        chain(nc.vector.bn_stats(retstat[:, 6 * t:6 * t + 6], bank[:, t, :]))
                    chain.wait()
                    for t in range(TT):
                        chain(nc.vector.bn_aggr(retmv[:, 2 * t:2 * t + 2], retstat[:, 6 * t:6 * t + 6]))
                    chain.wait()
                    mv = retmv.rearrange("p (t c) -> p c t", t=TT)
                    chain(nc.vector.tensor_scalar(retrs, mv[:, 1, :], EPS, None, ALU.add))
                    chain.wait()
                    nc.vector.reciprocal(retrs, retrs).then_inc(rs_var, 1)
                    dve.wait_ge(rs_sqrt, g + 1)
                    for t in range(TT):
                        yv = y_r[:, t, g * P:(g + 1) * P]
                        chain(nc.vector.scalar_tensor_tensor(yv, bank[:, t, :], mv[:, 0, t:t + 1], yv,
                                                             ALU.subtract, ALU.mult))
                    chain.wait()
                    for t in range(TT):
                        yv = y_r[:, t, g * P:(g + 1) * P]
                        nc.vector.tensor_scalar(yv, yv, retrs[:, t:t + 1], None, ALU.mult).then_inc(ro_out, 1)
                    dve.wait_ge(ro_out, 4 * (g + 1))
            for name in ("gs0", "gs1", "gr0", "gr1"):
                take(name, None)
            operand_lo(op_l, op_h, KT, KT, T)
            dve.wait_ge(tile_out["act"], GATED)
            for n in range(2):
                def gate_sb(t, n=n):
                    v = m_sb[:, 4 * n + t, :]
                    return nc.vector.tensor_tensor(v, ps[:, t, :], v, ALU.mult)
                take(f"so{n}", gate_sb)

                def gate_ret(t, n=n):
                    v = m_ret[:, 4 * n + t, :]
                    chain(nc.vector.tensor_tensor(v, ps[:, t, :], v, ALU.mult))
                    chain.wait()
                    return nc.vector.tensor_tensor(m_sb[:, 4 * n + t, :], m_sb[:, 4 * n + t, :], v, ALU.add)
                take(f"ro{n}", gate_ret)
            for k in range(KT):
                dve.wait_ge(op_hi, 2 * KT + k + 1)
                nc.vector.tensor_tensor(op_l[:, k, :], m_sb[:, k, :], op_h[:, k, :], ALU.subtract).then_inc(op_lo, 1)
            norm_scale(mem_nat, mem_nat, MT, msum, mrstd, 6, 2)
            operand_lo(opm_l, opm_h, 3 * KT, KT, M, gmem_c)
            dve.wait_ge(in_res, 16)
            for n in range(2):
                def add_res(t, n=n):
                    v = res[:, t, n * 512:(n + 1) * 512]
                    return nc.vector.tensor_tensor(v, ps[:, t, :], v, ALU.add)
                take(f"mo{n}", add_res)
            norm_scale(res, xs2, TT, ss, rstd, 10, 3)
            for name in ("mk0", "mk1", "mv0", "mv1"):
                take(name, None)
            operand_lo(op_l, op_h, 4 * KT, KT, T, gxat_c)
            take("cq0", None)
            take("cq1", None)
            for u in range(XH * TT + 2):
                if u < XH * TT:
                    dve.wait_ge(xs_done, u + 1)
                    if u >= 4:
                        dve.wait_ge(xs_exp, u - 3)
                    nc.vector.tensor_reduce(xmax[:, u % 4:u % 4 + 1], ps[:, u % 4, 0:M], AX.X, ALU.max,
                                            negate=True).then_inc(xs_max, 1)
                if 1 <= u <= XH * TT:
                    v = u - 1
                    dve.wait_ge(xs_exp, v + 1)
                    chain(nc.vector.reciprocal(xrec[:, v % 4:v % 4 + 1], xsum[:, v % 4:v % 4 + 1]))
                    chain.wait()
                    nc.vector.tensor_scalar(prob[:, v % 4, :], prob[:, v % 4, :], xrec[:, v % 4:v % 4 + 1], None,
                                            ALU.mult).then_inc(xs_prob, 1)
                if u >= 2:
                    v = u - 2
                    hd, t = v // TT, v % TT
                    dve.wait_ge(xt_done, v + 1)
                    if hd >= 2 and t == 0:
                        dve.wait_ge(xo_done, 2 * (hd - 1))
                    dst = prob_t[:, hd % 2, :].rearrange("p (m n) -> p m n", m=MT)[:, :, t * P:(t + 1) * P]
                    nc.vector.tensor_copy(dst, ps[:, 4 + v % 2, 0:M].rearrange("p (m n) -> p m n", m=MT)).then_inc(xt_out, 1)
                    if t == 2 and hd >= 1:
                        cross_lo(dve, hd - 1)
            cross_lo(dve, XH - 1)
            for n in range(2):
                def add_res(t, n=n):
                    v = res[:, t, n * 512:(n + 1) * 512]
                    return nc.vector.tensor_tensor(v, ps[:, t, :], v, ALU.add)
                take(f"co{n}", add_res)
                if n == 0:
                    dve.wait_ge(b_hi, 1)
                    for r in (NE, 64 + NE):
                        nc.vector.tensor_tensor(bias[r:r + NE, :], bias_f[r:r + NE, :], bias[r:r + NE, :].bitcast(F32),
                                                ALU.subtract).then_inc(b_lo, 1)
            dve.wait_ge(n_sq, 18)
            chain(nc.vector.tensor_tensor(ss, ss, ss_more, ALU.add))
            chain.wait()
            chain(nc.vector.tensor_scalar(rstd, ss, 1.0 / D, EPS, ALU.mult, ALU.add))
            chain.wait()
            nc.vector.reciprocal(rstd, rstd).then_inc(n_inv, 1)
            dve.wait_ge(n_sqrt, 4)
            dve.wait_ge(in_moe, 48)
            for t in range(TT):
                nc.vector.scalar_tensor_tensor(h_nat[:, t, :], res[:, t, :], rstd[:, t:t + 1], g_moe_b,
                                               ALU.mult, ALU.mult).then_inc(nat_ready, 1)

            def row_lo(t):
                dve.wait_ge(nat_hi, t + 1)
                nc.vector.tensor_tensor(hn_l[:, t, :], h_nat[:, t, :], hn_h[:, t, :], ALU.subtract).then_inc(nat_lo, 1)

            row_lo(0)
            row_lo(1)
            dve.wait_ge(lg_done, 1)
            for t in range(TT):
                chain(nc.vector.scalar_tensor_tensor(logit[:, t, :], ps[:, 1, t * NE:(t + 1) * NE], rstd[:, t:t + 1],
                                                     names["brt"], ALU.mult, ALU.add))
            chain.wait()
            for t in range(TT):
                chain(nc.vector.max(top[:, t, :], logit[:, t, :]))
            chain.wait()
            nc.vector.tensor_scalar(names["nmax"].rearrange("p (t o) -> p t o", o=1), top[:, :, 0:1], -1.0, None,
                                    ALU.mult).then_inc(route_done, 1)
            for t in range(TT):
                chain(nc.vector.max_index(topi[:, t, :], top[:, t, :], logit[:, t, :]))
            chain.wait()
            chain(nc.vector.tensor_copy(idxf, topi[:, :, 0:TOPK]))
            chain.wait()
            iota_b = iota[:, 0:NE].unsqueeze(1).unsqueeze(1).to_broadcast([P, TT, TOPK, NE])
            chain(nc.vector.tensor_tensor(oh, iota_b, idxf.unsqueeze(3).to_broadcast([P, TT, TOPK, NE]), ALU.is_equal))
            chain.wait()
            chain(nc.vector.tensor_reduce(sel, oh.rearrange("p t k e -> p t e k"), AX.X, ALU.add))
            chain.wait()
            dve.wait_ge(rt_ready, 3)
            nc.vector.tensor_copy(sel_b, sel).then_inc(rank_in, 1)
            row_lo(2)
            row_lo(3)
            dve.wait_ge(rank_done, 1)
            rank_ps = ps[:, 2, 0:TT * NE].rearrange("p (t e) -> p t e", t=TT)
            chain(nc.vector.scalar_tensor_tensor(slot, rank_ps, 1.0, sel, ALU.add, ALU.mult))
            chain(nc.vector.tensor_copy(rank, rank_ps))
            chain(nc.vector.tensor_copy(names["cnt"], ps[:, 3, 0:NE]))
            chain.wait()
            for j in range(4):
                chain(nc.vector.tensor_scalar(slots[:, :, j * NE:(j + 1) * NE], slot, -1.0 - P * j, None, ALU.add))
            chain.wait()
            for t in range(TT):
                for b in range(2):
                    nc.vector.tensor_scalar(pick[:, t, b, :], iota, slots[:, t, b:b + 1], None,
                                            ALU.is_equal).then_inc(pick0_ready, 1)
            chain(nc.vector.tensor_tensor(oh2, oh, rank.unsqueeze(2).to_broadcast([P, TT, TOPK, NE]), ALU.mult))
            chain.wait()
            rk = names["rk"]
            chain(nc.vector.tensor_reduce(rk.rearrange("p (t k) -> p t k", t=TT), oh2, AX.X, ALU.add))
            dve.wait_ge(gate_exp, 4)
            chain(nc.vector.reciprocal(names["grec"], names["gsum"]))
            chain.wait()
            chain(nc.vector.tensor_tensor(gate, gate, names["grec"].unsqueeze(2).to_broadcast([P, TT, TOPK]), ALU.mult))
            chain.wait()
            jj, jm, rowf, g16, g2 = names["jj"], names["jm"], names["rowf"], names["gate"], names["gate2"]
            chain(nc.vector.tensor_scalar(jj, rk, float(P), None, ALU.is_ge))
            chain(nc.vector.tensor_scalar(jm, rk, float(P), None, ALU.is_lt))
            chain(nc.vector.tensor_scalar(rowf, rk, float(P - 1), None, ALU.min))
            chain.wait()
            chain(nc.vector.tensor_tensor(g2, g16, jj, ALU.mult))
            chain(nc.vector.scalar_tensor_tensor(rowf, names["idxf"], float(P), rowf, ALU.mult, ALU.add))
            chain.wait()
            chain(nc.vector.tensor_copy(rowi, rowf))
            chain(nc.vector.tensor_tensor(g16, g16, jm, ALU.mult))
            chain.wait()
            chain(nc.vector.scalar_tensor_tensor(rowf, names["idxf"], float(P), rk, ALU.mult, ALU.add))
            for j in (2, 3):
                chain(nc.vector.scalar_tensor_tensor(jj, rk, float(P * j), jj, ALU.is_ge, ALU.add))
                chain.wait()
            chain(nc.vector.scalar_tensor_tensor(rowf, jj, float(NE * P - P), rowf, ALU.mult, ALU.add))
            chain.wait()
            chain(nc.vector.tensor_scalar(rowf, rowf, float(-NE * P), 0.0, ALU.add, ALU.max))
            chain.wait()
            nc.vector.tensor_copy(rowj, rowf).then_inc(route_done, 1)
            cnt = names["cnt"]
            for j in range(3):
                chain(nc.vector.tensor_scalar(ov_ex[:, j * NE:(j + 1) * NE], cnt[0:1, :], float(P * (j + 1)), None, ALU.is_gt))
            chain.wait()
            chain(nc.vector.tensor_tensor_scan(ov_pos, ov_ex, ov_ex, 0.0, ALU.add, ALU.bypass))
            chain(nc.vector.tensor_tensor(ov_c, iota[0:1, 0:96], ov_ex, ALU.mult))
            chain.wait()
            chain(nc.vector.tensor_scalar(ov_tab, iota[0:1, 0:16], 1.0, None, ALU.add))
            chain.wait()
            chain(nc.vector.tensor_tensor(ov_eq, ov_pos.unsqueeze(1).to_broadcast([1, 16, 96]),
                                          ov_tab.unsqueeze(2).to_broadcast([1, 16, 96]), ALU.is_equal))
            chain.wait()
            chain(nc.vector.tensor_tensor(ov_eq, ov_eq, ov_c.unsqueeze(1).to_broadcast([1, 16, 96]), ALU.mult))
            chain.wait()
            chain(nc.vector.tensor_reduce(ov_tab, ov_eq, AX.X, ALU.add))
            chain.wait()
            chain(nc.vector.tensor_copy(table, ov_tab))
            chain.wait()
            nc.vector.tensor_copy(n_over, ov_pos[:, 95:96]).then_inc(route_done, 1)

            def esplit(i, p):
                if p % EP in POOL:
                    return
                dve.wait_ge(w_hi, i * EP + (DP + p + 1))
                nc.vector.tensor_tensor(wl[:, (DP + p) % SPL, :], raw_e(p // 2)[:, p % 2 * PC:(p % 2 + 1) * PC], wh[:, (DP + p) % SPL, :],
                                        ALU.subtract).then_inc(w_lo, 1)

            def expert(i, last=False, alone=False):
                if alone:
                    for p in range(AHEAD):
                        esplit(i, p)
                for p in range(EP):
                    if p + AHEAD < EP or not (last or alone):
                        esplit(i, p + AHEAD)
                    if p in (4, 12):
                        half = p // 8
                        dve.wait_ge(w_used, i * EP + (DP + p))
                        nc.vector.tensor_scalar(glu, ps[:, 2 * half, :], LIMIT, None,
                                                ALU.min).then_inc(glu_step, 1)
                    if p in (8, 16):
                        half = p // 8 - 1
                        k = i * 6 + 3 * half
                        v = lin
                        dve.wait_ge(w_used, i * EP + (DP + p))
                        nc.vector.tensor_scalar(v, ps[:, 2 * half + 1, :], -LIMIT, LIMIT,
                                                ALU.max, ALU.min).then_inc(glu_step, 1)
                        dve.wait_ge(glu_step, k + 2)
                        dve.wait_ge(gs_done, i * 2 + (half + 1))
                        nc.vector.scalar_tensor_tensor(v, v, 1.0, sig, ALU.add, ALU.mult).then_inc(glu_step, 1)
                    if p == 12:
                        act_lo(i, 0)
                    if p == 19:
                        act_lo(i, 1)

            def act_lo(i, half):
                dve.wait_ge(a_hi, i * 2 + (half + 1))
                nc.vector.tensor_tensor(a_l[:, half, :, :], ps[:, 6 + half, :].rearrange("p (a n) -> p a n", a=4),
                                        a_h[:, half, :, :], ALU.subtract).then_inc(a_lo, 1)

            with dve.Fori(0, NE - 1) as i:
                expert(i)
            expert(NE - 1, last=True)
            n = dve.value_load(n_over, min_val=0, max_val=OVER)
            with dve.If(n > 0):
                with dve.Fori(0, OVER) as j:
                    with dve.If(j < n):
                        expert(j + NE, alone=True)
                for u in range(TT * TOPK):
                    dve.wait_ge(over_in[u % 4], 16 * (u // 4 + 1))
                    if u:
                        dve.wait_ge(over_used, u)
                    nc.vector.scalar_tensor_tensor(res[:, u // TOPK, :], y_rows[:, u % 4, :], g2[:, u:u + 1],
                                                   res[:, u // TOPK, :], ALU.mult, ALU.add).then_inc(over_used, 1)
                dve.wait_ge(over_used, TT * TOPK)
            for t in range(TT):
                for k in range(TOPK):
                    u = TOPK * t + k
                    dve.wait_ge(row_in[u % 4], 16 * (u // 4 + 1))
                    if k:
                        dve.wait_ge(row_used, u)
                    nc.vector.scalar_tensor_tensor(res[:, t, :], y_rows[:, u % 4, :], gate[:, t, k:k + 1], res[:, t, :],
                                                   ALU.mult, ALU.add).then_inc(row_used, 1)
                dve.wait_ge(n_sq, 19 + t)
                chain(nc.vector.tensor_scalar(rstd[:, t:t + 1], ss[:, t:t + 1], 1.0 / D, EPS, ALU.mult, ALU.add))
                chain.wait()
                nc.vector.reciprocal(rstd[:, t:t + 1], rstd[:, t:t + 1]).then_inc(n_inv, 1)
                dve.wait_ge(n_sqrt, 5 + t)
                dve.wait_ge(in_gfin, 16)
                if t >= 2:
                    dve.wait_ge(stored[t % 2], 16 * (t // 2))
                nc.vector.scalar_tensor_tensor(o_sb[:, t % 2, :], res[:, t, :], rstd[:, t:t + 1], g_fin_b,
                                               ALU.mult, ALU.mult).then_inc(f_out, 1)

        @block.tensor
        def _(pe):
            def three(o, a_hi_, a_lo_, b_hi_, b_lo_, start, stop):
                nc.tensor.matmul(o, a_hi_, b_hi_, start=start, stop=False)
                nc.tensor.matmul(o, a_hi_, b_lo_, start=False, stop=False)
                return nc.tensor.matmul(o, a_lo_, b_hi_, start=False, stop=stop)

            def project(name, oh_, ol_, ready=None, meanwhile={}):
                s = slabs[name]
                for c in range(2 * s.chunks):
                    g = 2 * s.chunk0 + c
                    pe.wait_ge(w_lo, g + 1)
                    w_h, w_l = (v[:, g % SPL, :].rearrange("p (a n) -> p a n", a=2) for v in (wh, wl))
                    for t in range(s.tiles):
                        if c == 0 and s.bank_free[t]:
                            owner, count = s.bank_free[t]
                            pe.wait_ge(tile_out[owner], count)
                        for a in range(2):
                            k = 2 * c + a
                            if ready and t == 0:
                                pe.wait_ge(ready[0], ready[1] + k + 1)
                            first, last = k == 0, k == 4 * s.chunks - 1
                            o = ps[:, t, 0:s.cols]
                            cut = slice(t * P, (t + 1) * P)
                            if s.kind == "T":
                                ins = three(o, w_h[:, a, cut], w_l[:, a, cut], oh_[:, k, :], ol_[:, k, :], first, last)
                            else:
                                ins = three(o, oh_[:, k, cut], ol_[:, k, cut], w_h[:, a, :], w_l[:, a, :], first, last)
                        if t == s.tiles - 1:
                            ins.then_inc(w_used, 1)
                        elif c == 2 * s.chunks - 1:
                            ins.then_inc(tile_done, 1)
                    if c in meanwhile:
                        meanwhile[c]()

            def transposes(src, tiles, n0):
                for k in range(KT):
                    if n0 + k >= 4:
                        pe.wait_ge(op_lo, n0 + k - 3)
                    for t in range(tiles):
                        ins = nc.tensor.transpose(ps[:, 4 + k % 4, t * P:(t + 1) * P], src[:, t, k * P:(k + 1) * P], ident)
                    ins.then_inc(tr_done, 1)

            pe.wait_ge(in_mats, 32)
            pe.wait_ge(n_xs, TT)
            transposes(x_nat, TT, 0)
            project("sbq", op_h, op_l, (op_lo, 0))
            project("sbk", op_h, op_l)
            project("sbv", op_h, op_l)
            units = [(h, kb) for h in range(HEADS) for kb in (3, 2, 1, 0)]
            pe.wait_ge(tile_out["act"], 12)
            for step in range(len(units) + 5):
                if step < len(units):
                    h, kb = units[step]
                    n = T - P * kb
                    r = 64 * (h % 2)
                    if step >= 6:
                        pe.wait_ge(wexp_done, step - 5)
                    nc.tensor.matmul(ps[:, step % 6, 0:n], k_sb[r:r + 64, h // 2, kb * P:(kb + 1) * P],
                                     q_sb[r:r + 64, h // 2, kb * P:T], start=True, stop=True).then_inc(z_done, 1)
                if 3 <= step < len(units) + 3:
                    u = step - 3
                    h, kb = units[u]
                    pe.wait_ge(soft_done, u + 1)
                    for b in range(3, kb - 1, -1):
                        n = T - P * b
                        ins = nc.tensor.matmul(ps[:, u % 6, P * (b - kb):P * (b - kb) + n], neg_from if b == kb else neg_ones,
                                               soft[:, h % 2, OFF[b]:OFF[b] + n], start=False, stop=True,
                                               skip_group_check=True)
                    ins.then_inc(zc_done, 1)
                if step >= 8 and step % 4 == 0:
                    head_out(pe, step // 4 - 2)
            pe.wait_ge(wexp_done, len(units))
            project("rq", op_h, op_l)
            project("rk", op_h, op_l)
            pe.wait_ge(tile_out["act"], 20)
            for u in range(8):
                if u >= 4:
                    pe.wait_ge(rot_out, u - 3)
                elif u == 0:
                    pe.wait_ge(o_lo, HEADS)
                nc.tensor.matmul(ps[:, 4 + u % 4, :], rot_swap, (q_r, k_r)[u // 4][:, u % 4, :], start=True,
                                 stop=True).then_inc(rot_done, 1)
            for name in ("rv0", "rv1", "rg0", "rg1"):
                project(name, op_h, op_l)
            pe.wait_ge(tile_out["act"], 36)
            pe.wait_ge(rot_out, 8)
            for h in range(HEADS + 1):
                if h < HEADS:
                    r = 64 * (h % 2)
                    for kb in range(4):
                        n = T - P * kb
                        if h >= 1:
                            pe.wait_ge(sc_out, 4 * (h - 1) + kb + 1)
                        nc.tensor.matmul(ps[:, 4 + kb, 0:n], k_r[r:r + 64, h // 2, kb * P:(kb + 1) * P],
                                         q_r[r:r + 64, h // 2, kb * P:T], start=True, stop=True).then_inc(sc_done, 1)
                if h >= 1:
                    g = h - 1
                    pe.wait_ge(sc_out, 4 * (g + 1))
                    if g >= 2:
                        pe.wait_ge(ro_out, 4 * (g - 1))
                    for t in range(TT):
                        for kb in range(t + 1):
                            a = OFFA[kb] + (t - kb) * P
                            ins = nc.tensor.matmul(ps[:, g % 2, t * P:(t + 1) * P], scores[:, g % 2, a:a + P],
                                                   v_r[:, kb, g * P:(g + 1) * P], start=(kb == 0), stop=(kb == t))
                    ins.then_inc(ro_done, 1)
            pe.wait_ge(ro_out, 4 * HEADS)
            for name in ("gs0", "gs1", "gr0", "gr1"):
                project(name, op_h, op_l)
            transposes(y_r, TT, KT)
            project("so0", op2_h, op2_l)
            project("ro0", op_h, op_l, (op_lo, KT))
            project("so1", op2_h, op2_l)
            project("ro1", op_h, op_l)
            pe.wait_ge(n_xs, TT + MT)
            transposes(mem_nat, MT, 3 * KT)
            project("mo0", op_h, op_l, (op_lo, 2 * KT))
            project("mo1", op_h, op_l)
            project("mk0", opm_h, opm_l, (op_lo, 3 * KT))
            for name in ("mk1", "mv0", "mv1"):
                project(name, opm_h, opm_l)
            pe.wait_ge(n_xs, 2 * TT + MT)
            transposes(xs2, TT, 4 * KT)
            project("cq0", op_h, op_l, (op_lo, 4 * KT))
            project("cq1", op_h, op_l)
            pe.wait_ge(tile_out["act"], outs_total["act"])
            for u in range(XH * TT + 5):
                if u < XH * TT:
                    hd, t = u // TT, u % TT
                    if u >= 4:
                        pe.wait_ge(xs_exp, u - 3)
                    for dt in range(2):
                        ins = nc.tensor.matmul(ps[:, u % 4, 0:M], q_x[:, 2 * hd + dt, t * P:(t + 1) * P],
                                               k_x[:, 2 * hd + dt, :], start=(dt == 0), stop=(dt == 1))
                    ins.then_inc(xs_done, 1)
                if 2 <= u < XH * TT + 2:
                    v = u - 2
                    pe.wait_ge(xs_prob, v + 1)
                    if v >= 2:
                        pe.wait_ge(xt_out, v - 1)
                    for m in range(MT):
                        ins = nc.tensor.transpose(ps[:, 4 + v % 2, m * P:(m + 1) * P], prob[:, v % 4, m * P:(m + 1) * P], ident)
                    ins.then_inc(xt_done, 1)
                if u >= 8 and u % TT == 0:
                    cross_out(pe, u // TT - 2)
            project("co0", op_h, op_l, (op_lo, 5 * KT))

            def router_transposes(half):
                for t in range(TT):
                    pe.wait_ge(tile_out["dve"], slabs[f"co{half}"].out0 + t + 1)
                    for k in range(4 * half, 4 * half + 4):
                        ins = nc.tensor.transpose(ps[:, ROUTER_BANK[k], t * P:(t + 1) * P], res[:, t, k * P:(k + 1) * P], ident)
                        if t == TT - 1:
                            ins.then_inc(ht_done, 1)

            def router_product(half):
                if half == 0:
                    pe.wait_ge(rt_ready, 1)
                    pe.wait_ge(ht_out, 4)
                for k in range(4 * half, 4 * half + 4):
                    if half == 1:
                        pe.wait_ge(ht_out, k + 1)
                    ins = nc.tensor.matmul(ps[0:NE, 4, :], w_rt[:, k, :], h_t[:, k % 4, :], start=(k == 0),
                                           stop=(k == KT - 1), skip_group_check=True)
                ins.then_inc((lg_half, lgt_done)[half], 1)

            project("co1", op_h, op_l, meanwhile={1: lambda: router_transposes(0), 2: lambda: router_product(0)})
            router_transposes(1)
            router_product(1)
            pe.wait_ge(lgt_out, 1)
            for t in range(TT):
                ins = nc.tensor.transpose(ps[:, 1, t * NE:(t + 1) * NE], logit_t[:, t * P:(t + 1) * P], ident[0:NE, 0:NE])
            ins.then_inc(lg_done, 1)
            pe.wait_ge(rank_in, 1)
            for t in range(TT):
                for b in range(t + 1):
                    nc.tensor.matmul(ps[:, 2, t * NE:(t + 1) * NE], before_b if b == t else ones_b, sel_b[:, b, :],
                                     start=(b == 0), stop=(b == t))
            for b in range(TT):
                ins = nc.tensor.matmul(ps[:, 3, 0:NE], ones_b, sel_b[:, b, :], start=(b == 0), stop=(b == TT - 1))
            ins.then_inc(rank_done, 1)

            def gather(m, u):
                src = (hn_h, hn_l)[u % 2]
                for a in range(2):
                    k = u - u % 2 + a
                    for t in range(TT):
                        ins = nc.tensor.matmul(ps[:, u % 4, a * 256:(a + 1) * 256], src[:, t, k * P:(k + 1) * P],
                                               pick[:, t, :, :].rearrange("p b n -> p (b n)"), start=(t == 0), stop=(t == TT - 1))
                ins.then_inc(gath, 1)

            def gather_alone(m):
                for u in range(8):
                    if u >= 4:
                        pe.wait_ge(x_out, m * 8 + (u - 3))
                    gather(m, u)

            def expert(i, m, b=0, following=False, first=False):
                for p in range(16):
                    q = p // 4
                    bank = ps[:, q, :]
                    if b == 0 and p != 1 and p < 4:
                        pe.wait_ge(x_out, m * 8 + {0: 5, 2: 6, 3: 8}[p])
                    if p % 4 == 0:
                        r, col = divmod((q % 2) * DFF + (q // 2) * 512, BC)
                        if q == 0:
                            pe.wait_ge(bsel_ready, i + 1)
                        nc.tensor.matmul(bank, bsel[64 * r:64 * r + 64, :], bias[64 * r:64 * r + 64, col:col + 512], start=True, stop=False)
                    wait_lo(pe, i, p)
                    s = (DP + p) % SPL
                    for a in range(2):
                        k = 2 * (p % 4) + a
                        ins = three(bank, x_h[:, k, b, :], x_l[:, k, b, :], wh[:, s, a * 512:(a + 1) * 512],
                                    wl[:, s, a * 512:(a + 1) * 512], False, k == KT - 1)
                    ins.then_inc(w_used, 1)
                    if p == 11:
                        turn(i, 0)
                for n in range(2):
                    if n == 0 and not first:
                        pe.wait_ge(y_evac, i * 2)
                    ins = nc.tensor.matmul(ps[:, 4 + n, :], bsel[64:128, :], bias[64:128, 2 * D - BC + n * 512:2 * D - BC + (n + 1) * 512],
                                           start=True, stop=False)
                ins.then_inc(bsel_used, 1)
                for f in range(KT):
                    p = 16 + f
                    s = (DP + p) % SPL
                    wait_lo(pe, i, p)
                    if f % 4 == 0:
                        pe.wait_ge(a_lo, i * 2 + (f // 4 + 1))
                    for n in range(2):
                        cut = slice(n * 512, (n + 1) * 512)
                        ins = three(ps[:, 4 + n, :], a_h[:, f // 4, f % 4, :], a_l[:, f // 4, f % 4, :], wh[:, s, cut], wl[:, s, cut],
                                    False, f == KT - 1)
                    ins.then_inc(w_used, 1)
                    if f == 2:
                        turn(i, 1)
                    if following:
                        if f == 0:
                            pe.wait_ge(pick_ready, m * 8 + 8)
                        if f >= 4:
                            pe.wait_ge(x_out, m * 8 + (f + 5))
                        gather(m + 1, f)

            def turn(i, half):
                pe.wait_ge(glu_step, i * 6 + (3 * half + 3))
                for a in range(4):
                    ins = nc.tensor.transpose(ps[:, 6 + half, a * P:(a + 1) * P], lin[:, a * P:(a + 1) * P], ident)
                ins.then_inc(at_done, 1)

            pe.wait_ge(nat_lo, TT)
            pe.wait_ge(b_lo, 2)
            pe.wait_ge(pick0_ready, 8)
            gather_alone(0)
            expert(0, 0, first=True)
            expert(1, 0, b=1, following=True)
            with pe.Fori(1, NE // 2 - 1) as m:
                expert(m * 2, m)
                expert(m * 2 + 1, m, b=1, following=True)
            expert(NE - 2, NE // 2 - 1)
            expert(NE - 1, NE // 2 - 1, b=1)
            pe.wait_ge(route_done, 3)
            n = pe.value_load(n_over, min_val=0, max_val=OVER)
            with pe.If(n > 0):
                with pe.Fori(0, OVER) as j:
                    with pe.If(j < n):
                        pe.wait_ge(pick_ready, j * 8 + NE * 4)
                        gather_alone(j + NE // 2)
                        expert(j + NE, j + NE // 2)

OFF = {3: 0, 2: 128, 1: 384, 0: 768}
OFFA = {0: 0, 1: 512, 2: 896, 3: 1152}
ROUTER_BANK = (4, 5, 6, 7, 5, 6, 7, 0)
TR_RET = 2 * KT
_S, _N, _O = lay_slabs()
MERGED = _S["ro1"].out0 + 4
MIXED = _S["mo1"].out0 + 4
GATED = _S["gr1"].out0 + 4

_INS = ["x", "mem", "g_mix", "w_in", "w_sb_o", "w_ret_o", "w_mix_out", "g_xattn", "g_mem", "w_cq", "w_ckv", "w_co",
        "g_moe", "w_router", "b_router", "w_exp_in", "b_exp_in", "w_exp_out", "b_exp_out", "g_final"]


def kernel(**inputs):
    import concourse.bacc as _bacc
    from concourse.bass_utils import run_bass_kernel_spmd as _run

    nc = _bacc.Bacc("TRN2", target_bir_lowering=False, num_devices=1)
    arrays, args = {}, []
    given = {name: np.ascontiguousarray(inputs[name]) for name in _INS}
    given.update(constant_tables())
    for name, a in given.items():
        arrays[f"in_{name}"] = a
        args.append(nc.dram_tensor(f"in_{name}", a.shape, mybir.dt.from_np(a.dtype), kind="ExternalInput").ap())
    args.append(nc.dram_tensor("out_rows", (1, T, D), F32, kind="ExternalOutput").ap())
    layer_kernel(nc, *args)
    r = _run(nc, [arrays], core_ids=[0])
    return r.results[0]["out_rows"]
```

```python
from contextlib import ExitStack

import numpy as np

import concourse.bass as bass
from concourse import mybir

ALU = mybir.AluOpType
ACT = mybir.ActivationFunctionType
F32 = mybir.dt.float32
F32R = mybir.dt.float32r
BF16 = mybir.dt.bfloat16
U32 = mybir.dt.uint32
AX = mybir.AxisListType

P = 128
T = 512
TT = T // P
D = 1024
KT = D // P
M = 256
MT = M // P
HEADS = 8
XH = 4
XD = D // XH
NE = 32
TOPK = 4
DFF = 1024
EPS = 1e-5
LIMIT = 7.0
ALPHA = 1.702
BC = 3 * D // 2
NC = 4 * NE
OVER = T * TOPK // P - 1
RAW = 4
RAWE = 6
CH = 2048
PC = CH // 2
SPL = 6
AHEAD = 5
ROWS = RAW * 2
EC = 12
EP = 2 * EC
POOL = (9, 14, 18, 20, 22)
LAG = 3

SLABS = [("sbq", "T", 2, 4, T, "act"), ("sbk", "T", 2, 4, T, "act"), ("sbv", "N", 2, 4, 512, "act"),
         ("rq", "T", 2, 4, T, "act"), ("rk", "T", 2, 4, T, "act"),
         ("rv0", "N", 2, 4, 512, "act"), ("rv1", "N", 2, 4, 512, "act"),
         ("rg0", "N", 2, 4, 512, "act"), ("rg1", "N", 2, 4, 512, "act"),
         ("gs0", "T", 2, 4, T, "act"), ("gs1", "T", 2, 4, T, "act"),
         ("gr0", "T", 2, 4, T, "act"), ("gr1", "T", 2, 4, T, "act"),
         ("so0", "T", 1, 4, T, "dve"), ("ro0", "T", 2, 4, T, "dve"),
         ("so1", "T", 1, 4, T, "dve"), ("ro1", "T", 2, 4, T, "dve"),
         ("mo0", "N", 2, 4, 512, "dve"), ("mo1", "N", 2, 4, 512, "dve"),
         ("mk0", "T", 2, 4, M, "act"), ("mk1", "T", 2, 4, M, "act"),
         ("mv0", "N", 2, 2, 512, "act"), ("mv1", "N", 2, 2, 512, "act"),
         ("cq0", "T", 2, 4, T, "act"), ("cq1", "T", 2, 4, T, "act"),
         ("co0", "N", 2, 4, 512, "dve"), ("co1", "N", 2, 4, 512, "dve")]


class Slab:

    def __init__(self, spec, chunk0, tile0, prev):
        self.name, self.kind, self.chunks, self.tiles, self.cols, self.owner = spec
        self.chunk0 = chunk0
        self.tile0 = tile0
        self.out0 = prev.get(self.owner, 0)


def lay_slabs():
    slabs, chunk, tile, outs = {}, 0, 0, {"act": 0, "dve": 0}
    last_user = [None] * 4
    for spec in SLABS:
        s = Slab(spec, chunk, tile, outs)
        s.bank_free = [last_user[t] for t in range(s.tiles)]
        for t in range(s.tiles):
            last_user[t] = (s.owner, outs[s.owner] + t + 1)
        chunk += s.chunks
        tile += s.tiles - 1
        outs[s.owner] += s.tiles
        slabs[s.name] = s
    return slabs, chunk, outs


LOG_DECAY = np.log1p(-np.exp2(-5.0 - np.arange(HEADS)))


def constant_tables():
    i = np.arange(P)
    mats = np.zeros((8, P, P), np.float32)
    mats[0] = np.eye(P)
    mats[1] = -1.0 * (i[:, None] >= i[None, :])
    mats[2] = -1.0
    for m in range(P):
        d = m % 64
        mats[3, m + 32 if d < 32 else m - 32, m] = -1.0 if d < 32 else 1.0
    mats[4] = i[:, None] < i[None, :]
    mats[5] = 1.0
    mats[6] = i[None, :]
    mats[7] = (i[:, None] % NE) == (i[None, :] % NE)
    inv = np.float32(10000.0) ** (-np.arange(0, 64, 2, dtype=np.float32) / np.float32(64))
    ang = (np.arange(T, dtype=np.float32)[None, :] * inv[:, None]).astype(np.float32)
    rot = np.stack([np.tile(np.cos(ang), (4, 1)), np.tile(np.sin(ang), (4, 1))]).astype(np.float32)
    u = np.arange(2 * P)[None, :] - i[:, None]
    dec = np.where(u >= 0, np.exp(LOG_DECAY[:, None, None] * np.maximum(u, 0)), 0.0) / 8.0
    return {"c_mats": mats, "c_rot": rot, "c_dec": dec.astype(np.float32)}


def layer_kernel(nc, x, mem, g_mix, w_in, w_sb_o, w_ret_o, w_mix_out, g_xattn, g_mem, w_cq, w_ckv, w_co,
                 g_moe, w_router, b_router, w_exp_in, b_exp_in, w_exp_out, b_exp_out, g_final,
                 c_mats, c_rot, c_dec, out):
    slabs, DENSE, outs_total = lay_slabs()
    assert DENSE % RAW == 0 and EC % RAWE == 0 and EP % SPL == 0
    DP = 2 * DENSE
    y_main = nc.dram_tensor("y_main", [NE * P, D], F32, kind="Internal").ap()
    y_over = nc.dram_tensor("y_over", [(NC - NE) * P, D], F32, kind="Internal").ap()

    with ExitStack() as ctx:
        def sb(name, shape, dt=F32):
            return ctx.enter_context(nc.sbuf_tensor(name, shape, dt))

        def sem(name):
            return ctx.enter_context(nc.semaphore(name))

        raw = sb("raw", [P, RAW, CH])
        wh = sb("wh", [P, SPL, PC], F32R)
        wl = sb("wl", [P, SPL, PC], F32R)
        oph = sb("oph", [P, KT * T], F32R)
        opl = sb("opl", [P, KT * T], F32R)
        op2 = sb("op2", [P, 4096], F32R)
        acts = sb("acts", [P, 3072], F32R)
        bsel = sb("bsel", [P, P], F32R)
        bias = sb("bias", [P, BC], F32R)
        ident = sb("ident", [P, P])[:, :]
        small = sb("small", [P, 100])
        work = sb("work", [P, 15360])
        ps = ctx.enter_context(nc.psum_tensor("ps", [P, 8, 512], F32))

        gmix_c, gxat_c, gmem_c = (small[:, 8 * n:8 * n + 8] for n in range(3))
        ss, rstd = small[:, 24:28], small[:, 28:32]
        msum, mrstd = small[:, 32:34], small[:, 34:36]
        retstat = small[:, 36:60]
        retmv = small[:, 60:68]
        retrs = small[:, 92:100].rearrange("p (b t) -> p b t", b=2)
        xmax = small[:, 72:76]
        xsum = small[:, 76:80]
        xrec = small[:, 80:84]
        cur = small[:, 84:92].rearrange("p (t o) -> p t o", t=TT)

        def w_(a, n):
            return work[:, a:a + n]

        def view(a, tiles, n):
            return w_(a, tiles * n).rearrange("p (t n) -> p t n", t=tiles)

        neg_from, neg_ones, rot_swap = (w_(14976 + P * n, P) for n in range(3))
        x_nat = view(0, TT, D)
        q_sb, k_sb, v_sb = view(0, 4, T), view(2048, 4, T), view(4096, TT, 512)
        abs_z = view(6144, 3, 512)
        soft = view(7680, 2, 1280)
        wts = view(10240, 2, 1280)
        q_r, k_r, v_r = view(0, 4, T), view(2048, 4, T), view(4096, TT, D)
        y_r = view(8192, TT, D)
        cosine, sine = w_(12288, T), w_(12800, T)
        rot_tmp = view(13312, 2, T)
        decay = view(12288, 2, 2 * P)
        scores = view(12800, 2, 1280)
        m_sb, m_ret = view(0, KT, T), view(4096, KT, T)
        res = view(8192, TT, D)
        xs2 = view(0, TT, D)
        q_x, k_x, v_x = view(0, KT, T), view(4096, KT, M), view(6144, MT, D)
        mem_nat = view(12288, MT, D)
        prob = view(12288, 4, M)
        prob_t = view(13312, 2, MT * T)
        neg_from_r, neg_ones_r = (op2[:, 1536 + P * n:1536 + P * n + P] for n in range(2))

        def soft_parts(h, kb):
            n = T - P * kb
            if h % 2 == 0:
                return acts[:, OFF[kb]:OFF[kb] + n], acts[:, 1280 + OFF[kb]:1280 + OFF[kb] + n]
            low = {0: acts[:, 2560:3072], 1: op2[:, 3584:3968], 2: bias[:, 1280:1536], 3: bsel[:, :]}[kb]
            return bias[:, OFF[kb]:OFF[kb] + n], low

        h_nat = view(0, TT, D)
        bias_f = w_(4096, BC)
        h_t = view(4096, 4, T)
        g_moe_b = w_(7168, D)
        mats2 = view(12288, 4, P)
        before, ones, iota, exp_rows = (mats2[:, n, :] for n in range(4))
        logit = view(12800, TT, NE)
        before_b, ones_b = (w_(15104 + 64 * n, 64).bitcast(BF16) for n in range(2))
        sel_b = w_(15232, 64).bitcast(BF16).rearrange("p (t e) -> p t e", t=TT)
        g_moe_c = small[:, 0:8]
        logit_t = work[0:NE, 6656:7168]
        square = view(0, 8, 512)
        ss_more = xmax
        at = 12928
        names = {}
        for name, n in (("top", 32), ("topi", 32), ("idxf", 16), ("gate", 16), ("gsum", 4), ("grec", 4), ("nmax", 4),
                        ("rk", 16), ("jj", 16), ("jm", 16), ("rowf", 16), ("rowi", 16), ("rowj", 16), ("gate2", 16), ("oh", 512), ("sel", 128),
                        ("rank", 128), ("slot", 128), ("cnt", 32), ("slots", 512), ("brt", 32), ("tabi", 16), ("nov", 1)):
            names[name] = w_(at, n)
            at += n
        assert at <= 15360
        w_rt = view(6144, KT, NE)
        top = names["top"].rearrange("p (t n) -> p t n", t=TT)
        topi = names["topi"].bitcast(U32).rearrange("p (t n) -> p t n", t=TT)
        idxf = names["idxf"].rearrange("p (t n) -> p t n", t=TT)
        gate = names["gate"].rearrange("p (t n) -> p t n", t=TT)
        rowi, rowj = names["rowi"].bitcast(U32), names["rowj"].bitcast(U32)
        oh = names["oh"].rearrange("p (t k e) -> p t k e", t=TT, k=TOPK)
        oh2 = w_(6656, 512).rearrange("p (t k e) -> p t k e", t=TT, k=TOPK)
        sel = names["sel"].rearrange("p (t e) -> p t e", t=TT)
        rank = names["rank"].rearrange("p (t e) -> p t e", t=TT)
        slot = names["slot"].rearrange("p (t e) -> p t e", t=TT)
        slots = names["slots"].rearrange("p (t c) -> p t c", t=TT)
        table = names["tabi"][0:1, :].bitcast(U32)
        n_over = names["nov"][0:1, :].bitcast(U32)
        ov_ex, ov_pos, ov_c = (work[0:1, 4096 + 96 * n:4096 + 96 * n + 96] for n in range(3))
        ov_eq = work[0:1, 4608:4608 + 16 * 96].rearrange("p (i c) -> p i c", i=16)
        ov_tab = work[0:1, 6400:6416]
        x_h = op2[:, 0:2048].rearrange("p (t b n) -> p t b n", t=KT, b=2)
        x_l = op2[:, 2048:4096].rearrange("p (t b n) -> p t b n", t=KT, b=2)
        glu, sig, lin = (w_(512 * n, 512) for n in range(3))
        pick = acts[:, 0:1024].rearrange("p (t b n) -> p t b n", t=TT, b=2)
        a_h, a_l = (acts[:, 1024 * n:1024 * n + 1024].rearrange("p (h t n) -> p h t n", h=2, t=4) for n in (1, 2))
        y_sb = w_(3072, D)
        raw_more = view(4096, 2, CH)

        def wait_lo(eng, i, p):
            mine = sum(q <= p % EP for q in POOL)
            b = p // EP
            if p % EP in POOL:
                eng.wait_ge(w_lo_pool, i * len(POOL) + (b * len(POOL) + mine))
            else:
                eng.wait_ge(w_lo, i * (EP - len(POOL)) + (b * (EP - len(POOL)) + DP + p % EP + 1 - mine))

        def raw_e(c):
            return raw[:, c % RAWE, :] if c % RAWE < RAW else raw_more[:, c % RAWE - RAW, :]

        y_rows = raw[:, :, :].rearrange("p c (b n) -> p (c b) n", b=2)
        g_fin_b = w_(5120, D)
        o_sb = view(6144, 2, D)

        op_h = oph[:, :].rearrange("p (t n) -> p t n", t=KT)
        op_l = opl[:, :].rearrange("p (t n) -> p t n", t=KT)
        op2_h = op2[:, 0:2048].rearrange("p (t n) -> p t n", t=4)
        op2_l = op2[:, 2048:4096].rearrange("p (t n) -> p t n", t=4)
        opm_h = op2[:, 0:2048].rearrange("p (t n) -> p t n", t=KT)
        opm_l = op2[:, 2048:4096].rearrange("p (t n) -> p t n", t=KT)
        hn_h = oph[:, :].rearrange("p (t n) -> p t n", t=TT)
        hn_l = opl[:, :].rearrange("p (t n) -> p t n", t=TT)

        w_landed = [sem(f"w_landed{n}") for n in range(RAWE)]
        w_hi, w_lo, w_lo_pool, w_used = sem("w_hi"), sem("w_lo"), sem("w_lo_pool"), sem("w_used")
        in_x = [sem(f"in_x{t}") for t in range(TT)]
        in_mats, in_cols, in_rot, in_mem, in_res = (
            sem(n) for n in ("in_mats", "in_cols", "in_rot", "in_mem", "in_res"))
        in_dec = [sem("in_dec0"), sem("in_dec1")]
        in_gmix, in_neg = sem("in_gmix"), sem("in_neg")
        in_moe, in_bias, in_gfin = sem("in_moe"), sem("in_bias"), sem("in_gfin")
        act_chain, dve_chain = sem("act_chain"), sem("dve_chain")
        tile_done = sem("tile_done")
        tile_out = {"act": sem("tile_out_act"), "dve": sem("tile_out_dve")}
        tr_done, op_hi, op_lo = sem("tr_done"), sem("op_hi"), sem("op_lo")
        z_done, soft_raw, soft_done, zc_done, wexp_done, wts_done, o_done, o_hi, o_lo = (
            sem(n) for n in ("z_done", "soft_raw", "soft_done", "zc_done", "wexp_done", "wts_done", "o_done", "o_hi", "o_lo"))
        ln_done, neg_ready, soft_hi, soft_lo = (sem(n) for n in ("ln_done", "neg_ready", "soft_hi", "soft_lo"))
        rot_done, rot_out = sem("rot_done"), sem("rot_out")
        sc_done, sc_out, ro_done, ro_out = (sem(n) for n in ("sc_done", "sc_out", "ro_done", "ro_out"))
        rs_var, rs_sqrt, y_done = sem("rs_var"), sem("rs_sqrt"), sem("y_done")
        n_sq, n_inv, n_sqrt, n_xs = (sem(n) for n in ("n_sq", "n_inv", "n_sqrt", "n_xs"))
        xs_done, xs_max, xs_exp, xs_prob, xt_done, xt_out, xo_done = (
            sem(n) for n in ("xs_done", "xs_max", "xs_exp", "xs_prob", "xt_done", "xt_out", "xo_done"))
        ht_done, ht_out, lg_half, lgt_done, lgt_out, lg_done, gate_exp, rank_in, rank_done, route_done = (
            sem(n) for n in ("ht_done", "ht_out", "lg_half", "lgt_done", "lgt_out", "lg_done", "gate_exp", "rank_in",
                             "rank_done", "route_done"))
        in_rt, rt_ready, pick0_ready = sem("in_rt"), sem("rt_ready"), sem("pick0_ready")
        nat_ready, nat_hi, nat_lo, nat_lo_pool, b_hi, b_lo = (sem(n) for n in ("nat_ready", "nat_hi", "nat_lo", "nat_lo_pool", "b_hi", "b_lo"))
        cur_ready, pick_ready, bsel_ready, bsel_used = (sem(n) for n in ("cur_ready", "pick_ready", "bsel_ready", "bsel_used"))
        gath, x_out, glu_step, sig_done, gs_done, at_done, a_hi, a_lo = (
            sem(n) for n in ("gath", "x_out", "glu_step", "sig_done", "gs_done", "at_done", "a_hi", "a_lo"))
        y_evac, y_stored = sem("y_evac"), sem("y_stored")
        pool_turn, sp_turn = sem("pool_turn"), sem("sp_turn")
        zero_ready, over_stored, over_used = (sem(n) for n in ("zero_ready", "over_stored", "over_used"))
        row_in = [sem(f"row_in{n}") for n in range(ROWS)]
        over_in = [sem(f"over_in{n}") for n in range(ROWS)]
        row_used, o_scaled, f_out, f_last = (sem(n) for n in ("row_used", "o_scaled", "f_out", "f_last"))
        stored = [sem("stored0"), sem("stored1")]

        def dense_source(g):
            for s in slabs.values():
                if s.chunk0 <= g < s.chunk0 + s.chunks:
                    break
            half, name = g - s.chunk0, s.name
            order = list(slabs)
            if order.index(name) < 13:
                src, col = w_in[0], order.index(name)
            else:
                src = {"so": w_sb_o, "ro": w_ret_o, "mo": w_mix_out, "mk": w_ckv, "mv": w_ckv,
                       "cq": w_cq, "co": w_co}[name[:2]][0]
                col = int(name[2]) + (2 if name[:2] == "mv" else 0)
            return src[half * 512:(half + 1) * 512, col * 512:(col + 1) * 512].rearrange("(a p) n -> p a n", p=P)

        def expert_sources(e):
            w1 = w_exp_in[0, bass.ds(e, 1), :, :].rearrange("o (a p) n -> p (o a) n", p=P)
            w2 = w_exp_out[0, bass.ds(e, 1), :, :].rearrange("o (a p) n -> p (o a) n", p=P)
            for half in range(2):
                for gl in range(2):
                    col = gl * DFF + half * 512
                    for a in (0, 4):
                        yield w1[:, a:a + 4, col:col + 512], "p (a n) -> p a n", 4
            for q in range(4):
                yield w2[:, 2 * q:2 * q + 2, :], "p (a n) -> p a n", 2

        class Chain:

            def __init__(self, eng, s):
                self.eng, self.s, self.n = eng, s, 0

            def __call__(self, ins):
                ins.then_inc(self.s, 1)
                self.n += 1

            def wait(self):
                self.eng.wait_ge(self.s, self.n)

        def head_out_act(act, h):
            act.wait_ge(o_done, h + 1)
            r = 64 * (h % 2)
            nc.scalar.activation(op2_h[r:r + 64, h // 2, :], ps[r:r + 64, 6 + h % 2, :], ACT.Copy).then_inc(o_hi, 1)

        def cross_hi(act, hd):
            for dt in range(2):
                act.wait_ge(xo_done, 2 * hd + dt + 1)
                nc.scalar.activation(op_h[:, 2 * hd + dt, :], ps[:, 6 + dt, :], ACT.Copy).then_inc(op_hi, 1)

        def head_out_dve(dve, h):
            dve.wait_ge(o_hi, h + 1)
            r = 64 * (h % 2)
            nc.vector.tensor_tensor(op2_l[r:r + 64, h // 2, :], ps[r:r + 64, 6 + h % 2, :], op2_h[r:r + 64, h // 2, :],
                                    ALU.subtract).then_inc(o_lo, 1)

        def cross_lo(dve, hd):
            for dt in range(2):
                k = 2 * hd + dt
                dve.wait_ge(op_hi, 5 * KT + k + 1)
                nc.vector.tensor_tensor(op_l[:, k, :], ps[:, 6 + dt, :], op_h[:, k, :], ALU.subtract).then_inc(op_lo, 1)

        def head_out(pe, h):
            pe.wait_ge(wts_done, 4 * h + 4)
            if h >= 2:
                pe.wait_ge(o_lo, h - 1)
            for kb in range(4):
                n = T - P * kb
                ins = nc.tensor.matmul(ps[:, 6 + h % 2, kb * P:T], v_sb[:, kb, (h // 2) * P:(h // 2 + 1) * P],
                                       wts[:, h % 2, OFF[kb]:OFF[kb] + n], start=(kb == 0), stop=(kb == 3),
                                       skip_group_check=True)
            ins.then_inc(o_done, 1)

        def cross_out(pe, hd):
            pe.wait_ge(xt_out, TT * (hd + 1))
            for dt in range(2):
                if hd >= 1:
                    pe.wait_ge(op_lo, 5 * KT + 2 * (hd - 1) + dt + 1)
                for m in range(MT):
                    a = hd * XD + dt * P
                    ins = nc.tensor.matmul(ps[:, 6 + dt, :], v_x[:, m, a:a + P],
                                           prob_t[:, hd % 2, m * T:(m + 1) * T], start=(m == 0), stop=(m == MT - 1))
                ins.then_inc(xo_done, 1)

        block = ctx.enter_context(nc.Block())

        @block.sync
        def _(sp):
            for t in range(TT):
                sp.dma_start(x_nat[:, t, :], x[0, t * P:(t + 1) * P, :]).then_inc(in_x[t], 16)
            for g in range(DENSE):
                if g >= RAW:
                    sp.wait_ge(w_lo, 2 * (g - RAW + 1))
                sp.dma_start(raw[:, g % RAW, :].rearrange("p (a n) -> p a n", a=4),
                             dense_source(g)).then_inc(w_landed[g % RAW], 16)

            def load_expert(i, e, first=False):
                for c, (src, pat, a) in enumerate(expert_sources(e)):
                    if not first or c >= RAWE:
                        p = 2 * (c - RAWE)
                        if p % EP in POOL or (p + 1) % EP in POOL:
                            wait_lo(sp, i, p)
                            sp.sem_inc(sp_turn, 1)
                        wait_lo(sp, i, p + 1)
                    elif c < RAW:
                        sp.wait_ge(w_lo, DP + 2 * (c - RAW + 1))
                    elif c == RAW:
                        sp.wait_ge(route_done, 3)
                    sp.dma_start(raw_e(c).rearrange(pat, a=a), src).then_inc(w_landed[c % RAWE], 16)

            load_expert(0, 0, first=True)
            with sp.Fori(1, NE) as i:
                load_expert(i, i)
            n = sp.value_load(n_over, min_val=0, max_val=OVER)
            with sp.If(n > 0):
                with sp.Fori(0, OVER) as j:
                    with sp.If(j < n):
                        c = sp.value_load(table[0:1, bass.ds(j, 1)], min_val=0, max_val=NC - NE - 1)
                        load_expert(j + NE, c % NE)
            for tt in range(TT):
                if tt < TT - 1:
                    sp.wait_ge(f_out, tt + 1)
                else:
                    sp.wait_ge(f_last, 1)
                sp.dma_start(out[0, tt * P:(tt + 1) * P, :], o_sb[:, tt % 2, :]).then_inc(stored[tt % 2], 16)
            sp.wait_ge(stored[0], 32)
            sp.wait_ge(stored[1], 32)

        @block.gpsimd
        def _(pool):
            pool.dma_start(ident, c_mats[0]).then_inc(in_mats, 16)
            for dst, src, done in ((gmix_c, g_mix, in_gmix), (gxat_c, g_xattn, in_cols), (gmem_c, g_mem, in_cols)):
                with nc.allow_non_contiguous_dma(reason="a gain for each channel"):
                    pool.dma_start(dst, src[0].rearrange("(k p) -> p k", p=P)).then_inc(done, 16)
            pool.dma_start(w_(14976, 3 * P).rearrange("p (c n) -> p c n", c=3),
                           c_mats[1:4].rearrange("c p n -> p c n")).then_inc(in_neg, 16)

            def keep_before(view_):
                return nc.gpsimd.affine_select(out=view_, in_=view_, pattern=[[1, P]], compare_op=ALU.is_gt, fill=0.0,
                                               base=0, channel_multiplier=-1)

            units = [(h, kb) for h in range(HEADS) for kb in (3, 2, 1, 0)]
            for step in range(len(units) + LAG):
                if step < len(units):
                    h, kb = units[step]
                    pool.wait_ge(soft_raw, step + 1)
                    keep_before(soft[:, h % 2, OFF[kb]:OFF[kb] + P]).then_inc(soft_done, 1)
                if step >= LAG:
                    h, kb = units[step - LAG]
                    pool.wait_ge(wexp_done, step - LAG + 1)
                    keep_before(wts[:, h % 2, OFF[kb]:OFF[kb] + P]).then_inc(wts_done, 1)
            pool.wait_ge(o_done, HEADS)
            pool.dma_start(w_(12288, 2 * T).rearrange("p (c n) -> p c n", c=2),
                           c_rot.rearrange("c p n -> p c n")).then_inc(in_rot, 16)
            for h in range(HEADS):
                if h == 0:
                    pool.wait_ge(rot_out, 8)
                if h >= 2:
                    pool.wait_ge(sc_out, 4 * (h - 1))
                pool.dma_start(decay[:, h % 2, :], c_dec[h]).then_inc(in_dec[h % 2], 16)
            pool.wait_ge(tr_done, TR_RET)
            pool.dma_start(mem_nat, mem[0].rearrange("(t p) d -> p t d", p=P)).then_inc(in_mem, 16)
            pool.dma_start(res, x[0].rearrange("(t p) d -> p t d", p=P)).then_inc(in_res, 16)
            pool.wait_ge(xo_done, 2 * XH)
            pool.dma_start(mats2, c_mats[4:8].rearrange("c p n -> p c n")).then_inc(in_moe, 16)
            pool.dma_start(names["brt"], b_router[0].partition_broadcast(P)).then_inc(in_moe, 16)
            pool.dma_start(w_rt, w_router[0].rearrange("(k p) e -> p k e", p=P)).then_inc(in_rt, 16)
            with nc.allow_non_contiguous_dma(reason="a gain for each channel"):
                pool.dma_start(g_moe_c, g_moe[0].rearrange("(k p) -> p k", p=P)).then_inc(in_rt, 16)
            pool.dma_start(g_moe_b, g_moe[0].partition_broadcast(P)).then_inc(in_moe, 16)
            for r in range(2):
                rows, more = slice(NE * r, NE * r + NE), slice(64 + NE * r, 64 + NE * r + NE)
                pool.dma_start(bias_f[rows, :], b_exp_in[0, :, 0:BC]).then_inc(in_bias, 16)
                pool.dma_start(bias_f[more, 0:2 * D - BC], b_exp_in[0, :, BC:2 * D]).then_inc(in_bias, 16)
                pool.dma_start(bias_f[more, 2 * D - BC:BC], b_exp_out[0]).then_inc(in_bias, 16)

            pool.wait_ge(in_rt, 32)
            nc.gpsimd.tensor_tensor(w_rt, w_rt, g_moe_c.unsqueeze(2).to_broadcast([P, KT, NE]), ALU.mult).then_inc(rt_ready, 1)
            pool.wait_ge(in_moe, 48)
            nc.gpsimd.tensor_copy(before_b, before).then_inc(rt_ready, 1)
            nc.gpsimd.tensor_copy(ones_b, ones).then_inc(rt_ready, 1)

            def choose_rows(m, c=None):
                pool.wait_ge(gath, m * 8)
                if c is None:
                    nc.gpsimd.tensor_copy(cur, slots[:, :, bass.ds(m * 2, 2)]).then_inc(cur_ready, 1)
                else:
                    nc.gpsimd.tensor_copy(cur, slots[:, :, bass.ds(c, 1)].to_broadcast([P, TT, 2])).then_inc(cur_ready, 1)
                pool.wait_ge(cur_ready, m)
                pool.sem_inc(pool_turn, 1)
                for t in range(TT):
                    for b in range(2):
                        nc.gpsimd.tensor_scalar(pick[:, t, b, :], iota, cur[:, t, b:b + 1], None,
                                                ALU.is_equal).then_inc(pick_ready, 1)

            def choose_bias(i, c, first=False):
                if not first:
                    pool.wait_ge(bsel_used, i)
                nc.gpsimd.tensor_copy(bsel[:, :], exp_rows[:, bass.ds(c, 1)].to_broadcast([P, P])).then_inc(bsel_ready, 1)

            choose_bias(0, 0, first=True)
            for t in (2, 3):
                pool.wait_ge(nat_hi, t + 1)
                nc.gpsimd.tensor_tensor(hn_l[:, t, :], h_nat[:, t, :], hn_h[:, t, :], ALU.subtract).then_inc(nat_lo_pool, 1)
            pool.wait_ge(route_done, 3)

            def gate_sigmoid(i, half):
                pool.wait_ge(sig_done, i * 2 + (half + 1))
                nc.gpsimd.tensor_tensor(sig, glu, sig, ALU.mult).then_inc(gs_done, 1)

            def split(i, p):
                pool.wait_ge(w_hi, i * EP + (DP + p + 1))
                s = (DP + p) % SPL
                nc.gpsimd.tensor_tensor(wl[:, s, :], raw_e(p // 2)[:, p % 2 * PC:(p % 2 + 1) * PC], wh[:, s, :],
                                        ALU.subtract).then_inc(w_lo_pool, 1)

            def block_work(i):
                split(i, POOL[0])
                gate_sigmoid(i, 0)
                split(i, POOL[1])
                gate_sigmoid(i, 1)
                for p in POOL[2:]:
                    split(i, p)

            def pair(m, last=False):
                i = m * 2
                block_work(i)
                choose_bias(i + 1, i + 1)
                if not last:
                    choose_rows(m + 1)
                block_work(i + 1)
                if not last:
                    choose_bias(i + 2, i + 2)

            pair(0)
            with pool.Fori(1, NE // 2 - 1) as m:
                pair(m)
            pair(NE // 2 - 1, last=True)
            n = pool.value_load(n_over, min_val=0, max_val=OVER)
            with pool.If(n > 0):
                pool.wait_ge(y_stored, NE * 16)
                nc.gpsimd.memset(y_sb, 0.0).then_inc(zero_ready, 1)
                with pool.Fori(0, OVER) as j:
                    with pool.If(j < n):
                        c = pool.value_load(table[0:1, bass.ds(j, 1)], min_val=0, max_val=NC - NE - 1)
                        choose_rows(j + NE // 2, c=c + NE)
                        choose_bias(j + NE, c % NE)
                        block_work(j + NE)
                pool.wait_ge(over_stored, n * 16 + 16)
                pool.sem_inc(pool_turn, 1)
                for u in range(TT * TOPK):
                    if u >= ROWS:
                        pool.wait_ge(over_used, u - ROWS + 1)
                    pool.indirect_dma_start(out=y_rows[:, u % ROWS, :], out_offset=None, in_=y_over,
                                            in_offset=bass.IndirectOffsetOnAxis(ap=rowj[:, u:u + 1], axis=0)
                                            ).then_inc(over_in[u % ROWS], 16)
                pool.wait_ge(over_used, TT * TOPK)
            pool.wait_ge(y_stored, NE * 16)
            for u in range(TT * TOPK):
                if u == ROWS:
                    pool.dma_start(g_fin_b, g_final.partition_broadcast(P)).then_inc(in_gfin, 16)
                if u >= ROWS:
                    pool.wait_ge(row_used, u - ROWS + 1)
                pool.indirect_dma_start(out=y_rows[:, u % ROWS, :], out_offset=None, in_=y_main,
                                        in_offset=bass.IndirectOffsetOnAxis(ap=rowi[:, u:u + 1], axis=0)
                                        ).then_inc(row_in[u % ROWS], 16)
            pool.wait_ge(in_gfin, 16)
            for t in range(TT - 1):
                pool.wait_ge(o_scaled, t + 1)
                nc.gpsimd.tensor_tensor(o_sb[:, t % 2, :], o_sb[:, t % 2, :], g_fin_b, ALU.mult).then_inc(f_out, 1)

        @block.scalar
        def _(act):
            chain = Chain(act, act_chain)

            def split(g):
                slot = g % SPL
                c = g // 2
                if g % 2 == 0:
                    act.wait_ge(w_landed[c % RAW], 16 * (c // RAW + 1))
                if g >= SPL:
                    act.wait_ge(w_used, g - SPL + 1)
                nc.scalar.activation(wh[:, slot, :], raw[:, c % RAW, g % 2 * PC:(g % 2 + 1) * PC], ACT.Copy).then_inc(w_hi, 1)

            def take(name, f, meanwhile={}):
                s = slabs[name]
                for c in range(2 * s.chunks):
                    split(2 * s.chunk0 + c + AHEAD)
                    if c in meanwhile:
                        meanwhile[c]()
                if s.owner != "act":
                    return
                for t in range(s.tiles):
                    if t < s.tiles - 1:
                        act.wait_ge(tile_done, s.tile0 + t + 1)
                    else:
                        act.wait_ge(w_used, 2 * (s.chunk0 + s.chunks))
                    f(t).then_inc(tile_out["act"], 1)

            def norm_stats(xv, tiles, acc, rs, sq0, inv_n, junk=ps[:, 6:8, :].rearrange("p a n -> p (a n)")):
                for t in range(tiles):
                    if t:
                        act.wait_ge(n_sq, sq0 + t)
                    nc.scalar.activation(junk, xv[:, t, :], ACT.Square,
                                         accum_out=acc[:, t:t + 1]).then_inc(n_sq, 1)
                act.wait_ge(n_inv, inv_n)
                nc.scalar.activation(rs, rs, ACT.Sqrt).then_inc(n_sqrt, 1)

            def operand_hi(dst, n0, tiles, cols, gain=None, first_tr=0, first=0):
                for k in range(first, tiles):
                    act.wait_ge(tr_done, first_tr + k + 1)
                    src = ps[:, 4 + k % 4, 0:cols]
                    nc.scalar.activation(dst[:, k, :], src, ACT.Copy,
                                         scale=1.0 if gain is None else gain[:, k:k + 1]).then_inc(op_hi, 1)

            act.preload_act_table_set("sqrt_and_others")
            for t in range(TT):
                act.wait_ge(in_x[t], 16)
                if t:
                    act.wait_ge(n_sq, t)
                nc.scalar.activation(ps[:, 0:2, :].rearrange("p a n -> p (a n)"), x_nat[:, t, :], ACT.Square,
                                     accum_out=ss[:, t:t + 1]).then_inc(n_sq, 1)
                if t:
                    act.wait_ge(n_inv, t)
                    nc.scalar.activation(rstd[:, t - 1:t], rstd[:, t - 1:t], ACT.Sqrt).then_inc(n_sqrt, 1)
            act.wait_ge(n_inv, TT)
            nc.scalar.activation(rstd[:, TT - 1:TT], rstd[:, TT - 1:TT], ACT.Sqrt).then_inc(n_sqrt, 1)
            split(0)
            act.wait_ge(in_gmix, 16)
            operand_hi(op_h, 0, KT, T, gmix_c, 0)
            for g in range(1, AHEAD):
                split(g)

            def copy(dst, scale=1.0):
                def f(t):
                    return nc.scalar.activation(dst[:, t, :], ps[:, t, 0:dst.shape[2]], ACT.Copy, scale=scale)
                return f

            take("sbq", copy(q_sb, 64 ** -0.5))
            take("sbk", copy(k_sb))
            take("sbv", copy(v_sb))
            act.preload_act_table_set("natural_log_exp_and_others")
            units = [(h, kb) for h in range(HEADS) for kb in (3, 2, 1, 0)]
            for step in range(len(units) + LAG):
                if step < len(units):
                    h, kb = units[step]
                    n = T - P * kb
                    z = abs_z[:, step % 3, 0:n]
                    act.wait_ge(z_done, step + 1)
                    if step >= 3:
                        act.wait_ge(soft_raw, step - 2)
                    chain(nc.scalar.activation(z, ps[:, step % 6, 0:n], ACT.Abs))
                    chain.wait()
                    chain(nc.scalar.activation(z, z, ACT.Exp, scale=-1.0))
                    chain.wait()
                    nc.scalar.activation(z, z, ACT.Ln, bias=1.0).then_inc(ln_done, 1)
                if step >= LAG:
                    u = step - LAG
                    h, kb = units[u]
                    n = T - P * kb
                    act.wait_ge(zc_done, u + 1)
                    if h >= 2 and kb == 3:
                        act.wait_ge(o_done, h - 1)
                    nc.scalar.activation(wts[:, h % 2, OFF[kb]:OFF[kb] + n], ps[:, u % 6, 0:n],
                                         ACT.Exp).then_inc(wexp_done, 1)
                if step >= LAG + 5 and (step - LAG) % 4 == 1 and step < len(units):
                    head_out_act(act, (step - LAG - 5) // 4)
            head_out_act(act, HEADS - 2)
            head_out_act(act, HEADS - 1)
            take("rq", copy(q_r))
            take("rk", copy(k_r))
            for n in range(2):
                def into(t, n=n):
                    return nc.scalar.activation(v_r[:, t, n * 512:(n + 1) * 512], ps[:, t, :], ACT.Copy)
                take(f"rv{n}", into)
            for n in range(2):
                def into(t, n=n):
                    return nc.scalar.activation(y_r[:, t, n * 512:(n + 1) * 512], ps[:, t, :], ACT.Silu)
                take(f"rg{n}", into)
            act.preload_act_table_set("sqrt_and_others")
            for h in range(HEADS):
                rs = retrs[:, h % 2, :]
                act.wait_ge(rs_var, h + 1)
                nc.scalar.activation(rs, rs, ACT.Sqrt).then_inc(rs_sqrt, 1)
                act.wait_ge(rs_sqrt, h + 1)
                for t in range(TT):
                    act.wait_ge(ro_out, 4 * h + t + 1)
                    yv = y_r[:, t, h * P:(h + 1) * P]
                    nc.scalar.activation(yv, yv, ACT.Copy, scale=rs[:, t:t + 1]).then_inc(y_done, 1)
            for n in range(2):
                def into(t, n=n):
                    return nc.scalar.activation(m_sb[:, 4 * n + t, :], ps[:, t, :], ACT.Sigmoid)
                take(f"gs{n}", into)
            for n in range(2):
                def into(t, n=n):
                    return nc.scalar.activation(m_ret[:, 4 * n + t, :], ps[:, t, :], ACT.Sigmoid)
                take(f"gr{n}", into)
            operand_hi(op_h, 8, 4, T, None, KT)
            take("so0", None)
            operand_hi(op_h, 8, KT, T, None, KT, 4)
            take("ro0", None)
            act.wait_ge(in_mem, 16)
            norm_stats(mem_nat, MT, msum, mrstd, 4, 5, w_(14336, D))
            take("so1", None)
            act.wait_ge(in_cols, 32)
            operand_hi(opm_h, 16, 4, M, gmem_c, 2 * KT)
            take("ro1", None, {1: lambda: operand_hi(opm_h, 16, KT, M, gmem_c, 2 * KT, 4)})
            act.wait_ge(w_used, 2 * slabs["ro1"].chunk0 + 4)
            for k in range(KT):
                act.wait_ge(tile_out["dve"], (slabs["ro0"].out0 if k < 4 else slabs["ro1"].out0 - 4) + k + 1)
                nc.scalar.activation(op_h[:, k, :], m_sb[:, k, :], ACT.Copy).then_inc(op_hi, 1)
            take("mo0", None)
            take("mo1", None)
            act.wait_ge(tile_out["dve"], MIXED)
            norm_stats(res, TT, ss, rstd, 6, 6)
            for n in range(2):
                def into(t, n=n):
                    return nc.scalar.activation(k_x[:, 4 * n + t, :], ps[:, t, 0:M], ACT.Copy)
                take(f"mk{n}", into)
            for n in range(2):
                def into(t, n=n):
                    return nc.scalar.activation(v_x[:, t, n * 512:(n + 1) * 512], ps[:, t, :], ACT.Copy)
                take(f"mv{n}", into)
            operand_hi(op_h, 32, KT, T, gxat_c, 3 * KT)
            for n in range(2):
                def into(t, n=n):
                    return nc.scalar.activation(q_x[:, 4 * n + t, :], ps[:, t, :], ACT.Copy, scale=XD ** -0.5)
                take(f"cq{n}", into)
            for u in range(XH * TT):
                act.wait_ge(xs_max, u + 1)
                nc.scalar.activation(prob[:, u % 4, :], ps[:, u % 4, 0:M], ACT.Exp, bias=xmax[:, u % 4:u % 4 + 1],
                                     accum_out=xsum[:, u % 4:u % 4 + 1]).then_inc(xs_exp, 1)
                if u % TT == 3 and u > TT:
                    cross_hi(act, u // TT - 1)
            cross_hi(act, XH - 1)
            take("co0", None)
            act.wait_ge(in_bias, 96)
            nc.scalar.activation(bias[:, :], bias_f, ACT.Copy).then_inc(b_hi, 1)
            act.preload_act_table_set("sqrt_and_others")

            def squares(half):
                acc = (ss, ss_more)[half]
                for t in range(TT):
                    act.wait_ge(tile_out["dve"], slabs[f"co{half}"].out0 + t + 1)
                    nc.scalar.activation(square[:, 4 * half + t, :], res[:, t, half * 512:(half + 1) * 512], ACT.Square,
                                         accum_out=acc[:, t:t + 1]).then_inc(n_sq, 1)

            def router_tile(k):
                act.wait_ge(ht_done, k + 1)
                if k == 4:
                    act.wait_ge(lg_half, 1)
                nc.scalar.activation(h_t[:, k % 4, :], ps[:, ROUTER_BANK[k], :], ACT.Copy).then_inc(ht_out, 1)

            def first_tiles():
                act.wait_ge(b_lo, 2)
                for k in range(4):
                    router_tile(k)

            take("co1", None, {1: lambda: squares(0), 2: first_tiles})
            squares(1)
            act.wait_ge(n_inv, 7)
            nc.scalar.activation(rstd, rstd, ACT.Sqrt).then_inc(n_sqrt, 1)

            def row_hi(t):
                act.wait_ge(nat_ready, t + 1)
                nc.scalar.activation(hn_h[:, t, :], h_nat[:, t, :], ACT.Copy).then_inc(nat_hi, 1)

            router_tile(4)
            router_tile(5)
            row_hi(0)
            router_tile(6)
            router_tile(7)
            row_hi(1)
            act.wait_ge(lgt_done, 1)
            nc.scalar.activation(logit_t, ps[0:NE, 4, :], ACT.Copy).then_inc(lgt_out, 1)
            row_hi(2)
            row_hi(3)
            act.preload_act_table_set("natural_log_exp_and_others")
            act.wait_ge(route_done, 1)
            for t in range(TT):
                ins = nc.scalar.activation(gate[:, t, :], top[:, t, 0:TOPK], ACT.Exp, bias=names["nmax"][:, t:t + 1],
                                           accum_out=names["gsum"][:, t:t + 1])
                ins.then_inc(gate_exp, 1)

            act.preload_act_table_set("sigmoid_and_others")

            def esplit(i, p):
                c = p // 2
                if p % 2 == 0:
                    landed = (EC // RAWE) * 16
                    before_ = (DENSE // RAW * 16 if c % RAWE < RAW else 0) + (c // RAWE + 1) * 16
                    act.wait_ge(w_landed[c % RAWE], i * landed + before_)
                act.wait_ge(w_used, i * EP + (DP + p - SPL + 1))
                nc.scalar.activation(wh[:, (DP + p) % SPL, :], raw_e(c)[:, p % 2 * PC:(p % 2 + 1) * PC], ACT.Copy).then_inc(w_hi, 1)

            def x_evac(m, u):
                act.wait_ge(gath, m * 8 + (u + 1))
                dst = (x_h, x_l)[u % 2][:, u - u % 2:u - u % 2 + 2, :, :].rearrange("p t b n -> p (t b n)")
                nc.scalar.activation(dst, ps[:, u % 4, :], ACT.Copy).then_inc(x_out, 1)

            def y_take(i):
                for n in range(2):
                    nc.scalar.activation(y_sb[:, n * 512:(n + 1) * 512], ps[:, 4 + n, :], ACT.Copy).then_inc(y_evac, 1)

            def y_store(i, c, dram, done):
                act.wait_ge(y_evac, i * 2 + 2)
                act.dma_start(dram.rearrange("(c p) d -> c p d", p=P)[bass.ds(c, 1), :, :].rearrange("o p d -> p (o d)"),
                              y_sb[:, :]).then_inc(done, 16)

            def expert(i, m, b=0, later=False, first=False, last=False, alone=False):
                if alone:
                    for p in range(AHEAD):
                        esplit(i, p)
                    for u in range(8):
                        x_evac(m, u)
                for p in range(EP):
                    if p == 19:
                        act_hi(i, 1)
                    if p + AHEAD < EP or not (last or alone):
                        esplit(i, p + AHEAD)
                    if p == 0 and not (first or alone):
                        if b == 0:
                            x_evac(m, 7)
                        act.wait_ge(w_used, i * EP + DP)
                        if later:
                            act.wait_ge(y_stored, i * 16 - 16)
                        y_take(i - 1)
                        y_store(i - 1, i - 1, y_main, y_stored)
                    if p == 5 or p == 13:
                        half = p // 8
                        act.wait_ge(glu_step, i * 6 + (3 * half + 1))
                        nc.scalar.activation(sig, glu, ACT.Sigmoid, scale=ALPHA).then_inc(sig_done, 1)
                    if p == 12:
                        act_hi(i, 0)
                    if p >= 17 and b == 1 and not last:
                        x_evac(m + 1, p - 17)

            def act_hi(i, half):
                act.wait_ge(at_done, i * 2 + (half + 1))
                nc.scalar.activation(a_h[:, half, :, :], ps[:, 6 + half, :].rearrange("p (a n) -> p a n", a=4),
                                     ACT.Copy).then_inc(a_hi, 1)

            for u in range(8):
                x_evac(0, u)
            expert(0, 0, first=True)
            expert(1, 0, b=1)
            with act.Fori(1, NE // 2 - 1) as m:
                expert(m * 2, m, later=True)
                expert(m * 2 + 1, m, b=1, later=True)
            expert(NE - 2, NE // 2 - 1, later=True)
            expert(NE - 1, NE // 2 - 1, b=1, later=True, last=True)
            act.wait_ge(w_used, NE * EP + DP)
            act.wait_ge(y_stored, NE * 16 - 16)
            y_take(NE - 1)
            y_store(NE - 1, NE - 1, y_main, y_stored)
            n = act.value_load(n_over, min_val=0, max_val=OVER)
            with act.If(n > 0):
                act.wait_ge(zero_ready, 1)
                act.dma_start(y_over.rearrange("(c p) d -> p c d", p=P),
                              y_sb.unsqueeze(1).to_broadcast([P, NC - NE, D])).then_inc(over_stored, 16)
                with act.Fori(0, OVER) as j:
                    with act.If(j < n):
                        c = act.value_load(table[0:1, bass.ds(j, 1)], min_val=0, max_val=NC - NE - 1)
                        expert(j + NE, j + NE // 2, alone=True)
                        act.wait_ge(w_used, j * EP + ((NE + 1) * EP + DP))
                        act.wait_ge(over_stored, j * 16 + 16)
                        y_take(j + NE)
                        y_store(j + NE, c, y_over, over_stored)
            act.preload_act_table_set("sqrt_and_others")
            for t in range(TT):
                act.wait_ge(row_used, 4 * t + 4)
                nc.scalar.activation(ps[:, 6:8, :].rearrange("p a n -> p (a n)"), res[:, t, :], ACT.Square,
                                     accum_out=ss[:, t:t + 1]).then_inc(n_sq, 1)
                act.wait_ge(n_inv, 8 + t)
                nc.scalar.activation(rstd[:, t:t + 1], rstd[:, t:t + 1], ACT.Sqrt).then_inc(n_sqrt, 1)
                if t < TT - 1:
                    act.wait_ge(n_sqrt, 8 + t)
                    if t >= 2:
                        act.wait_ge(stored[t % 2], 16 * (t // 2))
                    nc.scalar.activation(o_sb[:, t % 2, :], res[:, t, :], ACT.Copy, scale=rstd[:, t:t + 1]).then_inc(o_scaled, 1)

        @block.vector
        def _(dve):
            chain = Chain(dve, dve_chain)

            def split(g):
                dve.wait_ge(w_hi, g + 1)
                slot = g % SPL
                nc.vector.tensor_tensor(wl[:, slot, :], raw[:, g // 2 % RAW, g % 2 * PC:(g % 2 + 1) * PC], wh[:, slot, :], ALU.subtract).then_inc(w_lo, 1)

            def take(name, f, meanwhile={}):
                s = slabs[name]
                for c in range(2 * s.chunks):
                    split(2 * s.chunk0 + c + AHEAD)
                    if c in meanwhile:
                        meanwhile[c]()
                if s.owner != "dve":
                    return
                for t in range(s.tiles):
                    if t < s.tiles - 1:
                        dve.wait_ge(tile_done, s.tile0 + t + 1)
                    else:
                        dve.wait_ge(w_used, 2 * (s.chunk0 + s.chunks))
                    f(t).then_inc(tile_out["dve"], 1)

            def norm_scale(xv, dst, tiles, acc, rs, sq_n, inv_n):
                dve.wait_ge(n_sq, sq_n)
                chain(nc.vector.tensor_scalar(rs, acc, 1.0 / D, EPS, ALU.mult, ALU.add))
                chain.wait()
                nc.vector.reciprocal(rs, rs).then_inc(n_inv, 1)
                dve.wait_ge(n_sqrt, inv_n)
                for t in range(tiles):
                    nc.vector.tensor_scalar(dst[:, t, :], xv[:, t, :], rs[:, t:t + 1], None, ALU.mult).then_inc(n_xs, 1)

            def operand_lo(dst, hi, n0, tiles, cols, gain=None, first=0):
                for k in range(first, tiles):
                    dve.wait_ge(op_hi, n0 + k + 1)
                    src = ps[:, 4 + k % 4, 0:cols]
                    if gain is None:
                        ins = nc.vector.tensor_tensor(dst[:, k, :], src, hi[:, k, :], ALU.subtract)
                    else:
                        ins = nc.vector.scalar_tensor_tensor(dst[:, k, :], src, gain[:, k:k + 1], hi[:, k, :],
                                                             ALU.mult, ALU.subtract)
                    ins.then_inc(op_lo, 1)

            for t in range(TT):
                dve.wait_ge(n_sq, t + 1)
                chain(nc.vector.tensor_scalar(rstd[:, t:t + 1], ss[:, t:t + 1], 1.0 / D, EPS, ALU.mult, ALU.add))
                chain.wait()
                nc.vector.reciprocal(rstd[:, t:t + 1], rstd[:, t:t + 1]).then_inc(n_inv, 1)
                dve.wait_ge(n_sqrt, t + 1)
                nc.vector.tensor_scalar(x_nat[:, t, :], x_nat[:, t, :], rstd[:, t:t + 1], None, ALU.mult).then_inc(n_xs, 1)
            split(0)
            operand_lo(op_l, op_h, 0, KT, T, gmix_c)
            for g in range(1, AHEAD):
                split(g)
            for name in ("sbq", "sbk", "sbv"):
                take(name, None)
            units = [(h, kb) for h in range(HEADS) for kb in (3, 2, 1, 0)]
            dve.wait_ge(in_neg, 16)
            nc.vector.tensor_copy(neg_from_r, neg_from).then_inc(neg_ready, 1)
            nc.vector.tensor_copy(neg_ones_r, neg_ones).then_inc(neg_ready, 1)
            for step in range(len(units) + 1):
                if step < len(units):
                    h, kb = units[step]
                    n = T - P * kb
                    dve.wait_ge(ln_done, step + 1)
                    nc.vector.scalar_tensor_tensor(soft[:, h % 2, OFF[kb]:OFF[kb] + n], ps[:, step % 6, 0:n], 0.0,
                                                   abs_z[:, step % 3, 0:n], ALU.max, ALU.add).then_inc(soft_raw, 1)
                    u = step
                    high, low = soft_parts(h, kb)
                    whole = soft[:, h % 2, OFF[kb]:OFF[kb] + T - P * kb]
                    dve.wait_ge(soft_done, u + 1)
                    if h >= 2 and kb == 3:
                        dve.wait_ge(zc_done, 4 * (h - 1))
                    nc.vector.tensor_copy(high, whole).then_inc(soft_hi, 1)
                    dve.wait_ge(soft_hi, u + 1)
                    nc.vector.tensor_tensor(low, whole, high, ALU.subtract).then_inc(soft_lo, 1)
                if step >= 10 and step % 4 == 2:
                    head_out_dve(dve, step // 4 - 2)
            dve.wait_ge(zc_done, len(units))
            head_out_dve(dve, HEADS - 2)
            head_out_dve(dve, HEADS - 1)
            take("rq", None)
            take("rk", None)
            dve.wait_ge(in_rot, 16)
            for u in range(8):
                v = (q_r, k_r)[u // 4][:, u % 4, :]
                dve.wait_ge(rot_done, u + 1)
                if u >= 2:
                    dve.wait_ge(rot_out, u - 1)
                chain(nc.vector.tensor_tensor(rot_tmp[:, u % 2, :], ps[:, 4 + u % 4, :], sine, ALU.mult))
                chain(nc.vector.tensor_tensor(v, v, cosine, ALU.mult))
                chain.wait()
                nc.vector.tensor_tensor(v, v, rot_tmp[:, u % 2, :], ALU.add).then_inc(rot_out, 1)
            for name in ("rv0", "rv1", "rg0"):
                take(name, None)

            def decayed(h):
                dve.wait_ge(in_dec[h % 2], 16 * (h // 2 + 1))
                if h >= 2:
                    dve.wait_ge(ro_done, h - 1)
                for kb in range(4):
                    n = T - P * kb
                    dve.wait_ge(sc_done, 4 * h + kb + 1)
                    near = min(n, 2 * P)
                    ins = nc.vector.tensor_tensor(scores[:, h % 2, OFFA[kb]:OFFA[kb] + near], ps[:, 4 + kb, 0:near],
                                                  decay[:, h % 2, 0:near], ALU.mult)
                    for b in range(2, n // P):
                        ins = nc.vector.scalar_tensor_tensor(
                            scores[:, h % 2, OFFA[kb] + b * P:OFFA[kb] + b * P + P], ps[:, 4 + kb, b * P:b * P + P],
                            float(np.exp(LOG_DECAY[h] * P * (b - 1))), decay[:, h % 2, P:2 * P], ALU.mult, ALU.mult)
                    ins.then_inc(sc_out, 1)

            def normed(g):
                bank = ps[:, g % 2, :].rearrange("p (t n) -> p t n", t=TT)
                rs = retrs[:, g % 2, :]
                dve.wait_ge(ro_done, g + 1)
                for t in range(TT):
                    chain(nc.vector.bn_stats(retstat[:, 6 * t:6 * t + 6], bank[:, t, :]))
                chain.wait()
                for t in range(TT):
                    chain(nc.vector.bn_aggr(retmv[:, 2 * t:2 * t + 2], retstat[:, 6 * t:6 * t + 6]))
                chain.wait()
                mv = retmv.rearrange("p (t c) -> p c t", t=TT)
                if g >= 2:
                    dve.wait_ge(y_done, 4 * (g - 1))
                chain(nc.vector.tensor_scalar(rs, mv[:, 1, :], EPS, None, ALU.add))
                chain.wait()
                nc.vector.reciprocal(rs, rs).then_inc(rs_var, 1)
                for t in range(TT):
                    yv = y_r[:, t, g * P:(g + 1) * P]
                    nc.vector.scalar_tensor_tensor(yv, bank[:, t, :], mv[:, 0, t:t + 1], yv,
                                                   ALU.subtract, ALU.mult).then_inc(ro_out, 1)
                dve.wait_ge(ro_out, 4 * (g + 1))

            decayed(0)
            take("rg1", None)
            dve.wait_ge(tile_out["act"], slabs["rg1"].out0 + 4)
            for h in range(1, HEADS + 1):
                if h < HEADS:
                    decayed(h)
                normed(h - 1)
            for name in ("gs0", "gs1", "gr0", "gr1"):
                take(name, None)
            operand_lo(op_l, op_h, KT, 4, T)
            dve.wait_ge(tile_out["act"], GATED)
            for n in range(2):
                def gate_sb(t, n=n):
                    v = m_sb[:, 4 * n + t, :]
                    return nc.vector.tensor_tensor(v, ps[:, t, :], v, ALU.mult)
                take(f"so{n}", gate_sb)
                if n == 0:
                    operand_lo(op_l, op_h, KT, KT, T, None, 4)
                else:
                    operand_lo(opm_l, opm_h, 2 * KT, 4, M, gmem_c)

                def gate_ret(t, n=n):
                    v = m_ret[:, 4 * n + t, :]
                    chain(nc.vector.tensor_tensor(v, ps[:, t, :], v, ALU.mult))
                    chain.wait()
                    return nc.vector.tensor_tensor(m_sb[:, 4 * n + t, :], m_sb[:, 4 * n + t, :], v, ALU.add)
                if n == 0:
                    take("ro0", gate_ret)
                    norm_scale(mem_nat, mem_nat, MT, msum, mrstd, 6, 5)
                else:
                    take("ro1", gate_ret, {1: lambda: operand_lo(opm_l, opm_h, 2 * KT, KT, M, gmem_c, 4)})
            for k in range(KT):
                dve.wait_ge(op_hi, 3 * KT + k + 1)
                nc.vector.tensor_tensor(op_l[:, k, :], m_sb[:, k, :], op_h[:, k, :], ALU.subtract).then_inc(op_lo, 1)
            dve.wait_ge(in_res, 16)
            for n in range(2):
                def add_res(t, n=n):
                    v = res[:, t, n * 512:(n + 1) * 512]
                    return nc.vector.tensor_tensor(v, ps[:, t, :], v, ALU.add)
                take(f"mo{n}", add_res)
            norm_scale(res, xs2, TT, ss, rstd, 10, 6)
            for name in ("mk0", "mk1", "mv0", "mv1"):
                take(name, None)
            operand_lo(op_l, op_h, 4 * KT, KT, T, gxat_c)
            take("cq0", None)
            take("cq1", None)
            for u in range(XH * TT + 2):
                if u < XH * TT:
                    dve.wait_ge(xs_done, u + 1)
                    if u >= 4:
                        dve.wait_ge(xs_exp, u - 3)
                    nc.vector.tensor_reduce(xmax[:, u % 4:u % 4 + 1], ps[:, u % 4, 0:M], AX.X, ALU.max,
                                            negate=True).then_inc(xs_max, 1)
                if 1 <= u <= XH * TT:
                    v = u - 1
                    dve.wait_ge(xs_exp, v + 1)
                    chain(nc.vector.reciprocal(xrec[:, v % 4:v % 4 + 1], xsum[:, v % 4:v % 4 + 1]))
                    chain.wait()
                    nc.vector.tensor_scalar(prob[:, v % 4, :], prob[:, v % 4, :], xrec[:, v % 4:v % 4 + 1], None,
                                            ALU.mult).then_inc(xs_prob, 1)
                if u >= 2:
                    v = u - 2
                    hd, t = v // TT, v % TT
                    dve.wait_ge(xt_done, v + 1)
                    if hd >= 2 and t == 0:
                        dve.wait_ge(xo_done, 2 * (hd - 1))
                    dst = prob_t[:, hd % 2, :].rearrange("p (m n) -> p m n", m=MT)[:, :, t * P:(t + 1) * P]
                    nc.vector.tensor_copy(dst, ps[:, 4 + v % 2, 0:M].rearrange("p (m n) -> p m n", m=MT)).then_inc(xt_out, 1)
                    if t == 2 and hd >= 1:
                        cross_lo(dve, hd - 1)
            cross_lo(dve, XH - 1)
            for n in range(2):
                def add_res(t, n=n):
                    v = res[:, t, n * 512:(n + 1) * 512]
                    return nc.vector.tensor_tensor(v, ps[:, t, :], v, ALU.add)
                take(f"co{n}", add_res)
                if n == 0:
                    dve.wait_ge(b_hi, 1)
                    for r in (NE, 64 + NE):
                        nc.vector.tensor_tensor(bias[r:r + NE, :], bias_f[r:r + NE, :], bias[r:r + NE, :].bitcast(F32),
                                                ALU.subtract).then_inc(b_lo, 1)
            dve.wait_ge(n_sq, 18)
            chain(nc.vector.tensor_tensor(ss, ss, ss_more, ALU.add))
            chain.wait()
            chain(nc.vector.tensor_scalar(rstd, ss, 1.0 / D, EPS, ALU.mult, ALU.add))
            chain.wait()
            nc.vector.reciprocal(rstd, rstd).then_inc(n_inv, 1)
            dve.wait_ge(n_sqrt, 7)
            dve.wait_ge(in_moe, 48)
            for t in range(TT):
                nc.vector.scalar_tensor_tensor(h_nat[:, t, :], res[:, t, :], rstd[:, t:t + 1], g_moe_b,
                                               ALU.mult, ALU.mult).then_inc(nat_ready, 1)

            def row_lo(t):
                dve.wait_ge(nat_hi, t + 1)
                nc.vector.tensor_tensor(hn_l[:, t, :], h_nat[:, t, :], hn_h[:, t, :], ALU.subtract).then_inc(nat_lo, 1)

            row_lo(0)
            dve.wait_ge(lg_done, 1)
            for t in range(TT):
                chain(nc.vector.scalar_tensor_tensor(logit[:, t, :], ps[:, 1, t * NE:(t + 1) * NE], rstd[:, t:t + 1],
                                                     names["brt"], ALU.mult, ALU.add))
            chain.wait()
            for t in range(TT):
                chain(nc.vector.max(top[:, t, :], logit[:, t, :]))
            chain.wait()
            nc.vector.tensor_scalar(names["nmax"].rearrange("p (t o) -> p t o", o=1), top[:, :, 0:1], -1.0, None,
                                    ALU.mult).then_inc(route_done, 1)
            for t in range(TT):
                chain(nc.vector.max_index(topi[:, t, :], top[:, t, :], logit[:, t, :]))
            chain.wait()
            chain(nc.vector.tensor_copy(idxf, topi[:, :, 0:TOPK]))
            chain.wait()
            iota_b = iota[:, 0:NE].unsqueeze(1).unsqueeze(1).to_broadcast([P, TT, TOPK, NE])
            chain(nc.vector.tensor_tensor(oh, iota_b, idxf.unsqueeze(3).to_broadcast([P, TT, TOPK, NE]), ALU.is_equal))
            chain.wait()
            chain(nc.vector.tensor_reduce(sel, oh.rearrange("p t k e -> p t e k"), AX.X, ALU.add))
            chain.wait()
            dve.wait_ge(rt_ready, 3)
            nc.vector.tensor_copy(sel_b, sel).then_inc(rank_in, 1)
            row_lo(1)
            dve.wait_ge(rank_done, 1)
            rank_ps = ps[:, 2, 0:TT * NE].rearrange("p (t e) -> p t e", t=TT)
            chain(nc.vector.scalar_tensor_tensor(slot, rank_ps, 1.0, sel, ALU.add, ALU.mult))
            chain(nc.vector.tensor_copy(rank, rank_ps))
            chain(nc.vector.tensor_copy(names["cnt"], ps[:, 3, 0:NE]))
            chain.wait()
            chain(nc.vector.tensor_scalar(slots[:, :, 0:NE], slot, -1.0, None, ALU.add))
            chain.wait()
            for t in range(TT):
                for b in range(2):
                    nc.vector.tensor_scalar(pick[:, t, b, :], iota, slots[:, t, b:b + 1], None,
                                            ALU.is_equal).then_inc(pick0_ready, 1)
            for j in range(1, 4):
                chain(nc.vector.tensor_scalar(slots[:, :, j * NE:(j + 1) * NE], slot, -1.0 - P * j, None, ALU.add))
            chain(nc.vector.tensor_tensor(oh2, oh, rank.unsqueeze(2).to_broadcast([P, TT, TOPK, NE]), ALU.mult))
            chain.wait()
            rk = names["rk"]
            chain(nc.vector.tensor_reduce(rk.rearrange("p (t k) -> p t k", t=TT), oh2, AX.X, ALU.add))
            dve.wait_ge(gate_exp, 4)
            chain(nc.vector.reciprocal(names["grec"], names["gsum"]))
            chain.wait()
            chain(nc.vector.tensor_tensor(gate, gate, names["grec"].unsqueeze(2).to_broadcast([P, TT, TOPK]), ALU.mult))
            chain.wait()
            jj, jm, rowf, g16, g2 = names["jj"], names["jm"], names["rowf"], names["gate"], names["gate2"]
            chain(nc.vector.tensor_scalar(jj, rk, float(P), None, ALU.is_ge))
            chain(nc.vector.tensor_scalar(jm, rk, float(P), None, ALU.is_lt))
            chain(nc.vector.tensor_scalar(rowf, rk, float(P - 1), None, ALU.min))
            chain.wait()
            chain(nc.vector.tensor_tensor(g2, g16, jj, ALU.mult))
            chain(nc.vector.scalar_tensor_tensor(rowf, names["idxf"], float(P), rowf, ALU.mult, ALU.add))
            chain.wait()
            chain(nc.vector.tensor_copy(rowi, rowf))
            chain(nc.vector.tensor_tensor(g16, g16, jm, ALU.mult))
            chain.wait()
            chain(nc.vector.scalar_tensor_tensor(rowf, names["idxf"], float(P), rk, ALU.mult, ALU.add))
            for j in (2, 3):
                chain(nc.vector.scalar_tensor_tensor(jj, rk, float(P * j), jj, ALU.is_ge, ALU.add))
                chain.wait()
            chain(nc.vector.scalar_tensor_tensor(rowf, jj, float(NE * P - P), rowf, ALU.mult, ALU.add))
            chain.wait()
            chain(nc.vector.tensor_scalar(rowf, rowf, float(-NE * P), 0.0, ALU.add, ALU.max))
            chain.wait()
            nc.vector.tensor_copy(rowj, rowf).then_inc(route_done, 1)
            cnt = names["cnt"]
            for j in range(3):
                chain(nc.vector.tensor_scalar(ov_ex[:, j * NE:(j + 1) * NE], cnt[0:1, :], float(P * (j + 1)), None, ALU.is_gt))
            chain.wait()
            chain(nc.vector.tensor_tensor_scan(ov_pos, ov_ex, ov_ex, 0.0, ALU.add, ALU.bypass))
            chain(nc.vector.tensor_tensor(ov_c, iota[0:1, 0:96], ov_ex, ALU.mult))
            chain.wait()
            chain(nc.vector.tensor_scalar(ov_tab, iota[0:1, 0:16], 1.0, None, ALU.add))
            chain.wait()
            chain(nc.vector.tensor_tensor(ov_eq, ov_pos.unsqueeze(1).to_broadcast([1, 16, 96]),
                                          ov_tab.unsqueeze(2).to_broadcast([1, 16, 96]), ALU.is_equal))
            chain.wait()
            chain(nc.vector.tensor_tensor(ov_eq, ov_eq, ov_c.unsqueeze(1).to_broadcast([1, 16, 96]), ALU.mult))
            chain.wait()
            chain(nc.vector.tensor_reduce(ov_tab, ov_eq, AX.X, ALU.add))
            chain.wait()
            chain(nc.vector.tensor_copy(table, ov_tab))
            chain.wait()
            nc.vector.tensor_copy(n_over, ov_pos[:, 95:96]).then_inc(route_done, 1)

            def esplit(i, p):
                if p % EP in POOL:
                    return
                dve.wait_ge(w_hi, i * EP + (DP + p + 1))
                nc.vector.tensor_tensor(wl[:, (DP + p) % SPL, :], raw_e(p // 2)[:, p % 2 * PC:(p % 2 + 1) * PC], wh[:, (DP + p) % SPL, :],
                                        ALU.subtract).then_inc(w_lo, 1)

            def expert(i, last=False, alone=False):
                if alone:
                    for p in range(AHEAD):
                        esplit(i, p)
                for p in range(EP):
                    if p == 19:
                        act_lo(i, 1)
                    if p + AHEAD < EP or not (last or alone):
                        esplit(i, p + AHEAD)
                    if p in (4, 12):
                        half = p // 8
                        dve.wait_ge(w_used, i * EP + (DP + p))
                        nc.vector.tensor_scalar(glu, ps[:, 2 * half, :], LIMIT, None,
                                                ALU.min).then_inc(glu_step, 1)
                    if p in (8, 16):
                        half = p // 8 - 1
                        k = i * 6 + 3 * half
                        v = lin
                        dve.wait_ge(w_used, i * EP + (DP + p))
                        nc.vector.tensor_scalar(v, ps[:, 2 * half + 1, :], -LIMIT, LIMIT,
                                                ALU.max, ALU.min).then_inc(glu_step, 1)
                        dve.wait_ge(glu_step, k + 2)
                        dve.wait_ge(gs_done, i * 2 + (half + 1))
                        nc.vector.scalar_tensor_tensor(v, v, 1.0, sig, ALU.add, ALU.mult).then_inc(glu_step, 1)
                    if p == 12:
                        act_lo(i, 0)

            def act_lo(i, half):
                dve.wait_ge(a_hi, i * 2 + (half + 1))
                nc.vector.tensor_tensor(a_l[:, half, :, :], ps[:, 6 + half, :].rearrange("p (a n) -> p a n", a=4),
                                        a_h[:, half, :, :], ALU.subtract).then_inc(a_lo, 1)

            with dve.Fori(0, NE - 1) as i:
                expert(i)
            expert(NE - 1, last=True)
            n = dve.value_load(n_over, min_val=0, max_val=OVER)
            with dve.If(n > 0):
                with dve.Fori(0, OVER) as j:
                    with dve.If(j < n):
                        expert(j + NE, alone=True)
                for u in range(TT * TOPK):
                    dve.wait_ge(over_in[u % ROWS], 16 * (u // ROWS + 1))
                    if u:
                        dve.wait_ge(over_used, u)
                    nc.vector.scalar_tensor_tensor(res[:, u // TOPK, :], y_rows[:, u % ROWS, :], g2[:, u:u + 1],
                                                   res[:, u // TOPK, :], ALU.mult, ALU.add).then_inc(over_used, 1)
                dve.wait_ge(over_used, TT * TOPK)
            for t in range(TT):
                for k in range(TOPK):
                    u = TOPK * t + k
                    dve.wait_ge(row_in[u % ROWS], 16 * (u // ROWS + 1))
                    if k:
                        dve.wait_ge(row_used, u)
                    nc.vector.scalar_tensor_tensor(res[:, t, :], y_rows[:, u % ROWS, :], gate[:, t, k:k + 1], res[:, t, :],
                                                   ALU.mult, ALU.add).then_inc(row_used, 1)
                dve.wait_ge(n_sq, 19 + t)
                chain(nc.vector.tensor_scalar(rstd[:, t:t + 1], ss[:, t:t + 1], 1.0 / D, EPS, ALU.mult, ALU.add))
                chain.wait()
                nc.vector.reciprocal(rstd[:, t:t + 1], rstd[:, t:t + 1]).then_inc(n_inv, 1)
            t = TT - 1
            dve.wait_ge(n_sqrt, 8 + t)
            dve.wait_ge(in_gfin, 16)
            dve.wait_ge(stored[t % 2], 16 * (t // 2))
            nc.vector.scalar_tensor_tensor(o_sb[:, t % 2, :], res[:, t, :], rstd[:, t:t + 1], g_fin_b,
                                           ALU.mult, ALU.mult).then_inc(f_last, 1)

        @block.tensor
        def _(pe):
            def three(o, a_hi_, a_lo_, b_hi_, b_lo_, start, stop):
                nc.tensor.matmul(o, a_hi_, b_hi_, start=start, stop=False)
                nc.tensor.matmul(o, a_hi_, b_lo_, start=False, stop=False)
                return nc.tensor.matmul(o, a_lo_, b_hi_, start=False, stop=stop)

            def project(name, oh_, ol_, ready=None, meanwhile={}, free={}):
                s = slabs[name]
                for c in range(2 * s.chunks):
                    g = 2 * s.chunk0 + c
                    pe.wait_ge(w_lo, g + 1)
                    w_h, w_l = (v[:, g % SPL, :].rearrange("p (a n) -> p a n", a=2) for v in (wh, wl))
                    for t in range(s.tiles):
                        if c == 0 and s.bank_free[t]:
                            owner, count = s.bank_free[t]
                            pe.wait_ge(tile_out[owner], count)
                        if c == 0 and t in free:
                            pe.wait_ge(*free[t])
                        for a in range(2):
                            k = 2 * c + a
                            if ready and t == 0:
                                pe.wait_ge(ready[0], ready[1] + k + 1)
                            first, last = k == 0, k == 4 * s.chunks - 1
                            o = ps[:, t, 0:s.cols]
                            cut = slice(t * P, (t + 1) * P)
                            if s.kind == "T":
                                ins = three(o, w_h[:, a, cut], w_l[:, a, cut], oh_[:, k, :], ol_[:, k, :], first, last)
                            else:
                                ins = three(o, oh_[:, k, cut], ol_[:, k, cut], w_h[:, a, :], w_l[:, a, :], first, last)
                        if t == s.tiles - 1:
                            ins.then_inc(w_used, 1)
                        elif c == 2 * s.chunks - 1:
                            ins.then_inc(tile_done, 1)
                    if c in meanwhile:
                        meanwhile[c]()

            def transposes(src, tiles, n0, ks=range(KT)):
                for k in ks:
                    if n0 + k >= 4:
                        pe.wait_ge(op_lo, n0 + k - 3)
                    for t in range(tiles):
                        ins = nc.tensor.transpose(ps[:, 4 + k % 4, t * P:(t + 1) * P], src[:, t, k * P:(k + 1) * P], ident)
                    ins.then_inc(tr_done, 1)

            pe.wait_ge(in_mats, 16)
            for t in range(TT):
                pe.wait_ge(n_xs, t + 1)
                for k in range(4):
                    ins = nc.tensor.transpose(ps[:, 4 + k, t * P:(t + 1) * P], x_nat[:, t, k * P:(k + 1) * P], ident)
                    if t == TT - 1:
                        ins.then_inc(tr_done, 1)
            transposes(x_nat, TT, 0, range(4, KT))
            project("sbq", op_h, op_l, (op_lo, 0))
            project("sbk", op_h, op_l)
            project("sbv", op_h, op_l)
            pe.wait_ge(neg_ready, 2)
            units = [(h, kb) for h in range(HEADS) for kb in (3, 2, 1, 0)]
            pe.wait_ge(tile_out["act"], 12)
            for step in range(len(units) + LAG + 2):
                if step < len(units):
                    h, kb = units[step]
                    n = T - P * kb
                    r = 64 * (h % 2)
                    if step >= 6:
                        pe.wait_ge(wexp_done, step - 5)
                    nc.tensor.matmul(ps[:, step % 6, 0:n], k_sb[r:r + 64, h // 2, kb * P:(kb + 1) * P],
                                     q_sb[r:r + 64, h // 2, kb * P:T], start=True, stop=True).then_inc(z_done, 1)
                if LAG <= step < len(units) + LAG:
                    u = step - LAG
                    h, kb = units[u]
                    pe.wait_ge(soft_lo, u + 1)
                    for b in range(3, kb - 1, -1):
                        n = T - P * b
                        for part in soft_parts(h, b):
                            ins = nc.tensor.matmul(ps[:, u % 6, P * (b - kb):P * (b - kb) + n],
                                                   neg_from_r if b == kb else neg_ones_r, part, start=False, stop=True,
                                                   skip_group_check=True)
                    ins.then_inc(zc_done, 1)
                if step >= LAG + 5 and (step - LAG) % 4 == 1:
                    head_out(pe, (step - LAG - 5) // 4)
            pe.wait_ge(wexp_done, len(units))
            project("rq", op_h, op_l)
            project("rk", op_h, op_l)
            pe.wait_ge(tile_out["act"], 20)
            for u in range(8):
                if u >= 4:
                    pe.wait_ge(rot_out, u - 3)
                elif u == 0:
                    pe.wait_ge(o_lo, HEADS)
                nc.tensor.matmul(ps[:, 4 + u % 4, :], rot_swap, (q_r, k_r)[u // 4][:, u % 4, :], start=True,
                                 stop=True).then_inc(rot_done, 1)
            for name in ("rv0", "rv1", "rg0"):
                project(name, op_h, op_l)

            def retention_scores(h):
                r = 64 * (h % 2)
                for kb in range(4):
                    n = T - P * kb
                    if h >= 1:
                        pe.wait_ge(sc_out, 4 * (h - 1) + kb + 1)
                    nc.tensor.matmul(ps[:, 4 + kb, 0:n], k_r[r:r + 64, h // 2, kb * P:(kb + 1) * P],
                                     q_r[r:r + 64, h // 2, kb * P:T], start=True, stop=True).then_inc(sc_done, 1)

            pe.wait_ge(rot_out, 8)
            retention_scores(0)
            project("rg1", op_h, op_l)
            for h in range(1, HEADS + 1):
                if h < HEADS:
                    retention_scores(h)
                if h >= 1:
                    g = h - 1
                    pe.wait_ge(sc_out, 4 * (g + 1))
                    if g < 2:
                        pe.wait_ge(tile_out["act"], slabs["rg1"].out0 + g + 1)
                    if g >= 2:
                        pe.wait_ge(ro_out, 4 * (g - 1))
                    for t in range(TT):
                        for kb in range(t + 1):
                            a = OFFA[kb] + (t - kb) * P
                            ins = nc.tensor.matmul(ps[:, g % 2, t * P:(t + 1) * P], scores[:, g % 2, a:a + P],
                                                   v_r[:, kb, g * P:(g + 1) * P], start=(kb == 0), stop=(kb == t))
                    ins.then_inc(ro_done, 1)
            project("gs0", op_h, op_l, free={0: (ro_out, 4 * HEADS - 4), 1: (ro_out, 4 * HEADS)})
            pe.wait_ge(y_done, 4 * HEADS)
            transposes(y_r, TT, KT, range(4))
            for name in ("gs1", "gr0", "gr1"):
                project(name, op_h, op_l)
            project("so0", op2_h, op2_l)
            transposes(y_r, TT, KT, range(4, KT))
            project("ro0", op_h, op_l, (op_lo, KT))
            project("so1", op2_h, op2_l)
            pe.wait_ge(n_xs, TT + MT)
            transposes(mem_nat, MT, 2 * KT, range(4))
            project("ro1", op_h, op_l, meanwhile={0: lambda: transposes(mem_nat, MT, 2 * KT, range(4, KT))})
            project("mo0", op_h, op_l, (op_lo, 3 * KT))
            project("mo1", op_h, op_l)
            project("mk0", opm_h, opm_l)
            for name in ("mk1", "mv0", "mv1"):
                project(name, opm_h, opm_l)
            pe.wait_ge(n_xs, 2 * TT + MT)
            transposes(xs2, TT, 4 * KT)
            project("cq0", op_h, op_l, (op_lo, 4 * KT))
            project("cq1", op_h, op_l)
            pe.wait_ge(tile_out["act"], outs_total["act"])
            for u in range(XH * TT + 5):
                if u < XH * TT:
                    hd, t = u // TT, u % TT
                    if u >= 4:
                        pe.wait_ge(xs_exp, u - 3)
                    for dt in range(2):
                        ins = nc.tensor.matmul(ps[:, u % 4, 0:M], q_x[:, 2 * hd + dt, t * P:(t + 1) * P],
                                               k_x[:, 2 * hd + dt, :], start=(dt == 0), stop=(dt == 1))
                    ins.then_inc(xs_done, 1)
                if 2 <= u < XH * TT + 2:
                    v = u - 2
                    pe.wait_ge(xs_prob, v + 1)
                    if v >= 2:
                        pe.wait_ge(xt_out, v - 1)
                    for m in range(MT):
                        ins = nc.tensor.transpose(ps[:, 4 + v % 2, m * P:(m + 1) * P], prob[:, v % 4, m * P:(m + 1) * P], ident)
                    ins.then_inc(xt_done, 1)
                if u >= 8 and u % TT == 0:
                    cross_out(pe, u // TT - 2)
            project("co0", op_h, op_l, (op_lo, 5 * KT))

            def router_transposes(half):
                for t in range(TT):
                    pe.wait_ge(tile_out["dve"], slabs[f"co{half}"].out0 + t + 1)
                    for k in range(4 * half, 4 * half + 4):
                        ins = nc.tensor.transpose(ps[:, ROUTER_BANK[k], t * P:(t + 1) * P], res[:, t, k * P:(k + 1) * P], ident)
                        if t == TT - 1:
                            ins.then_inc(ht_done, 1)

            def router_product(half):
                if half == 0:
                    pe.wait_ge(rt_ready, 1)
                    pe.wait_ge(ht_out, 4)
                for k in range(4 * half, 4 * half + 4):
                    if half == 1:
                        pe.wait_ge(ht_out, k + 1)
                    ins = nc.tensor.matmul(ps[0:NE, 4, :], w_rt[:, k, :], h_t[:, k % 4, :], start=(k == 0),
                                           stop=(k == KT - 1), skip_group_check=True)
                ins.then_inc((lg_half, lgt_done)[half], 1)

            project("co1", op_h, op_l, meanwhile={1: lambda: router_transposes(0), 2: lambda: router_product(0)})
            router_transposes(1)
            router_product(1)
            pe.wait_ge(lgt_out, 1)
            for t in range(TT):
                ins = nc.tensor.transpose(ps[:, 1, t * NE:(t + 1) * NE], logit_t[:, t * P:(t + 1) * P], ident[0:NE, 0:NE])
            ins.then_inc(lg_done, 1)
            pe.wait_ge(rank_in, 1)
            for t in range(TT):
                for b in range(t + 1):
                    nc.tensor.matmul(ps[:, 2, t * NE:(t + 1) * NE], before_b if b == t else ones_b, sel_b[:, b, :],
                                     start=(b == 0), stop=(b == t))
            for b in range(TT):
                ins = nc.tensor.matmul(ps[:, 3, 0:NE], ones_b, sel_b[:, b, :], start=(b == 0), stop=(b == TT - 1))
            ins.then_inc(rank_done, 1)

            def gather(m, u):
                src = (hn_h, hn_l)[u % 2]
                for a in range(2):
                    k = u - u % 2 + a
                    for t in range(TT):
                        ins = nc.tensor.matmul(ps[:, u % 4, a * 256:(a + 1) * 256], src[:, t, k * P:(k + 1) * P],
                                               pick[:, t, :, :].rearrange("p b n -> p (b n)"), start=(t == 0), stop=(t == TT - 1))
                ins.then_inc(gath, 1)

            def gather_alone(m):
                for u in range(8):
                    if u >= 4:
                        pe.wait_ge(x_out, m * 8 + (u - 3))
                    gather(m, u)

            def expert(i, m, b=0, following=False, first=False):
                for p in range(16):
                    q = p // 4
                    bank = ps[:, q, :]
                    if b == 0 and p != 1 and p < 4:
                        pe.wait_ge(x_out, m * 8 + {0: 5, 2: 6, 3: 8}[p])
                    if p % 4 == 0:
                        r, col = divmod((q % 2) * DFF + (q // 2) * 512, BC)
                        if q == 0:
                            pe.wait_ge(bsel_ready, i + 1)
                        nc.tensor.matmul(bank, bsel[64 * r:64 * r + 64, :], bias[64 * r:64 * r + 64, col:col + 512], start=True, stop=False)
                    wait_lo(pe, i, p)
                    s = (DP + p) % SPL
                    for a in range(2):
                        k = 2 * (p % 4) + a
                        ins = three(bank, x_h[:, k, b, :], x_l[:, k, b, :], wh[:, s, a * 512:(a + 1) * 512],
                                    wl[:, s, a * 512:(a + 1) * 512], False, k == KT - 1)
                    ins.then_inc(w_used, 1)
                    if p == 11:
                        turn(i, 0)
                for n in range(2):
                    if n == 0 and not first:
                        pe.wait_ge(y_evac, i * 2)
                    ins = nc.tensor.matmul(ps[:, 4 + n, :], bsel[64:128, :], bias[64:128, 2 * D - BC + n * 512:2 * D - BC + (n + 1) * 512],
                                           start=True, stop=False)
                ins.then_inc(bsel_used, 1)
                for f in range(KT):
                    p = 16 + f
                    s = (DP + p) % SPL
                    wait_lo(pe, i, p)
                    if f % 4 == 0:
                        pe.wait_ge(a_lo, i * 2 + (f // 4 + 1))
                    for n in range(2):
                        cut = slice(n * 512, (n + 1) * 512)
                        ins = three(ps[:, 4 + n, :], a_h[:, f // 4, f % 4, :], a_l[:, f // 4, f % 4, :], wh[:, s, cut], wl[:, s, cut],
                                    False, f == KT - 1)
                    ins.then_inc(w_used, 1)
                    if f == 2:
                        turn(i, 1)
                    if following:
                        if f == 0:
                            pe.wait_ge(pick_ready, m * 8 + 8)
                        if f >= 4:
                            pe.wait_ge(x_out, m * 8 + (f + 5))
                        gather(m + 1, f)

            def turn(i, half):
                pe.wait_ge(glu_step, i * 6 + (3 * half + 3))
                for a in range(4):
                    ins = nc.tensor.transpose(ps[:, 6 + half, a * P:(a + 1) * P], lin[:, a * P:(a + 1) * P], ident)
                ins.then_inc(at_done, 1)

            pe.wait_ge(nat_lo, 2)
            pe.wait_ge(nat_lo_pool, 2)
            pe.wait_ge(b_lo, 2)
            pe.wait_ge(pick0_ready, 8)
            gather_alone(0)
            expert(0, 0, first=True)
            expert(1, 0, b=1, following=True)
            with pe.Fori(1, NE // 2 - 1) as m:
                expert(m * 2, m)
                expert(m * 2 + 1, m, b=1, following=True)
            expert(NE - 2, NE // 2 - 1)
            expert(NE - 1, NE // 2 - 1, b=1)
            pe.wait_ge(route_done, 3)
            n = pe.value_load(n_over, min_val=0, max_val=OVER)
            with pe.If(n > 0):
                with pe.Fori(0, OVER) as j:
                    with pe.If(j < n):
                        pe.wait_ge(pick_ready, j * 8 + NE * 4)
                        gather_alone(j + NE // 2)
                        expert(j + NE, j + NE // 2)

OFF = {3: 0, 2: 128, 1: 384, 0: 768}
OFFA = {0: 0, 1: 512, 2: 896, 3: 1152}
ROUTER_BANK = (4, 5, 6, 7, 5, 6, 7, 0)
TR_RET = 2 * KT
_S, _N, _O = lay_slabs()
MIXED = _S["mo1"].out0 + 4
GATED = _S["gr1"].out0 + 4

_INS = ["x", "mem", "g_mix", "w_in", "w_sb_o", "w_ret_o", "w_mix_out", "g_xattn", "g_mem", "w_cq", "w_ckv", "w_co",
        "g_moe", "w_router", "b_router", "w_exp_in", "b_exp_in", "w_exp_out", "b_exp_out", "g_final"]


def kernel(**inputs):
    import concourse.bacc as _bacc
    from concourse.bass_utils import run_bass_kernel_spmd as _run

    nc = _bacc.Bacc("TRN2", target_bir_lowering=False, num_devices=1)
    arrays, args = {}, []
    given = {name: np.ascontiguousarray(inputs[name]) for name in _INS}
    given.update(constant_tables())
    for name, a in given.items():
        arrays[f"in_{name}"] = a
        args.append(nc.dram_tensor(f"in_{name}", a.shape, mybir.dt.from_np(a.dtype), kind="ExternalInput").ap())
    args.append(nc.dram_tensor("out_rows", (1, T, D), F32, kind="ExternalOutput").ap())
    layer_kernel(nc, *args)
    r = _run(nc, [arrays], core_ids=[0])
    return r.results[0]["out_rows"]
```
